# Optimizing a Trainium2 kernel written in Bass

```python
import math
import functools
import jax
import jax.numpy as jnp
from jax import lax
import numpy as np

D_MODEL = 1024
BATCH = 1
SEQ = 512
DEPTH = 2

EPS = 1e-6
D_FF = 4 * D_MODEL
N_EVEN = (DEPTH + 1) // 2
N_ODD = DEPTH // 2
CHUNK = 128
BLOCK_Q = 128

REL_BUCKETS = 32
REL_MAX_DIST = 128
N_BIAS_HEADS = 8

SSD_D_INNER = D_MODEL
SSD_HEAD_DIM = 64
SSD_HEADS = SSD_D_INNER // SSD_HEAD_DIM
SSD_GROUPS = 4
SSD_STATE = 128
SSD_CONV = 4
SSD_CONV_CH = SSD_D_INNER + 2 * SSD_GROUPS * SSD_STATE

DIFF_HEADS = N_BIAS_HEADS
DIFF_HEAD_DIM = D_MODEL // (2 * DIFF_HEADS)
DIFF_QK = DIFF_HEADS * 2 * DIFF_HEAD_DIM
DIFF_V = DIFF_HEADS * 2 * DIFF_HEAD_DIM

EVEN_SPLITS = (SSD_D_INNER, SSD_CONV_CH, SSD_HEADS, DIFF_QK, DIFF_QK, DIFF_V)
EVEN_IN = sum(EVEN_SPLITS)
EVEN_MIX = SSD_D_INNER + DIFF_V

RET_HEADS = 4
RET_QK_DIM = 128
RET_V_DIM = 256
ROPE_BASE = 10000.0

SWA_HEADS = N_BIAS_HEADS
SWA_KV_HEADS = 2
SWA_HEAD_DIM = 64
WINDOW = 128

ODD_SPLITS = (RET_HEADS * RET_QK_DIM, RET_HEADS * RET_QK_DIM, RET_HEADS * RET_V_DIM,
              RET_HEADS * RET_V_DIM, SWA_HEADS * SWA_HEAD_DIM,
              SWA_KV_HEADS * SWA_HEAD_DIM, SWA_KV_HEADS * SWA_HEAD_DIM)
ODD_IN = sum(ODD_SPLITS)
ODD_MIX = RET_HEADS * RET_V_DIM + SWA_HEADS * SWA_HEAD_DIM


def rms_norm(x, w=None):
    x32 = x.astype(jnp.float32)
    y = x32 * lax.rsqrt(jnp.mean(x32 * x32, axis=-1, keepdims=True) + EPS)
    if w is not None:
        y = y * w.astype(jnp.float32)
    return y.astype(x.dtype)

def split_cols(a, sizes):
    return jnp.split(a, np.cumsum(sizes)[:-1].tolist(), axis=-1)

def t5_bucket(dist):
    dist = jnp.maximum(dist, 0)
    max_exact = REL_BUCKETS // 2
    logd = jnp.log(jnp.maximum(dist, 1).astype(jnp.float32) / max_exact)
    large = max_exact + (logd / math.log(REL_MAX_DIST / max_exact)
                         * (REL_BUCKETS - max_exact)).astype(jnp.int32)
    large = jnp.minimum(large, REL_BUCKETS - 1)
    return jnp.where(dist < max_exact, dist, large)

def scan_chunk_states(chunk_states, chunk_decay):
    def step(carry, inp):
        st, dec = inp
        return carry * dec + st, carry
    init = jnp.zeros_like(chunk_states[:, 0])
    _, prev = lax.scan(step, init, (jnp.moveaxis(chunk_states, 1, 0), jnp.moveaxis(chunk_decay, 1, 0)))
    return jnp.moveaxis(prev, 0, 1)

def causal_depthwise_conv(x, w, b):
    ch = x.shape[-1]
    out = lax.conv_general_dilated(x, w[:, None, :].astype(x.dtype), window_strides=(1,),
                                   padding=[(SSD_CONV - 1, 0)],
                                   dimension_numbers=("NWC", "WIO", "NWC"),
                                   feature_group_count=ch)
    return out + b.astype(x.dtype)

def ssd_chunked(xh, dt, A, Bg, Cg):
    b, s, h, p = xh.shape
    g, n = Bg.shape[-2:]
    r = h // g
    nc = s // CHUNK
    X = (xh * dt[..., None]).reshape(b, nc, CHUNK, g, r, p)
    Bc = Bg.reshape(b, nc, CHUNK, g, n)
    Cc = Cg.reshape(b, nc, CHUNK, g, n)
    a_cs = jnp.cumsum((dt * A).reshape(b, nc, CHUNK, g, r), axis=2)
    causal = jnp.tril(jnp.ones((CHUNK, CHUNK), dtype=bool))
    seg = a_cs[:, :, :, None] - a_cs[:, :, None, :]
    decay_in = jnp.exp(jnp.where(causal[:, :, None, None], seg, -jnp.inf))
    cb = jnp.einsum("bclgn,bcsgn->bclsg", Cc, Bc)
    y_diag = jnp.einsum("bclsg,bclsgr,bcsgrp->bclgrp", cb, decay_in, X)
    decay_to_end = jnp.exp(a_cs[:, :, -1:] - a_cs)
    chunk_states = jnp.einsum("bcsgn,bcsgr,bcsgrp->bcgrpn", Bc, decay_to_end, X)
    state_prev = scan_chunk_states(chunk_states, jnp.exp(a_cs[:, :, -1])[..., None, None])
    y_off = jnp.einsum("bclgn,bcgrpn,bclgr->bclgrp", Cc, state_prev, jnp.exp(a_cs))
    return (y_diag + y_off).reshape(b, s, h, p)

def ssd_mixer(z, xbc, dt_raw, conv_w, conv_b, dt_bias, A_log, D_skip, norm_w):
    b, s, _ = z.shape
    xbc = jax.nn.silu(causal_depthwise_conv(xbc, conv_w, conv_b))
    xs, Bs, Cs = split_cols(xbc, (SSD_D_INNER, SSD_GROUPS * SSD_STATE, SSD_GROUPS * SSD_STATE))
    xh = xs.astype(jnp.float32).reshape(b, s, SSD_HEADS, SSD_HEAD_DIM)
    dt = jax.nn.softplus(dt_raw.astype(jnp.float32) + dt_bias.astype(jnp.float32))
    A = -jnp.exp(A_log.astype(jnp.float32))
    y = ssd_chunked(xh, dt, A,
                    Bs.astype(jnp.float32).reshape(b, s, SSD_GROUPS, SSD_STATE),
                    Cs.astype(jnp.float32).reshape(b, s, SSD_GROUPS, SSD_STATE))
    y = y + xh * D_skip.astype(jnp.float32)[:, None]
    y = y.reshape(b, s, SSD_D_INNER) * jax.nn.silu(z.astype(jnp.float32))
    return rms_norm(y, norm_w).astype(z.dtype)

def diff_attention(q, k, v, lam, subln_w, rel_bias, layer_idx):
    b, s = q.shape[:2]
    lam_init = 0.8 - 0.6 * math.exp(-0.3 * layer_idx)
    lam32 = lam.astype(jnp.float32)
    lam_full = (jnp.exp(jnp.sum(lam32[0] * lam32[1])) - jnp.exp(jnp.sum(lam32[2] * lam32[3])) + lam_init)
    q32 = q.astype(jnp.float32) * DIFF_HEAD_DIM ** -0.5
    k32 = k.astype(jnp.float32)
    v32 = v.astype(jnp.float32)
    nb = s // BLOCK_Q
    q_blocks = jnp.moveaxis(q32.reshape(b, nb, BLOCK_Q, DIFF_HEADS, 2, DIFF_HEAD_DIM), 1, 0)
    key_pos = jnp.arange(s)

    def one_block(args):
        q_blk, blk = args
        dist = (blk * BLOCK_Q + jnp.arange(BLOCK_Q))[:, None] - key_pos[None, :]
        bias = jnp.transpose(rel_bias[t5_bucket(dist)], (2, 0, 1)).astype(jnp.float32)
        logits = jnp.einsum("bqhmd,bkhmd->bhmqk", q_blk, k32) + bias[None, :, None]
        logits = jnp.where(dist >= 0, logits, -jnp.inf)
        p = jax.nn.softmax(logits, axis=-1)
        attn = p[:, :, 0] - lam_full * p[:, :, 1]
        return jnp.einsum("bhqk,bkhe->bqhe", attn, v32)

    out = lax.map(one_block, (q_blocks, jnp.arange(nb)))
    out = jnp.moveaxis(out, 0, 1).reshape(b, s, DIFF_HEADS, 2 * DIFF_HEAD_DIM)
    out = rms_norm(out, subln_w) * (1.0 - lam_init)
    return out.reshape(b, s, DIFF_V).astype(q.dtype)

def rope(t, pos):
    half = t.shape[-1] // 2
    inv = ROPE_BASE ** (-jnp.arange(half, dtype=jnp.float32) / half)
    ang = pos[:, None] * inv[None]
    cos = jnp.cos(ang)[None, :, None]
    sin = jnp.sin(ang)[None, :, None]
    t1, t2 = t[..., :half], t[..., half:]
    return jnp.concatenate([t1 * cos - t2 * sin, t1 * sin + t2 * cos], axis=-1)

def retention(q, k, v):
    b, s = q.shape[:2]
    nc = s // CHUNK
    pos = jnp.arange(s, dtype=jnp.float32)
    Q = rope(q.astype(jnp.float32), pos).reshape(b, nc, CHUNK, RET_HEADS, RET_QK_DIM)
    K = (rope(k.astype(jnp.float32), pos) * RET_QK_DIM ** -0.5).reshape(b, nc, CHUNK, RET_HEADS, RET_QK_DIM)
    V = v.astype(jnp.float32).reshape(b, nc, CHUNK, RET_HEADS, RET_V_DIM)
    log_gamma = jnp.log(1.0 - 2.0 ** (-5.0 - jnp.arange(RET_HEADS, dtype=jnp.float32)))
    idx = jnp.arange(CHUNK, dtype=jnp.float32)
    rel = idx[:, None] - idx[None, :]
    decay_mat = jnp.where(rel >= 0, jnp.exp(jnp.maximum(rel, 0.0)[None] * log_gamma[:, None, None]), 0.0)
    scores = jnp.einsum("bclhd,bcshd->bchls", Q, K) * decay_mat
    inner = jnp.einsum("bchls,bcshe->bclhe", scores, V)
    zeta = jnp.exp((CHUNK - 1 - idx)[None] * log_gamma[:, None])
    kv = jnp.einsum("bcshd,hs,bcshe->bchde", K, zeta, V)
    chunk_decay = jnp.broadcast_to(jnp.exp(CHUNK * log_gamma)[:, None, None], (b, nc, RET_HEADS, 1, 1))
    state_prev = scan_chunk_states(kv, chunk_decay)
    xi = jnp.exp((idx + 1.0)[None] * log_gamma[:, None])
    cross = jnp.einsum("bclhd,bchde,hl->bclhe", Q, state_prev, xi)
    out = (inner + cross).reshape(b, s, RET_HEADS, RET_V_DIM)
    return rms_norm(out).reshape(b, s, RET_HEADS * RET_V_DIM)

def sliding_window_attention(q, k, v, sinks, rel_bias):
    b, s = q.shape[:2]
    rep = SWA_HEADS // SWA_KV_HEADS
    nb = s // BLOCK_Q
    q32 = q.astype(jnp.float32).reshape(b, nb, BLOCK_Q, SWA_KV_HEADS, rep, SWA_HEAD_DIM) * SWA_HEAD_DIM ** -0.5

    def band(t):
        t = jnp.pad(t.astype(jnp.float32), ((0, 0), (BLOCK_Q, 0), (0, 0), (0, 0)))
        t = t.reshape(b, nb + 1, BLOCK_Q, SWA_KV_HEADS, SWA_HEAD_DIM)
        return jnp.concatenate([t[:, :-1], t[:, 1:]], axis=2)

    kb, vb = band(k), band(v)
    q_off = jnp.arange(BLOCK_Q)
    k_off = jnp.arange(2 * BLOCK_Q) - BLOCK_Q
    dist = q_off[:, None] - k_off[None, :]
    k_pos = (jnp.arange(nb) * BLOCK_Q)[:, None] + k_off[None, :]
    valid = ((dist >= 0) & (dist < WINDOW))[None] & (k_pos >= 0)[:, None, :]
    bias = jnp.transpose(rel_bias[t5_bucket(dist)], (2, 0, 1)).astype(jnp.float32)
    bias = bias.reshape(SWA_KV_HEADS, rep, BLOCK_Q, 2 * BLOCK_Q)
    logits = jnp.einsum("bnqgrd,bnkgd->bngrqk", q32, kb) + bias
    logits = jnp.where(valid[None, :, None, None], logits, -jnp.inf)
    sink = jnp.broadcast_to(sinks.astype(jnp.float32).reshape(1, 1, SWA_KV_HEADS, rep, 1, 1),
                            logits.shape[:-1] + (1,))
    p = jax.nn.softmax(jnp.concatenate([logits, sink], axis=-1), axis=-1)[..., :-1]
    out = jnp.einsum("bngrqk,bnkgd->bnqgrd", p, vb)
    return out.reshape(b, s, SWA_HEADS * SWA_HEAD_DIM).astype(q.dtype)

def even_mixer(h, w_in, conv_w, conv_b, dt_bias, A_log, D_skip, ssd_norm, lam, diff_norm, w_out,
               rel_bias, layer_idx):
    b, s, _ = h.shape
    z, xbc, dt_raw, q, k, v = split_cols(h @ w_in, EVEN_SPLITS)
    y_ssd = ssd_mixer(z, xbc, dt_raw, conv_w, conv_b, dt_bias, A_log, D_skip, ssd_norm)
    y_diff = diff_attention(q.reshape(b, s, DIFF_HEADS, 2, DIFF_HEAD_DIM),
                            k.reshape(b, s, DIFF_HEADS, 2, DIFF_HEAD_DIM),
                            v.reshape(b, s, DIFF_HEADS, 2 * DIFF_HEAD_DIM),
                            lam, diff_norm, rel_bias, layer_idx)
    return jnp.concatenate([y_ssd, y_diff], axis=-1) @ w_out

def odd_mixer(h, w_in, sinks, w_out, rel_bias):
    b, s, _ = h.shape
    rq, rk, rv, rg, sq, sk, sv = split_cols(h @ w_in, ODD_SPLITS)
    y_ret = retention(rq.reshape(b, s, RET_HEADS, RET_QK_DIM),
                      rk.reshape(b, s, RET_HEADS, RET_QK_DIM),
                      rv.reshape(b, s, RET_HEADS, RET_V_DIM))
    y_ret = (y_ret * jax.nn.silu(rg.astype(jnp.float32))).astype(h.dtype)
    y_swa = sliding_window_attention(sq.reshape(b, s, SWA_HEADS, SWA_HEAD_DIM),
                                     sk.reshape(b, s, SWA_KV_HEADS, SWA_HEAD_DIM),
                                     sv.reshape(b, s, SWA_KV_HEADS, SWA_HEAD_DIM),
                                     sinks, rel_bias)
    return jnp.concatenate([y_ret, y_swa], axis=-1) @ w_out

def squared_relu_mlp(h, w1, w2):
    return jnp.square(jax.nn.relu(h @ w1)) @ w2

def sandwich(x, c_act, sublayer, g_pre, g_post, w_mod, b_mod):
    shift, scale, gate = jnp.split(c_act @ w_mod + b_mod, 3, axis=-1)
    h = rms_norm(x, g_pre) * (1 + scale[:, None]) + shift[:, None]
    return x + gate[:, None] * rms_norm(sublayer(h), g_post)

def first_inputs(seed: int = 0) -> dict:
    key = jax.random.key(seed)
    ks = jax.random.split(key, 24)

    def nrm(k, shape, scale):
        return jax.random.normal(k, shape, jnp.float32) * scale

    dt0 = jnp.exp(jax.random.uniform(ks[11], (N_EVEN, SSD_HEADS), jnp.float32,
                                     minval=math.log(1e-3), maxval=math.log(1e-1)))
    return {
        "x": nrm(ks[0], (BATCH, SEQ, D_MODEL), 1.0),
        "c": nrm(ks[1], (BATCH, D_MODEL), 1.0),
        "rel_bias": nrm(ks[2], (REL_BUCKETS, N_BIAS_HEADS), 0.5),
        "norm_gains": 1.0 + nrm(ks[3], (DEPTH, 4, D_MODEL), 0.05),
        "mod_w": nrm(ks[4], (DEPTH, 2, D_MODEL, 3 * D_MODEL), D_MODEL ** -0.5),
        "mod_b": nrm(ks[5], (DEPTH, 2, 3 * D_MODEL), 0.02),
        "mlp_w1": nrm(ks[6], (DEPTH, D_MODEL, D_FF), D_MODEL ** -0.5),
        "mlp_w2": nrm(ks[7], (DEPTH, D_FF, D_MODEL), D_FF ** -0.5),
        "e_w_in": nrm(ks[8], (N_EVEN, D_MODEL, EVEN_IN), D_MODEL ** -0.5),
        "e_conv_w": nrm(ks[9], (N_EVEN, SSD_CONV, SSD_CONV_CH), SSD_CONV ** -0.5),
        "e_conv_b": nrm(ks[10], (N_EVEN, SSD_CONV_CH), 0.02),
        "e_dt_bias": dt0 + jnp.log(-jnp.expm1(-dt0)),
        "e_A_log": jnp.log(jax.random.uniform(ks[12], (N_EVEN, SSD_HEADS), jnp.float32, minval=1.0, maxval=16.0)),
        "e_D": 1.0 + nrm(ks[13], (N_EVEN, SSD_HEADS), 0.05),
        "e_ssd_norm": 1.0 + nrm(ks[14], (N_EVEN, SSD_D_INNER), 0.05),
        "e_lambda": nrm(ks[15], (N_EVEN, 4, DIFF_HEAD_DIM), 0.1),
        "e_diff_norm": 1.0 + nrm(ks[16], (N_EVEN, 2 * DIFF_HEAD_DIM), 0.05),
        "e_w_out": nrm(ks[17], (N_EVEN, EVEN_MIX, D_MODEL), EVEN_MIX ** -0.5),
        "o_w_in": nrm(ks[18], (N_ODD, D_MODEL, ODD_IN), D_MODEL ** -0.5),
        "o_sinks": nrm(ks[19], (N_ODD, SWA_HEADS), 0.5),
        "o_w_out": nrm(ks[20], (N_ODD, ODD_MIX, D_MODEL), ODD_MIX ** -0.5),
    }

def first_block(x, c, rel_bias, norm_gains, mod_w, mod_b, mlp_w1, mlp_w2, e_w_in, e_conv_w, e_conv_b,
              e_dt_bias, e_A_log, e_D, e_ssd_norm, e_lambda, e_diff_norm, e_w_out, o_w_in, o_sinks,
              o_w_out):
    c_act = jax.nn.silu(c)
    for layer in range(DEPTH):
        j = layer // 2
        if layer % 2 == 0:
            mixer = functools.partial(even_mixer, w_in=e_w_in[j], conv_w=e_conv_w[j], conv_b=e_conv_b[j],
                                      dt_bias=e_dt_bias[j], A_log=e_A_log[j], D_skip=e_D[j],
                                      ssd_norm=e_ssd_norm[j], lam=e_lambda[j], diff_norm=e_diff_norm[j],
                                      w_out=e_w_out[j], rel_bias=rel_bias, layer_idx=layer)
        else:
            mixer = functools.partial(odd_mixer, w_in=o_w_in[j], sinks=o_sinks[j], w_out=o_w_out[j],
                                      rel_bias=rel_bias)
        x = sandwich(x, c_act, mixer, norm_gains[layer, 0], norm_gains[layer, 1],
                     mod_w[layer, 0], mod_b[layer, 0])
        mlp = functools.partial(squared_relu_mlp, w1=mlp_w1[layer], w2=mlp_w2[layer])
        x = sandwich(x, c_act, mlp, norm_gains[layer, 2], norm_gains[layer, 3],
                     mod_w[layer, 1], mod_b[layer, 1])
    return x


HEAD_DIM = 64
N_GDN = 6
N_NSA = 6
N_NSA_KV = 2
NSA_REP = N_NSA // N_NSA_KV
N_SB = 4
D_GDN = N_GDN * HEAD_DIM
D_NSA = N_NSA * HEAD_DIM
D_NSA_KV = N_NSA_KV * HEAD_DIM
D_SB = N_SB * HEAD_DIM
D_MIX = D_GDN + D_NSA + D_SB
GDN_CONV = 4
GDN_CHUNK = 64
CMP_LEN = 32
CMP_STRIDE = 16
CMP_HIDDEN = 128
SEL_BLOCK = 64
SEL_TOPK = 16
WINDOW_2 = 512
Q_BLOCK = 128
D_FF_2 = 2816
FFN_CONV = 3
D_PLE = 256
ROPE_THETA = 10000.0
NEG = -1e30
FORCE_SCORE = 1e4
SPLIT_SIZES = (D_GDN, D_GDN, D_GDN, D_GDN, N_GDN, N_GDN,
               D_NSA, D_NSA_KV, D_NSA_KV, D_NSA_KV, D_NSA_KV, D_NSA_KV, D_NSA_KV, 3 * N_NSA,
               D_SB, D_SB, D_SB)
SPLIT_POINTS = tuple(int(c) for c in np.cumsum(SPLIT_SIZES)[:-1])
N_IN = int(sum(SPLIT_SIZES))


def rmsnorm(x, w):
    xf = x.astype(jnp.float32)
    y = xf * lax.rsqrt(jnp.mean(xf * xf, axis=-1, keepdims=True) + EPS)
    return (y * w.astype(jnp.float32)).astype(x.dtype)

def head_rmsnorm(x, w):
    b, t, c = x.shape
    return rmsnorm(x.reshape(b, t, c // HEAD_DIM, HEAD_DIM), w).reshape(b, t, c)

def l2norm(x):
    return x * lax.rsqrt(jnp.sum(x * x, axis=-1, keepdims=True) + EPS)

def causal_dwconv(x, w):
    k, c = w.shape
    return lax.conv_general_dilated(x, w[:, None, :].astype(x.dtype), window_strides=(1,),
                                    padding=[(k - 1, 0)], dimension_numbers=('NWC', 'WIO', 'NWC'),
                                    feature_group_count=c)

def rope_2(x, pos):
    half = x.shape[-1] // 2
    inv = ROPE_THETA ** (-jnp.arange(half, dtype=jnp.float32) / half)
    ang = pos.astype(jnp.float32)[..., None] * inv
    cos = jnp.cos(ang)[:, :, None, :]
    sin = jnp.sin(ang)[:, :, None, :]
    xf = x.astype(jnp.float32)
    x1, x2 = xf[..., :half], xf[..., half:]
    return jnp.concatenate([x1 * cos - x2 * sin, x2 * cos + x1 * sin], axis=-1).astype(x.dtype)

def masked_softmax(s, mask):
    s = jnp.where(mask, s, NEG)
    e = jnp.where(mask, jnp.exp(s - jnp.max(s, axis=-1, keepdims=True)), 0.0)
    return e / jnp.maximum(jnp.sum(e, axis=-1, keepdims=True), 1e-30)

def gated_deltanet(q, k, v, z, a, b_logit, conv_w, a_log, dt_bias, norm_w):
    bsz, t, _ = q.shape
    H, D, C = N_GDN, HEAD_DIM, GDN_CHUNK
    n = t // C
    f32 = jnp.float32
    qkv = jax.nn.silu(causal_dwconv(jnp.concatenate([q, k, v], axis=-1), conv_w))
    q, k, v = jnp.split(qkv, 3, axis=-1)
    to_chunks = lambda u_: u_.astype(f32).reshape(bsz, n, C, H, D).transpose(0, 3, 1, 2, 4)
    q = l2norm(to_chunks(q)) * D ** -0.5
    k = l2norm(to_chunks(k))
    v = to_chunks(v)
    beta = jax.nn.sigmoid(b_logit.astype(f32)).reshape(bsz, n, C, H).transpose(0, 3, 1, 2)
    g = -jnp.exp(a_log.astype(f32)) * jax.nn.softplus(a.astype(f32) + dt_bias.astype(f32))
    g = jnp.cumsum(g.reshape(bsz, n, C, H).transpose(0, 3, 1, 2), axis=-1)
    idx = jnp.arange(C)
    incl = idx[:, None] >= idx[None, :]
    strict = idx[:, None] > idx[None, :]
    decay = jnp.exp(jnp.where(incl, g[..., :, None] - g[..., None, :], -jnp.inf))
    k_beta = k * beta[..., None]
    lower = jnp.where(strict, jnp.einsum('bhncd,bhnsd->bhncs', k_beta, k) * decay, 0.0)
    rhs = jnp.concatenate([v * beta[..., None], k_beta * jnp.exp(g)[..., None]], axis=-1)
    sol = lax.linalg.triangular_solve(lower, rhs, left_side=True, lower=True, unit_diagonal=True)
    u, w = jnp.split(sol, 2, axis=-1)
    attn = jnp.einsum('bhncd,bhnsd->bhncs', q, k) * decay

    def step(state, xs):
        q_i, k_i, u_i, w_i, g_i, a_i = xs
        v_new = u_i - jnp.einsum('bhcd,bhde->bhce', w_i, state)
        o_i = (jnp.einsum('bhcd,bhde->bhce', q_i * jnp.exp(g_i)[..., None], state)
               + jnp.einsum('bhcs,bhse->bhce', a_i, v_new))
        g_last = g_i[..., -1:]
        state = (state * jnp.exp(g_last)[..., None]
                 + jnp.einsum('bhcd,bhce->bhde', k_i * jnp.exp(g_last - g_i)[..., None], v_new))
        return state, o_i

    xs = tuple(jnp.moveaxis(t_, 2, 0) for t_ in (q, k, u, w, g, attn))
    _, o = lax.scan(step, jnp.zeros((bsz, H, D, D), f32), xs)
    o = o.transpose(1, 0, 3, 2, 4).reshape(bsz, t, H, D)
    o = rmsnorm(o, norm_w) * jax.nn.silu(z.astype(f32).reshape(bsz, t, H, D))
    return o.reshape(bsz, t, D_GDN).astype(z.dtype)

def compress(kv, pe, w1, w2):
    b, t, g, d = kv.shape
    n_cmp = (t - CMP_LEN) // CMP_STRIDE + 1
    idx = jnp.arange(n_cmp)[:, None] * CMP_STRIDE + jnp.arange(CMP_LEN)[None, :]
    blocks = kv[:, idx] + pe[None, None, :, None, :]
    blocks = blocks.transpose(0, 1, 3, 2, 4).reshape(b, n_cmp, g, CMP_LEN * d)
    return jax.nn.silu(blocks @ w1) @ w2

def native_sparse_attention(q, k_cmp, v_cmp, k_slc, v_slc, k_win, v_win, gates, positions,
                            pe_k, pe_v, ck_w1, ck_w2, cv_w1, cv_w2):
    b, t, _ = q.shape
    G, R, D = N_NSA_KV, NSA_REP, HEAD_DIM
    scale = D ** -0.5
    f32 = jnp.float32
    q = rope_2(q.reshape(b, t, N_NSA, D), positions).reshape(b, t, G, R, D)
    kv = lambda z_: z_.reshape(b, t, G, D)
    kc = compress(rope_2(kv(k_cmp), positions), pe_k, ck_w1, ck_w2)
    vc = compress(kv(v_cmp), pe_v, cv_w1, cv_w2)
    n_cmp = kc.shape[1]
    n_sel = t // SEL_BLOCK
    top_k = min(SEL_TOPK, n_sel)
    ks_blk = rope_2(kv(k_slc), positions).reshape(b, n_sel, SEL_BLOCK, G, D).transpose(0, 3, 1, 2, 4)
    vs_blk = kv(v_slc).reshape(b, n_sel, SEL_BLOCK, G, D).transpose(0, 3, 1, 2, 4)
    pad = ((0, 0), (WINDOW_2, 0), (0, 0), (0, 0))
    kw_pad = jnp.pad(rope_2(kv(k_win), positions), pad)
    vw_pad = jnp.pad(kv(v_win), pad)
    c0 = jnp.arange(n_cmp) * CMP_STRIDE
    s0 = jnp.arange(n_sel) * SEL_BLOCK
    overlap = jnp.clip(jnp.minimum(c0[:, None] + CMP_LEN, s0[None, :] + SEL_BLOCK)
                       - jnp.maximum(c0[:, None], s0[None, :]), 0).astype(f32) / CMP_LEN
    cmp_end = c0 + CMP_LEN - 1
    b_idx = jnp.arange(b)[:, None, None, None]
    g_idx = jnp.arange(G)[None, :, None, None]
    blk = jnp.arange(n_sel)

    def block(args):
        qb, gb, q0 = args
        tq = q0 + jnp.arange(Q_BLOCK)
        s_c = jnp.einsum('bqgrd,bigd->bgrqi', qb, kc).astype(f32) * scale
        p_c = masked_softmax(s_c, cmp_end[None, :] <= tq[:, None])
        o_c = jnp.einsum('bgrqi,bigd->bqgrd', p_c.astype(vc.dtype), vc)
        imp = jnp.einsum('bgrqi,ij->bgqj', p_c, overlap)
        cur = tq // SEL_BLOCK
        forced = (blk[None, :] == 0) | (blk[None, :] == cur[:, None]) | (blk[None, :] == cur[:, None] - 1)
        visible = blk[None, :] * SEL_BLOCK <= tq[:, None]
        score = jnp.where(forced, FORCE_SCORE, jnp.where(visible, imp, -1.0))
        _, sel = lax.top_k(score, top_k)
        k_sel = ks_blk[b_idx, g_idx, sel].reshape(b, G, Q_BLOCK, top_k * SEL_BLOCK, D)
        v_sel = vs_blk[b_idx, g_idx, sel].reshape(b, G, Q_BLOCK, top_k * SEL_BLOCK, D)
        key_pos = (sel[..., None] * SEL_BLOCK + jnp.arange(SEL_BLOCK)).reshape(b, G, 1, Q_BLOCK, top_k * SEL_BLOCK)
        s_s = jnp.einsum('bqgrd,bgqnd->bgrqn', qb, k_sel).astype(f32) * scale
        p_s = masked_softmax(s_s, key_pos <= tq[:, None])
        o_s = jnp.einsum('bgrqn,bgqnd->bqgrd', p_s.astype(v_sel.dtype), v_sel)
        kw = lax.dynamic_slice_in_dim(kw_pad, q0, WINDOW_2 + Q_BLOCK, axis=1)
        vw = lax.dynamic_slice_in_dim(vw_pad, q0, WINDOW_2 + Q_BLOCK, axis=1)
        pos_w = q0 - WINDOW_2 + jnp.arange(WINDOW_2 + Q_BLOCK)
        diff = tq[:, None] - pos_w[None, :]
        m_w = (diff >= 0) & (diff < WINDOW_2) & (pos_w >= 0)[None, :]
        s_w = jnp.einsum('bqgrd,bngd->bgrqn', qb, kw).astype(f32) * scale
        p_w = masked_softmax(s_w, m_w)
        o_w = jnp.einsum('bgrqn,bngd->bqgrd', p_w.astype(vw.dtype), vw)
        gt = jax.nn.sigmoid(gb.astype(f32))[..., None]
        return (gt[:, :, 0] * o_c + gt[:, :, 1] * o_s + gt[:, :, 2] * o_w).astype(qb.dtype)

    nb = t // Q_BLOCK
    q_blocks = q.reshape(b, nb, Q_BLOCK, G, R, D).transpose(1, 0, 2, 3, 4, 5)
    g_blocks = gates.reshape(b, nb, Q_BLOCK, 3, G, R).transpose(1, 0, 2, 3, 4, 5)
    out = lax.map(block, (q_blocks, g_blocks, jnp.arange(nb) * Q_BLOCK))
    return out.transpose(1, 0, 2, 3, 4, 5).reshape(b, t, D_NSA)

def stick_breaking_attention(q, k, v):
    b, t, _ = q.shape
    H, D = N_SB, HEAD_DIM
    scale = D ** -0.5
    k = k.reshape(b, t, H, D)
    v = v.reshape(b, t, H, D)
    nb = t // Q_BLOCK
    q_blocks = q.reshape(b, nb, Q_BLOCK, H, D).transpose(1, 0, 2, 3, 4)
    key_pos = jnp.arange(t)

    def block(args):
        qb, q0 = args
        tq = q0 + jnp.arange(Q_BLOCK)
        strict = key_pos[None, :] < tq[:, None]
        z = jnp.einsum('bqhd,bkhd->bhqk', qb, k).astype(jnp.float32) * scale
        log_1m = jnp.where(strict, jax.nn.log_sigmoid(-z), 0.0)
        log_stick = lax.cumsum(log_1m, axis=3, reverse=True) - log_1m
        a = jnp.where(strict, jnp.exp(jax.nn.log_sigmoid(z) + log_stick), 0.0)
        return jnp.einsum('bhqk,bkhd->bqhd', a.astype(v.dtype), v)

    out = lax.map(block, (q_blocks, jnp.arange(nb) * Q_BLOCK))
    return out.transpose(1, 0, 2, 3, 4).reshape(b, t, D_SB)

def conv_ffn(x, w_up, conv_w, w_down):
    u = causal_dwconv(x @ w_up, conv_w)
    gate, up = jnp.split(u, 2, axis=-1)
    return (jax.nn.silu(gate) * up) @ w_down

def second_inputs(seed: int = 0) -> dict:
    key = jax.random.key(seed)
    keys = iter(jax.random.split(key, 40))
    f32 = jnp.float32

    def normal(shape, scale):
        return jax.random.normal(next(keys), shape, f32) * scale

    def gain(shape):
        return 1.0 + 0.01 * jax.random.normal(next(keys), shape, f32)

    x = normal((BATCH, SEQ, D_MODEL), 1.0)
    p = normal((DEPTH, BATCH, SEQ, D_PLE), 1.0)
    positions = (jax.random.randint(next(keys), (BATCH, 1), 0, 1024, jnp.int32)
                 + jnp.arange(SEQ, dtype=jnp.int32)[None, :])
    a_log = jnp.log(jax.random.uniform(next(keys), (DEPTH, N_GDN), f32, 1.0, 16.0))
    dt = jnp.exp(jax.random.uniform(next(keys), (DEPTH, N_GDN), f32, -6.907755, -2.302585))
    dt_bias = dt + jnp.log(-jnp.expm1(-dt))
    return {
        'x': x,
        'p': p,
        'positions': positions,
        'ln_mix': gain((DEPTH, D_MODEL)),
        'w_in': normal((DEPTH, D_MODEL, N_IN), D_MODEL ** -0.5),
        'gdn_conv': normal((DEPTH, GDN_CONV, 3 * D_GDN), GDN_CONV ** -0.5),
        'gdn_a_log': a_log,
        'gdn_dt_bias': dt_bias,
        'gdn_norm': gain((DEPTH, HEAD_DIM)),
        'nsa_pe_k': normal((DEPTH, CMP_LEN, HEAD_DIM), 0.1),
        'nsa_pe_v': normal((DEPTH, CMP_LEN, HEAD_DIM), 0.1),
        'nsa_cmp_k_w1': normal((DEPTH, CMP_LEN * HEAD_DIM, CMP_HIDDEN), (CMP_LEN * HEAD_DIM) ** -0.5),
        'nsa_cmp_k_w2': normal((DEPTH, CMP_HIDDEN, HEAD_DIM), CMP_HIDDEN ** -0.5),
        'nsa_cmp_v_w1': normal((DEPTH, CMP_LEN * HEAD_DIM, CMP_HIDDEN), (CMP_LEN * HEAD_DIM) ** -0.5),
        'nsa_cmp_v_w2': normal((DEPTH, CMP_HIDDEN, HEAD_DIM), CMP_HIDDEN ** -0.5),
        'nsa_norm': gain((DEPTH, HEAD_DIM)),
        'sb_norm': gain((DEPTH, HEAD_DIM)),
        'w_out': normal((DEPTH, D_MIX, D_MODEL), D_MIX ** -0.5),
        'ln_ffn': gain((DEPTH, D_MODEL)),
        'w_up': normal((DEPTH, D_MODEL, 2 * D_FF_2), D_MODEL ** -0.5),
        'ffn_conv': normal((DEPTH, FFN_CONV, 2 * D_FF_2), FFN_CONV ** -0.5),
        'w_down': normal((DEPTH, D_FF_2, D_MODEL), D_FF_2 ** -0.5),
        'ln_ple': gain((DEPTH, D_MODEL)),
        'w_ple_gate': normal((DEPTH, D_MODEL, D_MODEL), D_MODEL ** -0.5),
        'w_ple': normal((DEPTH, D_PLE, D_MODEL), D_PLE ** -0.5),
        'ple_norm': gain((DEPTH, D_MODEL)),
        'ln_final': gain((D_MODEL,)),
    }

def second_block(x, p, positions, ln_mix, w_in, gdn_conv, gdn_a_log, gdn_dt_bias, gdn_norm,
              nsa_pe_k, nsa_pe_v, nsa_cmp_k_w1, nsa_cmp_k_w2, nsa_cmp_v_w1, nsa_cmp_v_w2,
              nsa_norm, sb_norm, w_out, ln_ffn, w_up, ffn_conv, w_down,
              ln_ple, w_ple_gate, w_ple, ple_norm, ln_final):
    h = x
    for i in range(DEPTH):
        hn = rmsnorm(h, ln_mix[i])
        (g_q, g_k, g_v, g_z, g_a, g_b,
         n_q, n_kc, n_vc, n_ks, n_vs, n_kw, n_vw, n_gate,
         s_q, s_k, s_v) = jnp.split(hn @ w_in[i], SPLIT_POINTS, axis=-1)
        o_gdn = gated_deltanet(g_q, g_k, g_v, g_z, g_a, g_b, gdn_conv[i], gdn_a_log[i],
                               gdn_dt_bias[i], gdn_norm[i])
        o_nsa = native_sparse_attention(n_q, n_kc, n_vc, n_ks, n_vs, n_kw, n_vw, n_gate, positions,
                                        nsa_pe_k[i], nsa_pe_v[i], nsa_cmp_k_w1[i], nsa_cmp_k_w2[i],
                                        nsa_cmp_v_w1[i], nsa_cmp_v_w2[i])
        o_sb = stick_breaking_attention(s_q, s_k, s_v)
        mix = jnp.concatenate([o_gdn, head_rmsnorm(o_nsa, nsa_norm[i]), head_rmsnorm(o_sb, sb_norm[i])], axis=-1)
        h = h + mix @ w_out[i]
        h = h + conv_ffn(rmsnorm(h, ln_ffn[i]), w_up[i], ffn_conv[i], w_down[i])
        gate = jax.nn.sigmoid(rmsnorm(h, ln_ple[i]) @ w_ple_gate[i])
        h = h + gate * rmsnorm(p[i] @ w_ple[i], ple_norm[i])
    return rmsnorm(h, ln_final)


def setup_inputs(seed=0):
    out = dict(first_inputs(seed))
    for name, value in second_inputs(seed + 1).items():
        if name != "x":
            out[name + "_2"] = value
    return out


def reference(
    x, c, rel_bias, norm_gains, mod_w, mod_b, mlp_w1, mlp_w2, e_w_in, e_conv_w, e_conv_b,
    e_dt_bias, e_A_log, e_D, e_ssd_norm, e_lambda, e_diff_norm, e_w_out, o_w_in, o_sinks,
    o_w_out, p_2, positions_2, ln_mix_2, w_in_2, gdn_conv_2, gdn_a_log_2, gdn_dt_bias_2,
    gdn_norm_2, nsa_pe_k_2, nsa_pe_v_2, nsa_cmp_k_w1_2, nsa_cmp_k_w2_2, nsa_cmp_v_w1_2,
    nsa_cmp_v_w2_2, nsa_norm_2, sb_norm_2, w_out_2, ln_ffn_2, w_up_2, ffn_conv_2, w_down_2,
    ln_ple_2, w_ple_gate_2, w_ple_2, ple_norm_2, ln_final_2,
):
    x = first_block(
        x, c, rel_bias, norm_gains, mod_w, mod_b, mlp_w1, mlp_w2, e_w_in, e_conv_w, e_conv_b,
        e_dt_bias, e_A_log, e_D, e_ssd_norm, e_lambda, e_diff_norm, e_w_out, o_w_in, o_sinks,
        o_w_out,
    )
    return second_block(
        x, p_2, positions_2, ln_mix_2, w_in_2, gdn_conv_2, gdn_a_log_2, gdn_dt_bias_2,
        gdn_norm_2, nsa_pe_k_2, nsa_pe_v_2, nsa_cmp_k_w1_2, nsa_cmp_k_w2_2, nsa_cmp_v_w1_2,
        nsa_cmp_v_w2_2, nsa_norm_2, sb_norm_2, w_out_2, ln_ffn_2, w_up_2, ffn_conv_2, w_down_2,
        ln_ple_2, w_ple_gate_2, w_ple_2, ple_norm_2, ln_final_2,
    )


_drawn_inputs = setup_inputs


def setup_inputs(seed=0):
    import zlib

    import numpy as np

    out = dict(_drawn_inputs(seed))
    spreads = {}
    factors = {'e_conv_b': 5.192,
     'e_D': 8.0,
     'o_sinks': 8.0,
     'ln_mix_2': 6.505,
     'gdn_norm_2': 23.199,
     'nsa_pe_k_2': 8.0,
     'nsa_norm_2': 64.0,
     'sb_norm_2': 64.0,
     'ln_ffn_2': 8.0,
     'ln_ple_2': 64.0,
     'ple_norm_2': 184.601,
     'ln_final_2': 170.0,
     'nsa_pe_v_2': 8.0}
    for name, (base, spread) in spreads.items():
        noise = np.random.default_rng([zlib.crc32(name.encode()), seed]).standard_normal(out[name].shape)
        drawn = base * np.exp(spread * noise) if base else spread * noise
        out[name] = jnp.asarray(drawn.astype(out[name].dtype))
    for name, factor in factors.items():
        out[name] = (out[name] * factor).astype(out[name].dtype)
    return out
```

```python
from contextlib import ExitStack, contextmanager

import numpy as np

import concourse.bass as bass
from concourse import mybir

P = 128
F32 = mybir.dt.float32
I32 = mybir.dt.int32
ACT = mybir.ActivationFunctionType
ALU = mybir.AluOpType
AX = mybir.AxisListType.X

D = 1024
DT = D // P
S = 512
TC = S // P
EPS = 1e-6
NEG = -1e30
COLS = 512
SLOTS = 2


@contextmanager
def stage(nc, names):
    with ExitStack() as ctx:
        sems = [ctx.enter_context(nc.semaphore(n)) for n in names.split()]
        with nc.Block() as block:
            yield (block, *sems)
        for s in sems:
            nc.gpsimd.sem_clear(s)
        nc.all_engine_barrier()


def constants():
    i = np.arange(P)
    c = {}
    c["ident"] = np.eye(P)
    c["ones"] = np.ones((P, P))
    c["upto"] = i[:, None] <= i[None, :]
    c["after"] = i[:, None] > i[None, :]
    c["flip"] = np.eye(P)[::-1]
    c["causal"] = np.where(i[None, :] > i[:, None], NEG, 0.0)
    dist = i[:, None] - np.arange(BAND)[None, :] + P
    c["window"] = np.where((dist >= 0) & (dist < P), 0.0, NEG)
    c["swap_128"] = np.eye(P)[(i + 64) % P]
    c["eps"] = np.full((P, 1), EPS)
    return c


def second_constants():
    i = np.arange(P)
    same = (i[:, None] // 64) == (i[None, :] // 64)
    causal = np.where(i[None, :] > i[:, None], NEG, 0.0)
    c = {}
    c["causal_row"] = np.concatenate([np.zeros((P, S - P)), causal], axis=1)
    c["strict_row"] = np.concatenate([np.where(i[None, :] <= i[:, None], NEG, 0.0), np.zeros((P, S - P))], axis=1)
    c["from_here"] = i[:, None] >= i[None, :]
    c["upto_64"] = (i[:, None] <= i[None, :]) & same
    c["after_64"] = (i[:, None] > i[None, :]) & same
    c["ones_64"] = same
    c["swap_32"] = np.eye(P)[i ^ 32]
    for level in range(6):
        n = 1 << level
        c[f"level_{level}"] = ((i[:, None] // (2 * n) == i[None, :] // (2 * n)) & (i[:, None] // n % 2 == 0) & (i[None, :] // n % 2 == 1))
    c["first_mask"] = c["level_0"].T
    inv = np.float32(10000.0) ** (-np.arange(32, dtype=np.float32) / 32)
    c["inv_freq"] = inv[i % 32][:, None]
    c["half_sign"] = np.where(i % 64 < 32, -1.0, 1.0)[:, None]
    ends = np.arange(N_CMP) * CMP_STRIDE + CMP_LEN - 1
    seen = ends[None, None, :] <= (np.arange(TC)[None, :, None] * P + i[:, None, None])
    c["cmp_keep"] = seen.reshape(P, -1)
    c["cmp_add"] = np.where(seen, 0.0, NEG).reshape(P, -1)
    return c


class Kit:

    def __init__(self, nc):
        self.nc = nc
        self.named = {}
        self.at = {}

    def unique(self, name):
        self.named[name] = self.named.get(name, 0) + 1
        return name if self.named[name] == 1 else f"{name}_{self.named[name]}"

    def sbuf(self, name, shape, dtype=F32):
        return self.nc.sbuf_tensor(self.unique(name), shape, dtype)

    def psum(self, name, shape):
        return self.nc.psum_tensor(self.unique(name), shape, F32)


def load_inputs(k, a):
    nc = k.nc
    with (
        k.sbuf("x_rows", [P, TC, D]) as x_rows,
        k.sbuf("vec_rows", [P, 3, P]) as vec_rows,
        k.psum("turned", [P, 8, S]) as turned,
        stage(nc, "const_in x_in rows_in x_turned x_out vec_turned vec_out_a") as
        (block, const_in, x_in, rows_in, x_turned, x_out, vec_turned, vec_out),
    ):
        rows = [
            (0, 0, 64, a["norm_gains"].rearrange("l n (f p) -> (l n f) p", p=P)),
            (0, 64, 64, a["e_conv_w"].rearrange("a t (f p) -> (a t f) p", p=P)),
            (1, 0, 96, a["mod_b"].rearrange("l s (f p) -> (l s f) p", p=P)),
            (1, 96, 16, a["e_conv_b"].rearrange("a (f p) -> (a f) p", p=P)),
            (1, 112, 8, a["e_ssd_norm"].rearrange("a (f p) -> (a f) p", p=P)),
            (1, 120, 8, a["c"].rearrange("a (f p) -> (a f) p", p=P)),
            (2, 0, 1, a["e_diff_norm"]),
        ]
        used = (P, P, 1)

        @block.sync
        def _(sp):
            sp.dma_start(k.const[:, :], a["const"]).then_inc(const_in, 16)
            for c in range(TC):
                sp.dma_start(x_rows[:, c, :], a["x"][0, c * P:(c + 1) * P, :]).then_inc(x_in, 16)
            for g, at, n, src in rows:
                sp.dma_start(vec_rows[at:at + n, g, :], src).then_inc(rows_in, 16)

        @block.tensor
        def _(pe):
            pe.wait_ge(const_in, 16)
            pe.wait_ge(x_in, 16 * TC)
            for f in range(DT):
                for c in range(TC):
                    last = nc.tensor.transpose(turned[:, f, c * P:(c + 1) * P],
                                               x_rows[:, c, f * P:(f + 1) * P], k.at["ident"])
                last.then_inc(x_turned, 1)
            pe.wait_ge(rows_in, 16 * len(rows))
            for g in range(3):
                pe.wait_ge(x_out, g + 1)
                n = used[g]
                nc.tensor.transpose(turned[:, g, 0:n], vec_rows[0:n, g, :],
                                    k.at["ident"][0:n, 0:n]).then_inc(vec_turned, 1)

        @block.vector
        def _(dve):
            for f in range(DT):
                dve.wait_ge(x_turned, f + 1)
                nc.vector.tensor_copy(k.xT[:, f, :], turned[:, f, :]).then_inc(x_out, 1)
            for g in range(3):
                dve.wait_ge(vec_turned, g + 1)
                nc.vector.tensor_copy(k.vec[:, g * P:g * P + used[g]], turned[:, g, 0:used[g]]).then_inc(vec_out, 1)

        @block.scalar
        def _(act):
            act.wait_ge(vec_out, 2)
            nc.scalar.activation(k.c_act, k.vec[:, P + 120:P + 128], ACT.Silu)


def modulation(k, a):
    nc = k.nc
    tiles = 3 * D // COLS
    w = a["mod_w"].rearrange("l s (k p) n -> (l s) p k n", p=P)
    with (
        k.sbuf("acc", [P, 2, COLS]) as acc,
        k.psum("mod_cols", [P, 96]) as mod_cols,
        stage(nc, "landed0 landed1 summed freed cols_done mod_ready") as
        (block, landed0, landed1, summed, freed, cols_done, mod_ready),
    ):
        landed = (landed0, landed1)

        @block.sync
        def _(sp):
            with sp.Fori(0, 4) as s:
                for j in range(tiles):
                    sp.wait_ge(freed, s * tiles + j + 1)
                    sp.dma_start(k.ring[:, j % 2, :, :],
                                 w[bass.ds(s, 1), :, :, j * COLS:(j + 1) * COLS].rearrange("a p k n -> p (a k) n")
                                 ).then_inc(landed[j % 2], 16)

        @block.vector
        def _(dve):
            dve.sem_inc(freed, 2)
            with dve.Fori(0, 4) as s:
                for j in range(tiles):
                    dve.wait_ge(landed[j % 2], s * (8 * tiles) + 16 * (j // 2) + 16)
                    dve.wait_ge(cols_done, s * tiles + j + 1)
                    for c in range(DT):
                        if c == 0:
                            step = nc.vector.tensor_scalar(acc[:, j % 2, :], k.ring[:, j % 2, c, :],
                                                           k.c_act[:, c:c + 1], None, ALU.mult)
                        else:
                            dve.wait_ge(summed, s * (tiles * DT) + j * DT + c)
                            step = nc.vector.scalar_tensor_tensor(acc[:, j % 2, :], k.ring[:, j % 2, c, :],
                                                                  k.c_act[:, c:c + 1], acc[:, j % 2, :],
                                                                  ALU.mult, ALU.add)
                        step.then_inc(summed, 1)
                    dve.wait_ge(summed, s * (tiles * DT) + (j + 1) * DT)
                    dve.sem_inc(freed, 1)
            dve.wait_ge(cols_done, 4 * tiles + 2)
            nc.vector.tensor_tensor(k.mod[:, :], mod_cols[:, :], k.vec[:, P:P + 96], ALU.add).then_inc(mod_ready, 1)
            dve.wait_ge(mod_ready, 1)
            for s in range(4):
                pre = k.vec[:, (2 * s) * DT:(2 * s + 1) * DT]
                post = k.vec[:, (2 * s + 1) * DT:(2 * s + 2) * DT]
                nc.vector.scalar_tensor_tensor(k.pre_gain[:, s, :], k.mod[:, s * 24 + DT:s * 24 + 2 * DT], 1.0, pre,
                                               ALU.add, ALU.mult)
                nc.vector.tensor_tensor(k.post_gain[:, s, :], k.mod[:, s * 24 + 2 * DT:s * 24 + 3 * DT], post, ALU.mult)

        @block.tensor
        def _(pe):
            pe.sem_inc(cols_done, 2)
            with pe.Fori(0, 4) as s:
                for j in range(tiles):
                    pe.wait_ge(summed, s * (tiles * DT) + (j + 1) * DT)
                    for q in range(4):
                        last = nc.tensor.matmul(mod_cols[:, bass.ds(s * 24 + (j * 4 + q), 1)], acc[:, j % 2, q * P:(q + 1) * P],
                                                k.at["ones"][:, 0:1], start=True, stop=True)
                    last.then_inc(cols_done, 1)


def norm_into(k, gain, shift=None):
    nc = k.nc
    with (
        k.sbuf("log_ms", [P, S]) as log_ms,
        k.sbuf("rstd", [P, S]) as rstd,
        k.psum("stat", [P, S]) as stat,
        stage(nc, "squared stat_done log_done rstd_done scaled") as
        (block, squared, stat_done, log_done, rstd_done, scaled),
    ):
        @block.scalar
        def _(act):
            for f in range(DT):
                nc.scalar.activation(k.hT[:, f, :], k.xT[:, f, :], ACT.Square).then_inc(squared, 1)
            act.wait_ge(stat_done, 1)
            inverse_root(k, act, rstd[:, :], log_ms[:, :], stat[:, :], 1.0 / D, log_done).then_inc(rstd_done, 1)
            if shift is not None:
                for f in range(DT):
                    act.wait_ge(scaled, f + 1)
                    nc.scalar.activation(k.hT[:, f, :], k.hT[:, f, :], ACT.Identity, bias=shift(f))

        @block.tensor
        def _(pe):
            for f in range(DT):
                pe.wait_ge(squared, f + 1)
                last = nc.tensor.matmul(stat[:, :], k.at["ones"], k.hT[:, f, :], start=(f == 0), stop=(f == DT - 1))
            last.then_inc(stat_done, 1)

        @block.vector
        def _(dve):
            dve.wait_ge(rstd_done, 1)
            for f in range(DT):
                nc.vector.scalar_tensor_tensor(k.hT[:, f, :], k.xT[:, f, :], gain(f), rstd[:, :],
                                               ALU.mult, ALU.mult).then_inc(scaled, 1)


def inverse_root(k, act, out, log, total, scale, log_done, nth=1):
    nc = k.nc
    nc.scalar.activation(log, total, ACT.Ln, bias=k.at["eps"][0:log.shape[0], :], scale=scale).then_inc(log_done, 1)
    act.wait_ge(log_done, nth)
    return nc.scalar.activation(out, log, ACT.Exp, scale=-0.5)


def project(k, n_tiles, w_tile, evac, rows=False, after=None, parts=1):
    nc = k.nc
    hT = k.hT
    width = COLS
    with (
        k.psum("out", [P, 2, 4, S]) as out,
        stage(nc, "landed0 landed1 bank_done act_freed dve_freed") as
        (block, landed0, landed1, bank_done, act_freed, dve_freed),
    ):
        landed = (landed0, landed1)

        @block.sync
        def _(sp):
            def load(i, u):
                sp.wait_ge(bank_done, (2 * i + u) * 4 + 4)
                for part in range(parts):
                    n = width // parts
                    sp.dma_start(k.ring[:, u, :, part * n:(part + 1) * n],
                                 w_tile(2 * i + u) if parts == 1 else w_tile(2 * i + u, part)).then_inc(landed[u], 16)
            pairs(sp, n_tiles, load)

        @block.tensor
        def _(pe):
            pe.sem_inc(bank_done, 8)

            def multiply(i, u):
                pe.wait_ge(landed[u], i * (16 * parts) + 16 * parts)
                for j in range(4):
                    pe.wait_ge((act_freed, dve_freed)[j % 2], (2 * i + u) * 2 + j // 2 + 1)
                    for c in range(DT):
                        if rows:
                            last = nc.tensor.matmul(out[:, u, j, 0:width], hT[:, c, j * P:(j + 1) * P],
                                                    k.ring[:, u, c, 0:width], start=(c == 0), stop=(c == DT - 1))
                        else:
                            last = nc.tensor.matmul(out[:, u, j, :], k.ring[:, u, c, j * P:(j + 1) * P],
                                                    hT[:, c, :], start=(c == 0), stop=(c == DT - 1))
                    last.then_inc(bank_done, 1)
            pairs(pe, n_tiles, multiply)

        @block.scalar
        def _(act):
            act.sem_inc(act_freed, 4)

            def empty(i, u):
                for j in (0, 2):
                    act.wait_ge(bank_done, (2 * i + u) * 4 + j + 9)
                    evac("act", 2 * i + u, j, out[:, u, j, 0:width if rows else S]).then_inc(act_freed, 1)
            pairs(act, n_tiles, empty)

        @block.vector
        def _(dve):
            dve.sem_inc(dve_freed, 4)

            def empty(i, u):
                for j in (1, 3):
                    dve.wait_ge(bank_done, (2 * i + u) * 4 + j + 9)
                    evac("dve", 2 * i + u, j, out[:, u, j, 0:width if rows else S]).then_inc(dve_freed, 1)
            pairs(dve, n_tiles, empty)

        @block.gpsimd
        def _(pool):
            def finish(i, u):
                for j in range(4):
                    pool.wait_ge((act_freed, dve_freed)[j % 2], (2 * i + u) * 2 + j // 2 + 5)
                    after(2 * i + u, j)
            if after is not None:
                pairs(pool, n_tiles, finish)


def copy_out(nc, engine, dst, src, scale=None):
    if engine == "act":
        return nc.scalar.activation(dst, src, ACT.Copy, scale=1.0 if scale is None else scale)
    if scale is None:
        return nc.vector.tensor_copy(dst, src)
    return nc.vector.tensor_scalar(dst, src, scale, None, ALU.mult)



SSD_HEADS, SSD_P, SSD_G = 16, 64, 4
CONV = 4
XBC_T = 16
E_Z, E_XBC, E_DT, E_Q, E_K, E_V = 0, 1024, 3072, 3088, 4112, 5136


def weight_tiles(w, col):
    v = w.rearrange("(k p) n -> p k n", p=P)
    return lambda t: v[:, :, bass.ds(t * COLS + col, COLS)]


def conv_silu(k, raw, n_tiles, taps, width, tap_col, bias_col):
    nc = k.nc
    pad = taps - 1
    with (
        k.sbuf("conv_acc", [P, 2, width]) as acc,
        stage(nc, "padded tap_done silu_done") as (block, padded, tap_done, silu_done),
    ):
        @block.vector
        def _(dve):
            nc.vector.memset(raw[:, :, 0:pad], 0.0).then_inc(padded, 1)
            dve.wait_ge(padded, 1)

            def taps_of(i, u):
                    t = 2 * i + u
                    dve.wait_ge(silu_done, 2 * i + u + 1)
                    for j in range(taps):
                        x = raw[:, bass.ds(t, 1), j:j + width].rearrange("p a n -> p (a n)")
                        if j == 0:
                            step = nc.vector.tensor_scalar(acc[:, u, :], x, tap_col(t, j), None, ALU.mult)
                        else:
                            dve.wait_ge(tap_done, (2 * i + u) * taps + j)
                            step = nc.vector.scalar_tensor_tensor(acc[:, u, :], x, tap_col(t, j), acc[:, u, :],
                                                                  ALU.mult, ALU.add)
                        step.then_inc(tap_done, 1)
            pairs(dve, n_tiles, taps_of)

        @block.scalar
        def _(act):
            act.sem_inc(silu_done, 2)

            def finish(i, u):
                    t = 2 * i + u
                    act.wait_ge(tap_done, (2 * i + u) * taps + taps)
                    out = raw[:, bass.ds(t, 1), pad:pad + width].rearrange("p a n -> p (a n)")
                    if bias_col is None:
                        step = nc.scalar.activation(out, acc[:, u, :], ACT.Silu)
                    else:
                        step = nc.scalar.activation(out, acc[:, u, :], ACT.Silu, bias=bias_col(t))
                    step.then_inc(silu_done, 1)
            pairs(act, n_tiles, finish)


def ssd_steps(k, a, dt, dt_a, eacs, to_end, total):
    nc = k.nc
    H = SSD_HEADS
    n = TC * H
    w = a["e_w_in"][0].rearrange("(k p) n -> p k n", p=P)
    with (
        k.sbuf("w_dt", [P, DT, H]) as w_dt,
        k.sbuf("rows", [P, 3, H]) as rows,
        k.sbuf("tmp", [P, 6, n]) as tmp,
        k.psum("dt_ps", [P, n]) as dt_ps,
        k.psum("sums", [P, 3, S]) as sums,
        stage(nc, "w_in rows_in dt_done step neg_a exp_done log_done sum_done") as
        (block, w_in, rows_in, dt_done, step, neg_a, exp_done, log_done, sum_done),
    ):
        v, mag, u, w1, corr, neg = (tmp[:, i, :] for i in range(6))

        @block.sync
        def _(sp):
            sp.dma_start(w_dt[:, :, :], w[:, :, E_DT:E_DT + H]).then_inc(w_in, 16)
            for i, name in enumerate(("e_dt_bias", "e_A_log", "e_D")):
                sp.dma_start(rows[:, i, :], a[name][0].partition_broadcast(P)).then_inc(rows_in, 16)

        @block.tensor
        def _(pe):
            pe.wait_ge(w_in, 16)
            for c in range(TC):
                for f in range(DT):
                    last = nc.tensor.matmul(dt_ps[:, c * H:(c + 1) * H], k.hT[:, f, c * P:(c + 1) * P], w_dt[:, f, :],
                                            start=(f == 0), stop=(f == DT - 1))
            last.then_inc(dt_done, 1)
            pe.wait_ge(step, 9)
            for i, m in enumerate((k.at["upto"], k.at["after"], k.at["ones"])):
                last = nc.tensor.matmul(sums[:, i, 0:n], m, dt_a, start=True, stop=True)
            last.then_inc(sum_done, 1)

        @block.scalar
        def _(act):
            act.wait_ge(rows_in, 48)
            nc.scalar.activation(k.ssd_d, rows[:, 2, :], ACT.Copy)
            nc.scalar.activation(neg[:, 0:H], rows[:, 1, :], ACT.Exp).then_inc(neg_a, 1)
            act.wait_ge(step, 2)
            nc.scalar.activation(u, mag, ACT.Exp, scale=-1.0).then_inc(exp_done, 1)
            act.wait_ge(step, 3)
            nc.scalar.activation(mag, w1, ACT.Ln).then_inc(log_done, 1)
            act.wait_ge(sum_done, 1)
            for i, out in enumerate((eacs, to_end, total)):
                nc.scalar.activation(out, sums[:, i, 0:n], ACT.Exp)

        @block.vector
        def _(dve):
            def per_head(row):
                return row.unsqueeze(1).to_broadcast([P, TC, H])

            def by_chunk(x):
                return x.rearrange("p (c h) -> p c h", h=H)

            dve.wait_ge(dt_done, 1)
            dve.wait_ge(rows_in, 48)
            nc.vector.tensor_tensor(by_chunk(v), by_chunk(dt_ps[:, :]), per_head(rows[:, 0, :]), ALU.add).then_inc(step, 1)
            dve.wait_ge(step, 1)
            nc.vector.scalar_tensor_tensor(mag, v, -1.0, v, ALU.mult, ALU.max).then_inc(step, 1)
            dve.wait_ge(exp_done, 1)
            nc.vector.tensor_scalar(w1, u, 1.0, None, ALU.add).then_inc(step, 1)
            dve.wait_ge(step, 3)
            nc.vector.tensor_scalar(corr, w1, -1.0, 1e-30, ALU.add, ALU.max).then_inc(step, 1)
            dve.wait_ge(step, 4)
            nc.vector.reciprocal(corr, corr).then_inc(step, 1)
            dve.wait_ge(step, 5)
            nc.vector.tensor_tensor(corr, corr, u, ALU.mult).then_inc(step, 1)
            dve.wait_ge(log_done, 1)
            dve.wait_ge(step, 6)
            nc.vector.tensor_tensor(corr, corr, mag, ALU.mult).then_inc(step, 1)
            nc.vector.scalar_tensor_tensor(u, w1, 1.0, u, ALU.is_equal, ALU.mult).then_inc(log_done, 1)
            dve.wait_ge(step, 7)
            nc.vector.scalar_tensor_tensor(v, v, 0.0, corr, ALU.max, ALU.add).then_inc(step, 1)
            dve.wait_ge(step, 8)
            dve.wait_ge(log_done, 2)
            nc.vector.tensor_tensor(dt, v, u, ALU.add).then_inc(log_done, 1)
            dve.wait_ge(log_done, 3)
            dve.wait_ge(neg_a, 1)
            nc.vector.scalar_tensor_tensor(by_chunk(dt_a), by_chunk(dt), -1.0, per_head(neg[:, 0:H]),
                                           ALU.mult, ALU.mult).then_inc(step, 1)


def ssd_scan(k, raw, z, dt, dt_a, eacs, to_end, total, mixT):
    nc = k.nc
    H, G, R = SSD_HEADS, SSD_G, SSD_HEADS // SSD_G
    N = SSD_HEADS * SSD_P
    with ExitStack() as ctx:
        def sb(name, shape):
            return ctx.enter_context(k.sbuf(name, shape))

        xc = sb("xc", [P, XBC_T, P])
        small = sb("small", [P, 4, H])
        dta_c = sb("dta_c", [P, H])
        x_rows = sb("xs_rows", [P, H, SSD_P])
        b_rows = sb("b_rows", [P, G, P])
        x_dt = sb("x_dt", [P, H, SSD_P])
        x_end = sb("x_end", [P, H, SSD_P])
        steps = sb("steps", [P, H, P])
        weights = sb("weights", [P, H, P])
        cb = sb("cb", [P, G, P])
        state = sb("state", [P, H, SSD_P])
        y = steps[:, N // P:2 * N // P, :].rearrange("p a (b d) -> p (a b) d", d=SSD_P)
        zs = steps[:, 0:N // P, :].rearrange("p h n -> p (h n)")
        stat = sb("stat", [P, 4])
        banks = ctx.enter_context(k.psum("banks", [P, 8, S]))

        def two(b):
            return banks[:, b:b + 2, :].rearrange("p b n -> p (b n)")

        def heads(x):
            return x.rearrange("p (h d) -> p h d", h=H)

        turned_x, turned_b, cb_ps = two(0), banks[:, 2, :], banks[:, 3, :]
        segs = banks[:, 4:8, :].rearrange("p b n -> p (b n)")
        y_diag, new_state, y_off, turned_y = two(4), two(6), two(0), two(0)

        (block, staged, x_turned, x_copied, b_copied, xdt_done, steps_done, seg_done, cb_done, cb_masked, exp_done,
         weighted, xend_done, diag_done, off_done, new_done, y_step, state_step, z_done, sq_done, log_done, rstd_done,
         y_normed, y_turned, chunk_done, state_zero) = ctx.enter_context(stage(nc, (
             "staged x_turned x_copied b_copied xdt_done steps_done seg_done cb_done cb_masked exp_done weighted xend_done "
             "diag_done off_done new_done y_step state_step z_done sq_done log_done rstd_done y_normed y_turned chunk_done "
             "state_zero")))

        def per_head(col):
            return col.unsqueeze(2).to_broadcast([P, H, SSD_P])

        @block.gpsimd
        def _(pool):
            nc.gpsimd.memset(state[:, :, :], 0.0).then_inc(state_zero, 1)
            pool.sem_inc(chunk_done, 1)
            with pool.Fori(0, TC) as c:
                pool.wait_ge(chunk_done, c + 1)
                pool.wait_ge(state_step, c * 2 + 1)
                for i, src in enumerate((dt, eacs, to_end, total)):
                    nc.gpsimd.tensor_copy(small[:, i, :], src[:, bass.ds(c * H, H)]).then_inc(staged, 1)
                nc.gpsimd.tensor_copy(dta_c[:, :], dt_a[:, bass.ds(c * H, H)]).then_inc(staged, 1)
                pool.wait_ge(y_step, c * 4 + 2)
                pool.wait_ge(x_copied, c + 1)
                pool.wait_ge(xend_done, c + 1)
                pool.wait_ge(diag_done, c + 1)
                nc.gpsimd.tensor_tensor(x_dt[:, :, :], x_rows[:, :, :], per_head(k.ssd_d), ALU.mult).then_inc(y_step, 1)
                pool.wait_ge(y_step, c * 4 + 3)
                nc.gpsimd.tensor_tensor(y[:, :, :], y[:, :, :], x_dt[:, :, :], ALU.add).then_inc(y_step, 1)
                pool.wait_ge(y_step, c * 4 + 4)
                pool.wait_ge(z_done, c + 1)
                nc.gpsimd.tensor_tensor(y[:, :, :], y[:, :, :], heads(zs), ALU.mult).then_inc(sq_done, 1)

        @block.scalar
        def _(act):
            with act.Fori(0, TC) as c:
                act.wait_ge(chunk_done, c + 1)
                act.wait_ge(state_step, c * 2 + 1)
                nc.scalar.activation(xc[:, :, :], raw[:, :, bass.ds(c * P + (CONV - 1), P)], ACT.Copy).then_inc(staged, 1)
                act.wait_ge(x_turned, c * 2 + 1)
                nc.scalar.activation(x_rows[:, :, :], heads(turned_x), ACT.Copy).then_inc(x_copied, 1)
                act.wait_ge(x_turned, c * 2 + 2)
                nc.scalar.activation(b_rows[:, :, :], turned_b.rearrange("p (g n) -> p g n", g=G), ACT.Copy).then_inc(b_copied, 1)
                for g in range(G):
                    act.wait_ge(seg_done, c * G + g + 1)
                    nc.scalar.activation(weights[:, g * R:(g + 1) * R, :],
                                         segs[:, g * S:(g + 1) * S].rearrange("p (r n) -> p r n", r=R),
                                         ACT.Exp).then_inc(exp_done, 1)
                nc.scalar.activation(zs, z[:, bass.ds(c, 1), :].rearrange("p a n -> p (a n)"),
                                     ACT.Silu).then_inc(z_done, 1)
                act.wait_ge(sq_done, c * 2 + 1)
                nc.scalar.activation(zs, y[:, :, :].rearrange("p h d -> p (h d)"), ACT.Square,
                                     accum_out=stat[:, 0:1]).then_inc(sq_done, 1)
                act.wait_ge(sq_done, c * 2 + 2)
                inverse_root(k, act, stat[:, 2:3], stat[:, 1:2], stat[:, 0:1], 1.0 / N, log_done, c + 1).then_inc(rstd_done, 1)
                act.wait_ge(rstd_done, c + 1)
                nc.scalar.activation(y[:, :, :], y[:, :, :], ACT.Copy, scale=stat[:, 2:3]).then_inc(y_normed, 1)

        @block.tensor
        def _(pe):
            with pe.Fori(0, TC) as c:
                pe.wait_ge(staged, c * 6 + 6)
                for f in range(DT):
                    last = nc.tensor.transpose(turned_x[:, f * P:(f + 1) * P], xc[:, f, :], k.at["ident"])
                last.then_inc(x_turned, 1)
                for g in range(G):
                    last = nc.tensor.transpose(turned_b[:, g * P:(g + 1) * P], xc[:, DT + g, :], k.at["ident"])
                last.then_inc(x_turned, 1)
                for g in range(G):
                    last = nc.tensor.matmul(cb_ps[:, g * P:(g + 1) * P], xc[:, DT + g, :], xc[:, DT + G + g, :],
                                            start=True, stop=True)
                last.then_inc(cb_done, 1)
                pe.wait_ge(steps_done, c + 1)
                for h in range(H):
                    last = nc.tensor.matmul(segs[:, h * P:(h + 1) * P], steps[:, h, :], k.at["upto"], start=True, stop=True)
                    if h % R == R - 1:
                        last.then_inc(seg_done, 1)
                pe.wait_ge(x_copied, c + 1)
                pe.wait_ge(xdt_done, c + 1)
                pe.wait_ge(state_zero, 1)
                for g in range(G):
                    last = nc.tensor.matmul(y_off[:, g * R * SSD_P:(g + 1) * R * SSD_P], xc[:, DT + G + g, :],
                                            state[:, g * R:(g + 1) * R, :], start=True, stop=True)
                last.then_inc(off_done, 1)
                pe.wait_ge(xend_done, c + 1)
                pe.wait_ge(b_copied, c + 1)
                pe.wait_ge(exp_done, c * G + G)
                for g in range(G):
                    last = nc.tensor.matmul(new_state[:, g * R * SSD_P:(g + 1) * R * SSD_P], b_rows[:, g, :],
                                            x_end[:, g * R:(g + 1) * R, :], start=True, stop=True)
                last.then_inc(new_done, 1)
                pe.wait_ge(weighted, c * G + G)
                for h in range(H):
                    last = nc.tensor.matmul(y_diag[:, h * SSD_P:(h + 1) * SSD_P], weights[:, h, :], x_dt[:, h, :],
                                            start=True, stop=True)
                last.then_inc(diag_done, 1)
                pe.wait_ge(y_normed, c + 1)
                for f in range(DT):
                    last = nc.tensor.transpose(turned_y[:, f * P:(f + 1) * P],
                                               y[:, 2 * f:2 * f + 2, :].rearrange("p h d -> p (h d)"), k.at["ident"])
                last.then_inc(y_turned, 1)

        @block.vector
        def _(dve):
            dve.sem_inc(state_step, 1)
            with dve.Fori(0, TC) as c:
                dve.wait_ge(staged, c * 6 + 6)
                nc.vector.tensor_tensor(steps[:, :, :], k.at["after"].unsqueeze(1).to_broadcast([P, H, P]),
                                        dta_c[:, :].unsqueeze(2).to_broadcast([P, H, P]), ALU.mult).then_inc(steps_done, 1)
                dve.wait_ge(x_turned, c * 2 + 1)
                dve.wait_ge(x_copied, c + 1)
                nc.vector.tensor_tensor(x_dt[:, :, :], x_rows[:, :, :], per_head(small[:, 0, :]), ALU.mult).then_inc(xdt_done, 1)
                dve.wait_ge(xdt_done, c + 1)
                nc.vector.tensor_tensor(x_end[:, :, :], x_dt[:, :, :], per_head(small[:, 2, :]), ALU.mult).then_inc(xend_done, 1)
                dve.wait_ge(cb_done, c + 1)
                nc.vector.tensor_tensor(cb[:, :, :], cb_ps.rearrange("p (g n) -> p g n", g=G),
                                        k.at["upto"].unsqueeze(1).to_broadcast([P, G, P]), ALU.mult).then_inc(cb_masked, 1)
                dve.wait_ge(cb_masked, c + 1)
                for g in range(G):
                    dve.wait_ge(exp_done, c * G + g + 1)
                    w = weights[:, g * R:(g + 1) * R, :]
                    nc.vector.tensor_tensor(w, w, cb[:, g, :].unsqueeze(1).to_broadcast([P, R, P]), ALU.mult).then_inc(weighted, 1)
                dve.wait_ge(off_done, c + 1)
                nc.vector.tensor_tensor(y[:, :, :], heads(y_off), per_head(small[:, 1, :]), ALU.mult).then_inc(y_step, 1)
                nc.vector.tensor_tensor(state[:, :, :], state[:, :, :], per_head(small[:, 3, :]), ALU.mult).then_inc(state_step, 1)
                dve.wait_ge(new_done, c + 1)
                dve.wait_ge(state_step, c * 2 + 2)
                nc.vector.tensor_tensor(state[:, :, :], heads(new_state), state[:, :, :], ALU.add).then_inc(state_step, 1)
                dve.wait_ge(diag_done, c + 1)
                dve.wait_ge(y_step, c * 4 + 1)
                nc.vector.tensor_tensor(y[:, :, :], heads(y_diag), y[:, :, :], ALU.add).then_inc(y_step, 1)
                dve.wait_ge(y_turned, c + 1)
                nc.vector.tensor_tensor(mixT[:, 0:DT, bass.ds(c * P, P)], turned_y.rearrange("p (f n) -> p f n", f=DT),
                                        k.vec[:, P + 112:P + 120].unsqueeze(2).to_broadcast([P, DT, P]),
                                        ALU.mult).then_inc(chunk_done, 1)


def even_ssd(k, a, mixT):
    nc = k.nc
    w = a["e_w_in"][0]
    with (
        k.sbuf("z_rows", [P, TC, D]) as z,
        k.sbuf("xbc", [P, XBC_T, CONV - 1 + S]) as raw,
        k.sbuf("decays", [P, 5, TC * SSD_HEADS]) as decays,
    ):
        dt, dt_a, eacs, to_end, total = (decays[:, i, :] for i in range(5))
        project(k, 2, weight_tiles(w, E_Z),
                lambda e, t, j, ps: copy_out(nc, e, z[:, j, bass.ds(t * COLS, COLS)], ps), rows=True)
        project(k, 4, weight_tiles(w, E_XBC),
                lambda e, t, j, ps: copy_out(nc, e, raw[:, bass.ds(4 * t + j, 1), CONV - 1:].rearrange("p a n -> p (a n)"), ps))
        ssd_steps(k, a, dt, dt_a, eacs, to_end, total)
        conv_silu(k, raw, XBC_T, CONV, S, lambda t, j: k.vec[:, bass.ds(t + (64 + 16 * j), 1)],
                  lambda t: k.vec[:, bass.ds(t + (P + 96), 1)])
        ssd_scan(k, raw, z, dt, dt_a, eacs, to_end, total, mixT)



REL_BUCKETS, REL_MAX_DIST = 32, 128
HEADS = 8
BAND = 2 * P
LAM_INIT = 0.8 - 0.6 * float(np.exp(-0.3 * 0))


def bucket_of(dist):
    dist = np.maximum(dist, 0)
    exact = REL_BUCKETS // 2
    logd = np.log(np.maximum(dist, 1).astype(np.float32) / np.float32(exact))
    large = exact + (logd / np.float32(np.log(REL_MAX_DIST / exact)) * np.float32(REL_BUCKETS - exact)).astype(np.int32)
    return np.where(dist < exact, dist, np.minimum(large, REL_BUCKETS - 1))


def relative_bias(k, a):
    nc = k.nc
    n = 3 * P
    rows = nc.dram_tensor("bias_rows", [HEADS, n], F32)
    with (
        k.sbuf("bias_in", [REL_BUCKETS, HEADS + n]) as bias_in,
        k.sbuf("bias_sb", [HEADS, n]) as bias_sb,
        k.sbuf("flipped", [P, HEADS, BAND]) as flipped,
        k.psum("bias_ps", [P, 5, S]) as ps,
        stage(nc, "tab_in far_in list_done list_out list_kept band_in turned") as
        (block, tab_in, far_in, list_done, list_out, list_kept, band_in, turned),
    ):
        @block.sync
        def _(sp):
            sp.dma_start(bias_in[:, 0:HEADS], a["rel_bias"]).then_inc(tab_in, 16)
            sp.dma_start(bias_in[:, HEADS:], a["one_hot"]).then_inc(tab_in, 16)
            sp.dma_start(k.far, a["rel_bias"][REL_BUCKETS - 1].partition_broadcast(P)).then_inc(far_in, 16)
            sp.wait_ge(list_out, 1)
            sp.dma_start(rows.ap(), bias_sb[:, :]).then_inc(list_kept, 16)
            sp.wait_ge(list_kept, 16)
            sp.dma_start(flipped[:, :, :], bass.AP(rows, 0, [[1, P], [n, HEADS], [1, BAND]])).then_inc(band_in, 16)
            sp.wait_ge(far_in, 16)

        @block.tensor
        def _(pe):
            pe.wait_ge(tab_in, 32)
            nc.tensor.matmul(ps[0:HEADS, 4, 0:n], bias_in[:, 0:HEADS], bias_in[:, HEADS:], start=True, stop=True).then_inc(list_done, 1)
            pe.wait_ge(band_in, 16)
            for i in range(4):
                nc.tensor.matmul(ps[:, i, :], k.at["flip"], flipped[:, 2 * i:2 * i + 2, :], start=True, stop=True).then_inc(turned, 1)

        @block.vector
        def _(dve):
            dve.wait_ge(list_done, 1)
            nc.vector.tensor_copy(bias_sb[:, :], ps[0:HEADS, 4, 0:n]).then_inc(list_out, 1)
            for i in range(4):
                dve.wait_ge(turned, i + 1)
                nc.vector.tensor_copy(k.band[:, 2 * i:2 * i + 2, :], ps[:, i, :].rearrange("p (h n) -> p h n", h=2))


def lambda_stage(k, a, neg_lam, out_gain):
    nc = k.nc
    d = 64
    with (
        k.sbuf("lam", [P, 4, d]) as lam,
        k.sbuf("lam_tmp", [P, d]) as tmp,
        k.sbuf("dots", [P, 4]) as dots,
        stage(nc, "lam_in dot_done exp_done neg_done") as (block, lam_in, dot_done, exp_done, neg_done),
    ):
        @block.sync
        def _(sp):
            sp.dma_start(lam[:, :, :], a["e_lambda"][0].partition_broadcast(P)).then_inc(lam_in, 16)

        @block.vector
        def _(dve):
            dve.wait_ge(lam_in, 16)
            for i in range(2):
                if i:
                    dve.wait_ge(dot_done, i)
                nc.vector.tensor_tensor_reduce(tmp[:, :], lam[:, 2 * i, :], lam[:, 2 * i + 1, :], 1.0, 0.0, ALU.mult, ALU.add,
                                               dots[:, i:i + 1]).then_inc(dot_done, 1)
            nc.vector.tensor_scalar(out_gain, k.vec[:, 2 * P:2 * P + 1], 1.0 - LAM_INIT, None, ALU.mult)
            dve.wait_ge(exp_done, 1)
            nc.vector.scalar_tensor_tensor(neg_lam, dots[:, 2:3], -1.0, dots[:, 3:4], ALU.mult, ALU.add).then_inc(neg_done, 1)
            dve.wait_ge(neg_done, 1)
            nc.vector.tensor_scalar(neg_lam, neg_lam, -LAM_INIT, None, ALU.add)

        @block.scalar
        def _(act):
            act.wait_ge(dot_done, 2)
            nc.scalar.activation(dots[:, 2:4], dots[:, 0:2], ACT.Exp).then_inc(exp_done, 1)


def diff_attention(k, qT, kT, v_rows, neg_lam, out_gain, mixT, mix_at):
    nc = k.nc
    UNITS = 2 * TC
    with ExitStack() as ctx:
        def sb(name, shape):
            return ctx.enter_context(k.sbuf(name, shape))

        q_pair, k_pair, v_pair = sb("q_pair", [P, 2, S]), sb("k_pair", [P, 2, S]), sb("v_pair", [P, TC, 2 * P])
        bias = sb("bias", [P, 2, S])
        probs = sb("probs", [P, 2, 2, S])
        attn_t = sb("attn_t", [P, 2, S])
        neg_max, sums, weight = sb("neg_max", [P, 2, 2]), sb("sums", [P, 2, 2]), sb("weight", [P, 2, 2])
        sq, log_ms, rstd = sb("sq", [P, S]), sb("log_ms", [P, S]), sb("rstd", [P, S])
        banks = ctx.enter_context(k.psum("banks", [P, 8, S]))
        logits = banks[:, 0:4, :].rearrange("p (u m) n -> p u m n", m=2)
        turned, out_ps, stat = banks[:, 4:6, :], banks[:, 6, :], banks[:, 7, :]
        (block, admitted, staged, logit_done, shifted, exp_done, recip_done, lam_done, scaled, mixed, turn_done, turn_out, pv_done,
         sq_done, stat_done, log_done, rstd_done, head_done) = ctx.enter_context(stage(nc, (
             "admitted staged logit_done shifted exp_done recip_done lam_done scaled mixed turn_done turn_out pv_done sq_done "
             "stat_done log_done rstd_done head_done")))

        def unit(n):
            u, qb = divmod(n, TC)
            return u, qb, (qb + 1) * P, S - (qb + 1) * P

        @block.gpsimd
        def _(pool):
            with pool.Fori(0, HEADS // 2) as i:
                pool.wait_ge(logit_done, i * UNITS + 1)
                nc.gpsimd.tensor_copy(q_pair[:, :, :], qT[:, bass.ds(i * 2, 2), :]).then_inc(staged, 1)
                nc.gpsimd.tensor_copy(k_pair[:, :, :], kT[:, bass.ds(i * 2, 2), :]).then_inc(staged, 1)
                pool.wait_ge(shifted, i * (2 * UNITS) + 1)
                nc.gpsimd.tensor_copy(bias[:, :, BAND:S], k.band[:, bass.ds(i * 2, 2), :]).then_inc(staged, 1)
                nc.gpsimd.tensor_copy(bias[:, :, 0:BAND], k.far[:, bass.ds(i * 2, 2)].unsqueeze(2).to_broadcast([P, 2, BAND])
                                      ).then_inc(staged, 1)
                pool.wait_ge(staged, i * 6 + 3)
                nc.gpsimd.tensor_tensor(bias[:, :, S - P:S], bias[:, :, S - P:S],
                                        k.at["causal"].unsqueeze(1).to_broadcast([P, 2, P]), ALU.add).then_inc(staged, 1)
                pool.wait_ge(pv_done, i * UNITS + 1)
                nc.gpsimd.tensor_copy(v_pair[:, :, :], v_rows[:, :, bass.ds(i * (2 * P), 2 * P)]).then_inc(staged, 1)

        @block.tensor
        def _(pe):
            pe.sem_inc(stat_done, 1)
            pe.sem_inc(turn_done, 1)
            pe.sem_inc(pv_done, 1)
            pe.sem_inc(logit_done, 1)
            with pe.Fori(0, HEADS // 2) as i:
                def score(n):
                    u, qb, keys, _ = unit(n)
                    if n >= 2:
                        pe.wait_ge(shifted, i * (2 * UNITS) + 2 * n - 1)
                    for m in range(2):
                        at = slice(64 * m, 64 * m + 64)
                        last = nc.tensor.matmul(logits[:, n % 2, m, 0:keys], q_pair[at, u, qb * P:(qb + 1) * P],
                                                k_pair[at, u, 0:keys], start=True, stop=True)
                    last.then_inc(logit_done, 1)

                pe.wait_ge(staged, i * 6 + 2)
                pe.wait_ge(shifted, i * (2 * UNITS) + 1)
                score(0)
                for n in range(UNITS):
                    u, qb, keys, _ = unit(n)
                    if n + 1 < UNITS:
                        score(n + 1)
                    pe.wait_ge(mixed, i * UNITS + n + 1)
                    pe.wait_ge(turn_out, i * UNITS + max(n, 1))
                    for b in range(qb + 1):
                        last = nc.tensor.transpose(turned[:, n % 2, b * P:(b + 1) * P], probs[:, n % 2, 0, b * P:(b + 1) * P], k.at["ident"])
                    last.then_inc(turn_done, 1)
                    pe.wait_ge(turn_out, i * UNITS + n + 2)
                    pe.wait_ge(staged, i * 6 + 6)
                    if qb == 0:
                        pe.wait_ge(head_done, i * 2 + u + 1)
                    for b in range(qb + 1):
                        last = nc.tensor.matmul(out_ps[:, qb * P:(qb + 1) * P], v_pair[:, b, u * P:(u + 1) * P],
                                                attn_t[:, n % 2, b * P:(b + 1) * P], start=(b == 0), stop=(b == qb))
                    last.then_inc(pv_done, 1)
                    if qb == TC - 1:
                        pe.wait_ge(sq_done, i * 2 + u + 1)
                        nc.tensor.matmul(stat, k.at["ones"], sq[:, :], start=True, stop=True).then_inc(stat_done, 1)

        @block.vector
        def _(dve):
            dve.sem_inc(head_done, 1)
            dve.sem_inc(shifted, 1)
            with dve.Fori(0, HEADS // 2) as i:
                def shift(n):
                    u, qb, keys, at = unit(n)
                    dve.wait_ge(logit_done, i * UNITS + n + 2)
                    dve.wait_ge(staged, i * 6 + 5)
                    if n >= 2:
                        dve.wait_ge(turn_done, i * UNITS + n)
                    else:
                        dve.wait_ge(turn_done, i * UNITS + 1)
                    dve.sem_inc(admitted, 1)
                    for m in range(2):
                        nc.vector.tensor_tensor_reduce(probs[:, n % 2, m, 0:keys], logits[:, n % 2, m, 0:keys], bias[:, u, at:S],
                                                       -1.0, 3e38, ALU.add, ALU.min, neg_max[:, n % 2, m:m + 1]).then_inc(shifted, 1)

                shift(0)
                for n in range(UNITS):
                    u, qb, keys, _ = unit(n)
                    if n + 1 < UNITS:
                        shift(n + 1)
                    p = n % 2
                    dve.wait_ge(exp_done, i * (2 * UNITS) + 2 * n + 2)
                    nc.vector.reciprocal(weight[:, p, :], sums[:, p, :]).then_inc(recip_done, 1)
                    dve.wait_ge(recip_done, i * UNITS + n + 1)
                    nc.vector.tensor_scalar(weight[:, p, 1:2], weight[:, p, 1:2], neg_lam, None, ALU.mult).then_inc(lam_done, 1)
                    dve.wait_ge(lam_done, i * UNITS + n + 1)
                    nc.vector.tensor_scalar(probs[:, p, 1, 0:keys], probs[:, p, 1, 0:keys], weight[:, p, 1:2], None,
                                            ALU.mult).then_inc(scaled, 1)
                    dve.wait_ge(scaled, i * UNITS + n + 1)
                    nc.vector.scalar_tensor_tensor(probs[:, p, 0, 0:keys], probs[:, p, 0, 0:keys], weight[:, p, 0:1],
                                                   probs[:, p, 1, 0:keys], ALU.mult, ALU.add).then_inc(mixed, 1)
                    if qb == TC - 1:
                        dve.wait_ge(rstd_done, i * 2 + u + 1)
                        nc.vector.scalar_tensor_tensor(mixT[:, bass.ds(i * 2 + (mix_at + u), 1), :].rearrange("p a n -> p (a n)"), out_ps,
                                                       out_gain, rstd[:, :], ALU.mult, ALU.mult).then_inc(head_done, 1)

        @block.scalar
        def _(act):
            act.sem_inc(turn_out, 1)
            with act.Fori(0, HEADS // 2) as i:
                def exps(n):
                    u, qb, keys, _ = unit(n)
                    p = n % 2
                    for m in range(2):
                        act.wait_ge(shifted, i * (2 * UNITS) + 2 * n + m + 2)
                        nc.scalar.activation(probs[:, p, m, 0:keys], probs[:, p, m, 0:keys], ACT.Exp, scale=-1.0,
                                             bias=neg_max[:, p, m:m + 1], accum_out=sums[:, p, m:m + 1]).then_inc(exp_done, 1)

                exps(0)
                for n in range(UNITS):
                    u, qb, keys, _ = unit(n)
                    if n + 1 < UNITS:
                        exps(n + 1)
                    act.wait_ge(turn_done, i * UNITS + n + 2)
                    act.wait_ge(pv_done, i * UNITS + max(n, 1))
                    nc.scalar.activation(attn_t[:, n % 2, 0:keys], turned[:, n % 2, 0:keys], ACT.Copy).then_inc(turn_out, 1)
                    if qb == TC - 1:
                        act.wait_ge(pv_done, i * UNITS + n + 2)
                        act.wait_ge(stat_done, i * 2 + u + 1)
                        nc.scalar.activation(sq[:, :], out_ps, ACT.Square).then_inc(sq_done, 1)
                        act.wait_ge(stat_done, i * 2 + u + 2)
                        act.wait_ge(head_done, i * 2 + u + 1)
                        inverse_root(k, act, rstd[:, :], log_ms[:, :], stat, 1.0 / P, log_done, i * 2 + u + 1).then_inc(rstd_done, 1)


def even_diff(k, a, mixT):
    nc = k.nc
    w = a["e_w_in"][0]
    with (
        k.sbuf("qT", [P, HEADS, S]) as qT, k.sbuf("kT", [P, HEADS, S]) as kT, k.sbuf("v_rows", [P, TC, D]) as v_rows,
        k.sbuf("lam_cols", [P, 2]) as lam_cols,
    ):
        neg_lam, out_gain = lam_cols[:, 0:1], lam_cols[:, 1:2]

        def to(dst, scale=None):
            return lambda e, t, j, ps: copy_out(nc, e, dst[:, bass.ds(4 * t + j, 1), :].rearrange("p a n -> p (a n)"), ps, scale)

        project(k, 2, weight_tiles(w, E_Q), to(qT, 64 ** -0.5))
        project(k, 2, weight_tiles(w, E_K), to(kT))
        project(k, 2, weight_tiles(w, E_V), lambda e, t, j, ps: copy_out(nc, e, v_rows[:, j, bass.ds(t * COLS, COLS)], ps), rows=True)
        lambda_stage(k, a, neg_lam, out_gain)
        diff_attention(k, qT, kT, v_rows, neg_lam, out_gain, mixT, DT)



def pairs(eng, n_tiles, body):
    if n_tiles >= 4:
        with eng.Fori(0, n_tiles // 2) as i:
            for u in range(2):
                body(i, u)
    elif n_tiles >= 2:
        for u in range(2):
            body(0, u)
    if n_tiles % 2:
        body(n_tiles // 2, 0)


def down_project(k, w, moving, per, post=None, gate=None):
    nc = k.nc
    n_tiles = w.shape[0] // (P * per)
    v = w.rearrange("(t c p) n -> t p c n", c=per, p=P)
    slot = k.ring[:, :, :, :].rearrange("p u c n -> p u (c n)")[:, :, 0:per * D].rearrange("p u (c n) -> p u c n", c=per)
    with (
        k.sbuf("y0", [P, S]) as y0, k.sbuf("log_ms", [P, S]) as log_ms, k.sbuf("rstd", [P, S]) as rstd,
        k.psum("y", [P, DT, S]) as y,
        stage(nc, "zeroed landed0 landed1 slot_read bank_done y0_kept squared stat_done log_done rstd_done scaled gate_done") as
        (block, zeroed, landed0, landed1, slot_read, bank_done, y0_kept, squared, stat_done, log_done, rstd_done, scaled, gate_done),
    ):
        landed = (landed0, landed1)
        done = 8 * (n_tiles - 1)

        @block.sync
        def _(sp):
            def load(i, u):
                sp.wait_ge(slot_read, 2 * i + u + 1)
                sp.dma_start(slot[:, u, :, :], v[bass.ds(2 * i + u, 1)].rearrange("a p c n -> p (a c) n")).then_inc(landed[u], 16)
            pairs(sp, n_tiles, load)

        @block.tensor
        def _(pe):
            pe.sem_inc(slot_read, 2)
            pe.wait_ge(zeroed, 1)

            def multiply(i, u):
                pe.wait_ge(landed[u], i * 16 + 16)
                for f in range(DT):
                    for c in range(per):
                        last = nc.tensor.matmul(y[:, f, :], slot[:, u, c, f * P:(f + 1) * P],
                                                moving[:, bass.ds((2 * i + u) * per + c, 1), :].rearrange("p a n -> p (a n)"),
                                                start=False, stop=False, skip_group_check=True)
                    if f < DT - 1:
                        last.then_inc(bank_done, 1)
                last.then_inc(bank_done, 1)
                pe.wait_ge(bank_done, (2 * i + u) * 8 + 8)
                pe.sem_inc(slot_read, 1)
            pairs(pe, n_tiles, multiply)
            if post is not None:
                pe.wait_ge(y0_kept, 1)
                for f in range(DT):
                    pe.wait_ge(squared, f + 1)
                    last = nc.tensor.matmul(y[:, 0, :], k.at["ones"], k.hT[:, f, :], start=(f == 0), stop=(f == DT - 1))
                last.then_inc(stat_done, 1)

        @block.vector
        def _(dve):
            nc.vector.memset(y[:, :, :], 0.0).then_inc(zeroed, 1)
            if post is None:
                for f in range(DT):
                    dve.wait_ge(bank_done, done + f + 1)
                    nc.vector.tensor_tensor(k.xT[:, f, :], y[:, f, :], k.xT[:, f, :], ALU.add)
            else:
                dve.wait_ge(bank_done, done + 1)
                nc.vector.tensor_copy(y0[:, :], y[:, 0, :]).then_inc(y0_kept, 1)
                dve.wait_ge(rstd_done, 1)
                dve.wait_ge(y0_kept, 1)
                for f in range(DT):
                    nc.vector.scalar_tensor_tensor(k.hT[:, f, :], y0[:, :] if f == 0 else y[:, f, :], post(f), rstd[:, :],
                                                   ALU.mult, ALU.mult).then_inc(scaled, 1)

        @block.scalar
        def _(act):
            if post is not None:
                for f in range(DT):
                    act.wait_ge(bank_done, done + f + 1)
                    if f == 0:
                        act.wait_ge(y0_kept, 1)
                    nc.scalar.activation(k.hT[:, f, :], y0[:, :] if f == 0 else y[:, f, :], ACT.Square).then_inc(squared, 1)
                act.wait_ge(stat_done, 1)
                inverse_root(k, act, rstd[:, :], log_ms[:, :], y[:, 0, :], 1.0 / D, log_done).then_inc(rstd_done, 1)

        @block.gpsimd
        def _(pool):
            if post is not None:
                for f in range(DT):
                    pool.wait_ge(scaled, f + 1)
                    if gate is not None:
                        nc.gpsimd.tensor_tensor(k.hT[:, f, :], k.hT[:, f, :], gate[:, f, :], ALU.mult).then_inc(gate_done, 1)
                        pool.wait_ge(gate_done, f + 1)
                    nc.gpsimd.tensor_tensor(k.xT[:, f, :], k.xT[:, f, :], k.hT[:, f, :], ALU.add)


def squared_relu_mlp(k, a, layer, sub):
    nc = k.nc
    F = 4 * D // P
    with k.sbuf("hidden", [P, F, S]) as hidden:
        def tile(t, j):
            return hidden[:, bass.ds(4 * t + j, 1), :].rearrange("p a n -> p (a n)")

        def relu(e, t, j, ps):
            if e == "act":
                return nc.scalar.activation(tile(t, j), ps, ACT.Relu)
            return nc.vector.tensor_scalar(tile(t, j), ps, 0.0, None, ALU.max)

        project(k, 8, weight_tiles(a["mlp_w1"][layer], 0), relu,
                after=lambda t, j: nc.gpsimd.tensor_tensor(tile(t, j), tile(t, j), tile(t, j), ALU.mult))
        down_project(k, a["mlp_w2"][layer], hidden, 4, post=lambda f: k.post_gain[:, sub, f:f + 1])


def pre_norm(k, sub):
    norm_into(k, lambda f: k.pre_gain[:, sub, f:f + 1], lambda f: k.mod[:, sub * 24 + f:sub * 24 + f + 1])



def project_items(k, w, loads):
    nc = k.nc
    v = w.rearrange("(k p) n -> p k n", p=P)
    items = [(n, *item) for n, (_, its) in enumerate(loads) for item in its]
    with (
        k.psum("item_out", [P, 8, S]) as out,
        stage(nc, "landed0 landed1 item_done act_freed dve_freed") as
        (block, landed0, landed1, item_done, act_freed, dve_freed),
    ):
        landed = (landed0, landed1)
        last_item = [max(m for m, item in enumerate(items) if item[0] == n) for n in range(len(loads))]

        def arrived(n):
            return 16 * sum(len(ranges) for ranges, _ in loads[n % 2:n + 1:2])

        def view(m):
            _, kind, _, width, _ = items[m]
            if kind == "rows":
                return out[:, m % 8, 0:TC * width].rearrange("p (c n) -> p c n", c=TC)
            return out[:, m % 8, :]

        def empty(eng, name, freed, parity):
            for m in range(parity, len(items), 2):
                eng.wait_ge(item_done, m + 1)
                items[m][4](name, view(m)).then_inc(freed, 1)

        @block.sync
        def _(sp):
            for n, (ranges, _) in enumerate(loads):
                if n >= 2:
                    sp.wait_ge(item_done, last_item[n - 2] + 1)
                at = 0
                for col, width in ranges:
                    sp.dma_start(k.ring[:, n % 2, :, at:at + width], v[:, :, bass.ds(col, width)]).then_inc(landed[n % 2], 16)
                    at += width

        @block.tensor
        def _(pe):
            for m, (n, kind, at, width, _) in enumerate(items):
                pe.wait_ge(landed[n % 2], arrived(n))
                if m >= 8:
                    pe.wait_ge((act_freed, dve_freed)[m % 2], (m - 8) // 2 + 1)
                weights = k.ring[:, n % 2, :, at:at + width]
                if kind == "rows":
                    for c in range(TC):
                        for f in range(DT):
                            last = nc.tensor.matmul(view(m)[:, c, :], k.hT[:, f, c * P:(c + 1) * P], weights[:, f, :],
                                                    start=(f == 0), stop=(f == DT - 1))
                elif kind == "feat":
                    for f in range(DT):
                        last = nc.tensor.matmul(view(m), weights[:, f, :], k.hT[:, f, :], start=(f == 0), stop=(f == DT - 1))
                else:
                    for half in (0, 64):
                        for f in range(DT):
                            last = nc.tensor.matmul(view(m)[half:half + 64, :], weights[:, f, :], k.hT[:, f, :],
                                                    start=(f == 0), stop=(f == DT - 1))
                last.then_inc(item_done, 1)

        @block.scalar
        def _(act):
            empty(act, "act", act_freed, 0)

        @block.vector
        def _(dve):
            empty(dve, "dve", dve_freed, 1)


def rotate(k, tiles, swap, cos, sin):
    nc = k.nc
    n = len(tiles)
    with (
        k.sbuf("crossed", [P, 2, S]) as crossed,
        k.psum("swapped", [P, 2, S]) as swapped,
        stage(nc, "swap_done cross_done cos_done added") as (block, swap_done, cross_done, cos_done, added),
    ):
        @block.tensor
        def _(pe):
            for j in range(n):
                if j >= 2:
                    pe.wait_ge(cross_done, j - 1)
                nc.tensor.matmul(swapped[:, j % 2, :], swap, tiles[j], start=True, stop=True).then_inc(swap_done, 1)

        @block.gpsimd
        def _(pool):
            for j in range(n):
                pool.wait_ge(swap_done, j + 1)
                nc.gpsimd.tensor_tensor(tiles[j], tiles[j], cos, ALU.mult).then_inc(cos_done, 1)

        @block.vector
        def _(dve):
            for j in range(n):
                dve.wait_ge(swap_done, j + 1)
                if j >= 2:
                    dve.wait_ge(added, j - 1)
                nc.vector.tensor_tensor(crossed[:, j % 2, :], swapped[:, j % 2, :], sin, ALU.mult).then_inc(cross_done, 1)
                dve.wait_ge(cross_done, j + 1)
                dve.wait_ge(cos_done, j + 1)
                nc.vector.tensor_tensor(tiles[j], tiles[j], crossed[:, j % 2, :], ALU.add).then_inc(added, 1)



RET_H, RET_QK, RET_V = 4, 128, 256
O_RQ, O_RV, O_RG, O_SQ, O_SK = 0, 1024, 2048, 3072, 3584


def retention_constants():
    half = RET_QK // 2
    inv = np.float32(10000.0) ** (-np.arange(half, dtype=np.float32) / half)
    ang = np.arange(S, dtype=np.float32)[None, :] * inv[:, None]
    log_gamma = np.log(1.0 - 2.0 ** (-5.0 - np.arange(RET_H)))
    i = np.arange(P)
    rel = i[None, :] - i[:, None]
    decay = [np.where(rel >= 0, np.exp(np.maximum(rel, 0) * g), 0.0) for g in log_gamma]
    xi = [np.broadcast_to(np.exp((i + 1.0) * g), (P, P)) for g in log_gamma]
    zeta = [np.exp((P - 1 - i) * g)[:, None] for g in log_gamma]
    table = np.concatenate([np.concatenate([np.cos(ang)] * 2), np.concatenate([-np.sin(ang), np.sin(ang)])]
                           + [np.concatenate(x, axis=1) for x in (decay, xi, zeta)], axis=1)
    return table.astype(np.float32), [float(np.exp(P * g)) for g in log_gamma]


def retention(k, qkT, v_rows, table, gammas, outT):
    nc = k.nc
    H = RET_H
    decay = table[:, 2 * S:2 * S + H * P].rearrange("p (h n) -> p h n", h=H)
    xi = table[:, 2 * S + H * P:2 * S + 2 * H * P].rearrange("p (h n) -> p h n", h=H)
    zeta = table[:, 2 * S + 2 * H * P:2 * S + 2 * H * P + H]
    with ExitStack() as ctx:
        def sb(name, shape):
            return ctx.enter_context(k.sbuf(name, shape))

        qk_c = sb("qk_c", [P, 2 * H, P])
        v_c = sb("v_c", [P, H, RET_V])
        q_xi = sb("q_xi", [P, H, P])
        scores = sb("scores", [P, H, P])
        k_zeta = sb("k_zeta", [P, H, P])
        state = sb("ret_state", [P, H, RET_V])
        banks = ctx.enter_context(k.psum("banks", [P, 6, S]))
        score_ps, turned = banks[:, 0, :], banks[:, 1, :]
        out_ps = banks[:, 2:4, :].rearrange("p b (t n) -> p (b t) n", n=P)
        new_ps = banks[:, 4:6, :].rearrange("p b (t n) -> p (b t) n", n=RET_V)
        (block, staged, xi_done, score_done, scored, turn_done, kz_done, out_done, new_done, state_done, chunk_out,
         zeroed) = ctx.enter_context(stage(nc, (
             "staged xi_done score_done scored turn_done kz_done out_done new_done state_done chunk_out zeroed")))

        @block.gpsimd
        def _(pool):
            nc.gpsimd.memset(state[:, :, :], 0.0).then_inc(zeroed, 1)
            with pool.Fori(0, TC) as c:
                pool.wait_ge(chunk_out, c + 1)
                pool.wait_ge(state_done, c * H + 1)
                nc.gpsimd.tensor_copy(v_c[:, :, :], v_rows[:, bass.ds(c, 1), :].rearrange("p a (h n) -> p (a h) n", h=H)).then_inc(staged, 1)
                pool.wait_ge(staged, c * 2 + 2)
                nc.gpsimd.tensor_tensor(q_xi[:, :, :], qk_c[:, 0:H, :], xi, ALU.mult).then_inc(xi_done, 1)

        @block.scalar
        def _(act):
            act.sem_inc(chunk_out, 1)
            with act.Fori(0, TC) as c:
                act.wait_ge(out_done, c + 1)
                act.wait_ge(new_done, c + 1)
                nc.scalar.activation(qk_c[:, :, :], qkT[:, :, bass.ds(c * P, P)], ACT.Copy).then_inc(staged, 1)
                act.wait_ge(out_done, c + 2)
                nc.scalar.activation(outT[:, :, bass.ds(c * P, P)], out_ps, ACT.Copy).then_inc(chunk_out, 1)

        @block.tensor
        def _(pe):
            pe.sem_inc(new_done, 1)
            pe.sem_inc(out_done, 1)
            pe.wait_ge(zeroed, 1)
            with pe.Fori(0, TC) as c:
                pe.wait_ge(staged, c * 2 + 2)
                for h in range(H):
                    last = nc.tensor.matmul(score_ps[:, h * P:(h + 1) * P], qk_c[:, H + h, :], qk_c[:, h, :], start=True, stop=True)
                last.then_inc(score_done, 1)
                for h in range(H):
                    last = nc.tensor.transpose(turned[:, h * P:(h + 1) * P], qk_c[:, H + h, :], k.at["ident"])
                last.then_inc(turn_done, 1)
                pe.wait_ge(scored, c + 1)
                pe.wait_ge(xi_done, c + 1)
                pe.wait_ge(chunk_out, c + 1)
                for h in range(H):
                    for e in range(2):
                        to = out_ps[:, 2 * h + e, :]
                        nc.tensor.matmul(to, v_c[:, h, e * P:(e + 1) * P], scores[:, h, :], start=True, stop=False)
                        last = nc.tensor.matmul(to, state[:, h, e * P:(e + 1) * P], q_xi[:, h, :], start=False, stop=True)
                last.then_inc(out_done, 1)
                pe.wait_ge(kz_done, c + 1)
                for h in range(H):
                    last = nc.tensor.matmul(new_ps[:, h, :], k_zeta[:, h, :], v_c[:, h, :], start=True, stop=True)
                last.then_inc(new_done, 1)

        @block.vector
        def _(dve):
            dve.sem_inc(state_done, 1)
            dve.wait_ge(zeroed, 1)
            with dve.Fori(0, TC) as c:
                dve.wait_ge(score_done, c + 1)
                nc.vector.tensor_tensor(scores[:, :, :], score_ps.rearrange("p (h n) -> p h n", h=H), decay, ALU.mult).then_inc(scored, 1)
                dve.wait_ge(turn_done, c + 1)
                nc.vector.tensor_tensor(k_zeta[:, :, :], turned.rearrange("p (h n) -> p h n", h=H),
                                        zeta.unsqueeze(2).to_broadcast([P, H, P]), ALU.mult).then_inc(kz_done, 1)
                dve.wait_ge(new_done, c + 2)
                dve.wait_ge(out_done, c + 2)
                for h in range(H):
                    nc.vector.scalar_tensor_tensor(state[:, h, :], state[:, h, :], gammas[h], new_ps[:, h, :],
                                                   ALU.mult, ALU.add).then_inc(state_done, 1)


def norm_gate_heads(k, x, gate, n_heads, per, mixT):
    nc = k.nc
    n = n_heads * per
    sq = k.hT
    with (
        k.sbuf("log_ms", [P, 2, S]) as log_ms, k.sbuf("rstd", [P, 2, S]) as rstd,
        k.psum("stat", [P, n_heads, S]) as stat,
        stage(nc, "squared gated stat_done log_done rstd_done normed") as (block, squared, gated, stat_done, log_done, rstd_done, normed),
    ):
        @block.scalar
        def _(act):
            for f in range(n):
                nc.scalar.activation(sq[:, f, :], x[:, f, :], ACT.Square).then_inc(squared, 1)
            for f in range(n):
                nc.scalar.activation(gate[:, f, :], gate[:, f, :], ACT.Silu).then_inc(gated, 1)
            for h in range(n_heads):
                act.wait_ge(stat_done, h + 1)
                if h >= 2:
                    act.wait_ge(normed, (h - 1) * per)
                inverse_root(k, act, rstd[:, h % 2, :], log_ms[:, h % 2, :], stat[:, h, :], 1.0 / (per * P), log_done, h + 1
                             ).then_inc(rstd_done, 1)

        @block.tensor
        def _(pe):
            for h in range(n_heads):
                for e in range(per):
                    pe.wait_ge(squared, h * per + e + 1)
                    last = nc.tensor.matmul(stat[:, h, :], k.at["ones"], sq[:, h * per + e, :], start=(e == 0), stop=(e == per - 1))
                last.then_inc(stat_done, 1)

        @block.vector
        def _(dve):
            for f in range(n):
                dve.wait_ge(rstd_done, f // per + 1)
                nc.vector.tensor_tensor(mixT[:, f, :], x[:, f, :], rstd[:, (f // per) % 2, :], ALU.mult).then_inc(normed, 1)

        @block.gpsimd
        def _(pool):
            for f in range(n):
                pool.wait_ge(normed, f + 1)
                pool.wait_ge(gated, f + 1)
                nc.gpsimd.tensor_tensor(mixT[:, f, :], mixT[:, f, :], gate[:, f, :], ALU.mult)



def sliding_window(k, a, qT, k_dup, v_rows, mixT, mix_at):
    nc = k.nc
    UNITS = 2 * TC
    with ExitStack() as ctx:
        def sb(name, shape):
            return ctx.enter_context(k.sbuf(name, shape))

        q_pair, k_pair, v_pair = sb("q_pair", [P, S]), sb("k_pair", [P, S]), sb("v_pair", [P, TC, 64])
        bias = sb("bias", [P, 2, BAND])
        sinks, neg_sinks, neg_sink = sb("sinks", [P, HEADS]), sb("neg_sinks", [P, HEADS]), sb("neg_sink", [P, 2])
        probs, probs_t = sb("probs", [P, 2, BAND]), sb("probs_t", [P, 2, BAND])
        neg_max, sums, sink_exp = sb("neg_max", [P, 2]), sb("sums", [P, 2]), sb("sink_exp", [P, 2])
        banks = ctx.enter_context(k.psum("banks", [P, 6, S]))
        logits, turned, out_ps = banks[:, 0:2, 0:BAND], banks[:, 2:4, 0:BAND], banks[:, 4:6, :]
        (block, admitted, sinks_in, sinks_turned, staged, logit_done, shifted, max_done, exp_done, sink_done, sum_done, recip_done, scaled, turn_done,
         turn_out, pv_done, pair_out) = ctx.enter_context(stage(nc, (
             "admitted sinks_in sinks_turned staged logit_done shifted max_done exp_done sink_done sum_done recip_done scaled turn_done turn_out "
             "pv_done pair_out")))

        def unit(n):
            u, qb = divmod(n, TC)
            first = max(qb - 1, 0)
            return u, qb, first, (qb + 1 - first) * P, 0 if qb else P

        @block.sync
        def _(sp):
            sp.dma_start(sinks[:, :], a["o_sinks"][0].partition_broadcast(P)).then_inc(sinks_in, 16)

        @block.gpsimd
        def _(pool):
            pool.wait_ge(sinks_in, 16)
            nc.gpsimd.tensor_scalar(neg_sinks[:, :], sinks[:, :], -1.0, None, ALU.mult).then_inc(sinks_turned, 1)
            pool.wait_ge(sinks_turned, 1)
            with pool.Fori(0, 2) as g:
                for w in range(2):
                    i = g * 2 + w
                    pool.wait_ge(pv_done, g * (2 * UNITS) + w * UNITS + 1)
                    nc.gpsimd.tensor_copy(q_pair[:, :], qT[:, bass.ds(i, 1), :].rearrange("p a n -> p (a n)")).then_inc(staged, 1)
                    nc.gpsimd.tensor_copy(k_pair[:, :], k_dup[:, bass.ds(g, 1), :].rearrange("p a n -> p (a n)")).then_inc(staged, 1)
                    nc.gpsimd.tensor_tensor(bias[:, :, :], k.band[:, bass.ds(i * 2, 2), :],
                                            k.at["window"].unsqueeze(1).to_broadcast([P, 2, BAND]), ALU.add).then_inc(staged, 1)
                    nc.gpsimd.tensor_copy(neg_sink[:, :], neg_sinks[:, bass.ds(i * 2, 2)]).then_inc(staged, 1)
                    nc.gpsimd.tensor_copy(v_pair[:, :, :], v_rows[:, :, bass.ds(g * 64, 64)]).then_inc(staged, 1)

        @block.tensor
        def _(pe):
            pe.sem_inc(turn_done, 1)
            pe.sem_inc(pv_done, 1)
            with pe.Fori(0, HEADS // 2) as i:
                def score(n):
                    u, qb, first, keys, _ = unit(n)
                    if n >= 2:
                        pe.wait_ge(shifted, i * UNITS + n)
                    nc.tensor.matmul(logits[:, n % 2, 0:keys], q_pair[64 * u:64 * u + 64, qb * P:(qb + 1) * P],
                                     k_pair[64 * u:64 * u + 64, first * P:first * P + keys], start=True, stop=True).then_inc(logit_done, 1)

                pe.wait_ge(staged, i * 5 + 5)
                pe.wait_ge(shifted, i * UNITS + 1)
                score(0)
                for n in range(UNITS):
                    u, qb, first, keys, _ = unit(n)
                    if n + 1 < UNITS:
                        score(n + 1)
                    pe.wait_ge(scaled, i * UNITS + n + 2)
                    pe.wait_ge(turn_out, i * UNITS + max(n, 1))
                    for b in range(keys // P):
                        last = nc.tensor.transpose(turned[:, n % 2, b * P:(b + 1) * P], probs[:, n % 2, b * P:(b + 1) * P], k.at["ident"])
                    last.then_inc(turn_done, 1)
                    pe.wait_ge(turn_out, i * UNITS + n + 2)
                    pe.wait_ge(pair_out, i * 2 + u + 1)
                    for b in range(keys // P):
                        last = nc.tensor.matmul(out_ps[64 * u:64 * u + 64, u, qb * P:(qb + 1) * P], v_pair[:, first + b, :],
                                                probs_t[:, n % 2, b * P:(b + 1) * P], start=(b == 0), stop=(b == keys // P - 1))
                    last.then_inc(pv_done, 1)

        @block.vector
        def _(dve):
            dve.sem_inc(scaled, 1)
            dve.sem_inc(sum_done, 1)
            dve.sem_inc(pair_out, 1)
            dve.sem_inc(shifted, 1)
            with dve.Fori(0, HEADS // 2) as i:
                def shift(n):
                    u, qb, first, keys, at = unit(n)
                    p = n % 2
                    dve.wait_ge(logit_done, i * UNITS + n + 1)
                    dve.wait_ge(staged, i * 5 + 5)
                    dve.wait_ge(turn_done, i * UNITS + max(n, 1))
                    dve.wait_ge(sum_done, i * UNITS + max(n, 1))
                    dve.sem_inc(admitted, 1)
                    nc.vector.tensor_tensor_reduce(probs[:, p, 0:keys], logits[:, p, 0:keys], bias[:, u, at:at + keys],
                                                   -1.0, 3e38, ALU.add, ALU.min, neg_max[:, p:p + 1]).then_inc(shifted, 1)
                    dve.wait_ge(shifted, i * UNITS + n + 2)
                    nc.vector.tensor_tensor(neg_max[:, p:p + 1], neg_max[:, p:p + 1], neg_sink[:, u:u + 1], ALU.min).then_inc(max_done, 1)

                shift(0)
                for n in range(UNITS):
                    u, qb, first, keys, _ = unit(n)
                    p = n % 2
                    if n + 1 < UNITS:
                        shift(n + 1)
                    dve.wait_ge(sink_done, i * UNITS + n + 1)
                    nc.vector.tensor_tensor(sums[:, p:p + 1], sums[:, p:p + 1], sink_exp[:, p:p + 1], ALU.add).then_inc(sum_done, 1)
                    dve.wait_ge(sum_done, i * UNITS + n + 2)
                    nc.vector.reciprocal(sums[:, p:p + 1], sums[:, p:p + 1]).then_inc(recip_done, 1)
                    dve.wait_ge(recip_done, i * UNITS + n + 1)
                    nc.vector.tensor_scalar(probs[:, p, 0:keys], probs[:, p, 0:keys], sums[:, p:p + 1], None, ALU.mult).then_inc(scaled, 1)
                    if qb == TC - 1:
                        half = slice(64 * u, 64 * u + 64)
                        dve.wait_ge(pv_done, i * UNITS + n + 2)
                        nc.vector.tensor_copy(mixT[half, bass.ds(i + mix_at, 1), :].rearrange("p a n -> p (a n)"),
                                              out_ps[half, u, :]).then_inc(pair_out, 1)

        @block.scalar
        def _(act):
            act.sem_inc(turn_out, 1)
            with act.Fori(0, HEADS // 2) as i:
                def exps(n):
                    u, qb, first, keys, _ = unit(n)
                    p = n % 2
                    act.wait_ge(max_done, i * UNITS + n + 1)
                    act.wait_ge(scaled, i * UNITS + max(n, 1))
                    nc.scalar.activation(probs[:, p, 0:keys], probs[:, p, 0:keys], ACT.Exp, scale=-1.0,
                                         bias=neg_max[:, p:p + 1], accum_out=sums[:, p:p + 1]).then_inc(exp_done, 1)
                    act.wait_ge(exp_done, i * UNITS + n + 1)
                    nc.scalar.activation(sink_exp[:, p:p + 1], neg_sink[:, u:u + 1], ACT.Exp, scale=-1.0,
                                         bias=neg_max[:, p:p + 1]).then_inc(sink_done, 1)

                exps(0)
                for n in range(UNITS):
                    u, qb, first, keys, _ = unit(n)
                    if n + 1 < UNITS:
                        exps(n + 1)
                    act.wait_ge(turn_done, i * UNITS + n + 2)
                    act.wait_ge(pv_done, i * UNITS + max(n, 1))
                    nc.scalar.activation(probs_t[:, n % 2, 0:keys], turned[:, n % 2, 0:keys], ACT.Copy).then_inc(turn_out, 1)


def tile_of(buf, index):
    return buf[:, bass.ds(index, 1), :].rearrange("p a n -> p (a n)")


def odd_mixer(k, a, mixT):
    nc = k.nc
    w = a["o_w_in"][0]

    def feat(dst, scale=None, at=0):
        return lambda e, t, j, ps: copy_out(nc, e, tile_of(dst, 4 * t + (j + at)), ps, scale)

    with k.sbuf("sqT", [P, 4, S]) as sqT, k.sbuf("sk_dup", [P, 2, S]) as sk_dup, k.sbuf("sv_rows", [P, TC, P]) as sv_rows:
        with (
            k.sbuf("rqkT", [P, 2 * RET_H, S]) as qkT, k.sbuf("rv_rows", [P, TC, D]) as v_rows, k.sbuf("rgT", [P, DT, S]) as gate,
            k.sbuf("ret_table", [P, a["ret_table"].shape[1]]) as table,
        ):
            with stage(nc, "table_in") as (block, table_in):
                @block.sync
                def _(sp):
                    sp.dma_start(table[:, :], a["ret_table"]).then_inc(table_in, 16)
                    sp.wait_ge(table_in, 16)
            project(k, 1, weight_tiles(w, O_RQ), feat(qkT))
            project(k, 1, weight_tiles(w, O_RQ + COLS), feat(qkT, RET_QK ** -0.5, RET_H))
            project(k, 2, weight_tiles(w, O_RV), lambda e, t, j, ps: copy_out(nc, e, v_rows[:, j, bass.ds(t * COLS, COLS)], ps), rows=True)
            project(k, 2, weight_tiles(w, O_RG), feat(gate))
            project(k, 1, weight_tiles(w, O_SQ), feat(sqT, 64 ** -0.5))
            project_items(k, w, [([(O_SK, BAND)], [
                ("dup", 0, 64, lambda e, ps: copy_out(nc, e, sk_dup[:, 0, :], ps)),
                ("dup", 64, 64, lambda e, ps: copy_out(nc, e, sk_dup[:, 1, :], ps)),
                ("rows", P, P, lambda e, ps: copy_out(nc, e, sv_rows[:, :, :], ps))])])
            rotate(k, [qkT[:, j, :] for j in range(2 * RET_H)], k.at["swap_128"], table[:, 0:S], table[:, S:2 * S])
            with k.sbuf("retT", [P, DT, S]) as retT:
                retention(k, qkT, v_rows, table, retention_constants()[1], retT)
                norm_gate_heads(k, retT, gate, RET_H, 2, mixT)
        sliding_window(k, a, sqT, sk_dup, sv_rows, mixT, DT)



N_GDN, N_NSA, N_SB, HD = 6, 6, 4, 64
GDN_T, NSA_T, SB_T = N_GDN // 2, N_NSA // 2, N_SB // 2
FF_T = 22
CMP_LEN, CMP_STRIDE = 32, 16
N_CMP = (S - CMP_LEN) // CMP_STRIDE + 1
V_MIX, V_GCONV, V_FFN, V_PLE, V_PLEN, V_PEK, V_PEV, V_GN, V_NN, V_SN, V_FIN, V_FCONV = 0, 8, 44, 52, 60, 68, 84, 100, 101, 102, 103, 111
W_GDN, W_AB, W_NQ, W_KC, W_KW, W_GATE, W_SQ, W_SV = 0, 1536, 1548, 1932, 2444, 2700, 2718, 3230


def layer_of(ap, l):
    names = " ".join(f"d{i}" for i in range(len(ap.shape) - 1))
    first, *rest = names.split()
    return ap[bass.ds(l, 1)].rearrange(f"a {names} -> (a {first}) {' '.join(rest)}".rstrip())


def layer_vectors(k, a, l):
    nc = k.nc
    rows = [
        (0, V_MIX, 8, 0, P, layer_of(a["ln_mix_2"], l).rearrange("(f p) -> f p", p=P)),
        (0, V_GCONV, 36, 0, P, layer_of(a["gdn_conv_2"], l).rearrange("t (f p) -> (t f) p", p=P)),
        (0, V_FFN, 8, 0, P, layer_of(a["ln_ffn_2"], l).rearrange("(f p) -> f p", p=P)),
        (0, V_PLE, 8, 0, P, layer_of(a["ln_ple_2"], l).rearrange("(f p) -> f p", p=P)),
        (0, V_PLEN, 8, 0, P, layer_of(a["ple_norm_2"], l).rearrange("(f p) -> f p", p=P)),
        (0, V_PEK, 16, 0, P, layer_of(a["nsa_pe_k_2"], l).rearrange("(m j) d -> m (j d)", j=2)),
        (0, V_PEV, 16, 0, P, layer_of(a["nsa_pe_v_2"], l).rearrange("(m j) d -> m (j d)", j=2)),
        (0, V_FIN, 8, 0, P, a["ln_final_2"].rearrange("(f p) -> f p", p=P)),
        (1, 0, 88, 0, P, layer_of(a["ffn_conv_2"], l)[0:2].rearrange("t (f p) -> (t f) p", p=P)),
        (2, 0, 44, 0, P, layer_of(a["ffn_conv_2"], l)[2:3].rearrange("t (f p) -> (t f) p", p=P)),
    ]
    for at, name in ((V_GN, "gdn_norm_2"), (V_NN, "nsa_norm_2"), (V_SN, "sb_norm_2")):
        for half in (0, HD):
            rows.append((0, at, 1, half, HD, a[name][bass.ds(l, 1)]))
    used = (V_FCONV, 88, 44)
    with (
        k.sbuf("vec_rows", [P, 3, P]) as vec_rows, k.psum("turned", [P, 3, S]) as turned,
        stage(nc, "rows_in vec_turned") as (block, rows_in, vec_turned),
    ):
        @block.sync
        def _(sp):
            for g, at, n, col, width, src in rows:
                sp.dma_start(vec_rows[at:at + n, g, col:col + width], src).then_inc(rows_in, 16)

        @block.tensor
        def _(pe):
            pe.wait_ge(rows_in, 16 * len(rows))
            for g in range(3):
                n = used[g]
                nc.tensor.transpose(turned[:, g, 0:n], vec_rows[0:n, g, :], k.at["ident"][0:n, 0:n]).then_inc(vec_turned, 1)

        @block.vector
        def _(dve):
            at = 0
            for g in range(3):
                dve.wait_ge(vec_turned, g + 1)
                nc.vector.tensor_copy(k.vec2[:, at:at + used[g]], turned[:, g, 0:used[g]])
                at += used[g]


def rotary_tables(k, a):
    nc = k.nc
    turn = 2 * np.pi
    c1 = 6.28125
    c2 = float(np.float32(np.round((turn - c1) * 2 ** 21) / 2 ** 21))
    c3 = float(np.float32(turn - c1 - c2))
    magic = 1.5 * 2.0 ** 23
    edge = 3.1415925
    with (
        k.sbuf("pos_int", [P, S], I32) as pos_int, k.sbuf("ang", [P, S]) as ang, k.sbuf("turns", [P, S]) as turns,
        k.sbuf("over", [P, S]) as over,
        stage(nc, "pos_in step sin_done") as (block, pos_in, step, sin_done),
    ):
        @block.sync
        def _(sp):
            sp.dma_start(pos_int[:, :], a["positions_2"][0].partition_broadcast(P)).then_inc(pos_in, 16)

        @block.vector
        def _(dve):
            dve.wait_ge(pos_in, 16)
            nc.vector.tensor_copy(ang[:, :], pos_int[:, :]).then_inc(step, 1)
            dve.wait_ge(step, 1)
            nc.vector.tensor_scalar(ang[:, :], ang[:, :], k.at["inv_freq"], None, ALU.mult).then_inc(step, 1)
            dve.wait_ge(step, 2)
            nc.vector.tensor_scalar(turns[:, :], ang[:, :], 1.0 / turn, magic, ALU.mult, ALU.add).then_inc(step, 1)
            dve.wait_ge(step, 3)
            nc.vector.tensor_scalar(turns[:, :], turns[:, :], -magic, None, ALU.add).then_inc(step, 1)
            for n, c in enumerate((c1, c2, c3)):
                dve.wait_ge(step, 4 + n)
                nc.vector.scalar_tensor_tensor(ang[:, :], turns[:, :], -c, ang[:, :], ALU.mult, ALU.add).then_inc(step, 1)
            dve.wait_ge(step, 7)
            nc.vector.tensor_scalar(turns[:, :], ang[:, :], np.pi / 2, None, ALU.add).then_inc(step, 1)
            dve.wait_ge(step, 8)
            nc.vector.tensor_scalar(over[:, :], turns[:, :], edge, -turn, ALU.is_gt, ALU.mult).then_inc(step, 1)
            dve.wait_ge(step, 9)
            nc.vector.tensor_tensor(turns[:, :], turns[:, :], over[:, :], ALU.add).then_inc(step, 1)
            dve.wait_ge(step, 10)
            nc.vector.tensor_scalar(turns[:, :], turns[:, :], edge, -edge, ALU.min, ALU.max).then_inc(step, 1)
            nc.vector.tensor_scalar(ang[:, :], ang[:, :], edge, -edge, ALU.min, ALU.max).then_inc(step, 1)
            dve.wait_ge(sin_done, 1)
            nc.vector.tensor_scalar(k.sin, k.sin, k.at["half_sign"], None, ALU.mult)

        @block.scalar
        def _(act):
            act.wait_ge(step, 12)
            nc.scalar.activation(k.sin, ang[:, :], ACT.Sin).then_inc(sin_done, 1)
            nc.scalar.activation(k.cos, turns[:, :], ACT.Sin)


def swap_halves(k, tiles):
    nc = k.nc
    with (
        k.psum("swapped", [P, len(tiles), S]) as swapped,
        stage(nc, "swap_done") as (block, swap_done),
    ):
        @block.tensor
        def _(pe):
            for j, (orig, _) in enumerate(tiles):
                nc.tensor.matmul(swapped[:, j, :], k.at["swap_128"], orig, start=True, stop=True).then_inc(swap_done, 1)

        @block.vector
        def _(dve):
            for j in range(0, len(tiles), 2):
                dve.wait_ge(swap_done, j + 1)
                nc.vector.tensor_copy(tiles[j][1], swapped[:, j, :])

        @block.scalar
        def _(act):
            for j in range(1, len(tiles), 2):
                act.wait_ge(swap_done, j + 1)
                nc.scalar.activation(tiles[j][1], swapped[:, j, :], ACT.Copy)



def gdn_steps(k, a, l, ab, g, beta, beta_eg, to_end, gates):
    nc = k.nc
    H = N_GDN
    n = TC * H
    with (
        k.sbuf("rows", [P, 2, H]) as rows, k.sbuf("tmp", [P, 4, n]) as tmp, k.psum("sums", [P, 2, S]) as sums,
        stage(nc, "rows_in step exp_done act_done sum_done") as (block, rows_in, step, exp_done, act_done, sum_done),
    ):
        v, mag, eg, rate = (tmp[:, i, :] for i in range(4))

        def by_pair(x):
            return x.rearrange("p (c h) -> p c h", h=H)

        def per_head(row):
            return row.unsqueeze(1).to_broadcast([P, TC, H])

        @block.sync
        def _(sp):
            sp.dma_start(rows[:, 0, :], layer_of(a["gdn_dt_bias_2"], l).partition_broadcast(P)).then_inc(rows_in, 16)
            sp.dma_start(rows[:, 1, :], layer_of(a["gdn_a_log_2"], l).partition_broadcast(P)).then_inc(rows_in, 16)

        @block.scalar
        def _(act):
            nc.scalar.activation(by_pair(beta), ab[:, :, H:2 * H], ACT.Sigmoid).then_inc(act_done, 1)
            nc.scalar.activation(gates, ab[:, :, 2 * H:2 * H + 3 * N_NSA], ACT.Sigmoid)
            act.wait_ge(rows_in, 32)
            nc.scalar.activation(rate[:, 0:H], rows[:, 1, :], ACT.Exp).then_inc(act_done, 1)
            act.wait_ge(step, 2)
            nc.scalar.activation(mag, mag, ACT.Exp, scale=-1.0).then_inc(exp_done, 1)
            act.wait_ge(exp_done, 1)
            nc.scalar.activation(mag, mag, ACT.Ln, bias=1.0).then_inc(exp_done, 1)
            act.wait_ge(sum_done, 1)
            nc.scalar.activation(eg, sums[:, 0, 0:n], ACT.Exp).then_inc(exp_done, 1)
            nc.scalar.activation(to_end, sums[:, 1, 0:n], ACT.Exp)

        @block.vector
        def _(dve):
            dve.wait_ge(rows_in, 32)
            nc.vector.tensor_tensor(by_pair(v), ab[:, :, 0:H], per_head(rows[:, 0, :]), ALU.add).then_inc(step, 1)
            dve.wait_ge(step, 1)
            nc.vector.scalar_tensor_tensor(mag, v, -1.0, v, ALU.mult, ALU.max).then_inc(step, 1)
            dve.wait_ge(exp_done, 2)
            nc.vector.scalar_tensor_tensor(v, v, 0.0, mag, ALU.max, ALU.add).then_inc(step, 1)
            dve.wait_ge(step, 3)
            dve.wait_ge(act_done, 2)
            nc.vector.scalar_tensor_tensor(by_pair(g), by_pair(v), -1.0, per_head(rate[:, 0:H]), ALU.mult, ALU.mult).then_inc(step, 1)
            dve.wait_ge(exp_done, 3)
            nc.vector.tensor_tensor(beta_eg, eg, beta, ALU.mult)

        @block.tensor
        def _(pe):
            pe.wait_ge(step, 4)
            nc.tensor.matmul(sums[:, 0, 0:n], k.at["upto_64"], g, start=True, stop=True)
            nc.tensor.matmul(sums[:, 1, 0:n], k.at["after_64"], g, start=True, stop=True).then_inc(sum_done, 1)


def norm_heads(k, tiles, total_scale):
    nc = k.nc
    n = len(tiles)
    squares = k.ring[:, 0, :, :]
    gated = [j for j in range(n) if tiles[j][2] is not None]
    with (
        k.sbuf("log_ms", [P, 2, S]) as log_ms, k.sbuf("rstd", [P, 2, S]) as rstd, k.psum("stat", [P, n, S]) as stat,
        stage(nc, "squared gate_done stat_done log_done rstd_done normed") as
        (block, squared, gate_done, stat_done, log_done, rstd_done, normed),
    ):
        @block.scalar
        def _(act):
            for j, (x, _, _) in enumerate(tiles):
                nc.scalar.activation(squares[:, j, :], x, ACT.Square).then_inc(squared, 1)
            for j in gated:
                nc.scalar.activation(tiles[j][2], tiles[j][2], ACT.Silu).then_inc(gate_done, 1)
            for j in range(n):
                act.wait_ge(stat_done, j + 1)
                if j >= 2:
                    act.wait_ge(normed, j - 1)
                inverse_root(k, act, rstd[:, j % 2, :], log_ms[:, j % 2, :], stat[:, j, :], total_scale, log_done, j + 1
                             ).then_inc(rstd_done, 1)

        @block.tensor
        def _(pe):
            for j in range(n):
                pe.wait_ge(squared, j + 1)
                nc.tensor.matmul(stat[:, j, :], k.at["ones_64"], squares[:, j, :], start=True, stop=True).then_inc(stat_done, 1)

        @block.vector
        def _(dve):
            for j, (x, gain, _) in enumerate(tiles):
                dve.wait_ge(rstd_done, j + 1)
                nc.vector.scalar_tensor_tensor(x, x, gain, rstd[:, j % 2, :], ALU.mult, ALU.mult).then_inc(normed, 1)

        @block.gpsimd
        def _(pool):
            for m, j in enumerate(gated):
                pool.wait_ge(normed, j + 1)
                pool.wait_ge(gate_done, m + 1)
                nc.gpsimd.tensor_tensor(tiles[j][0], tiles[j][0], tiles[j][2], ALU.mult)


def delta_rule(k, qkv, g, beta, beta_eg, to_end, mixT):
    nc = k.nc
    H, T = N_GDN, GDN_T
    LEVELS = 5
    with ExitStack() as ctx:
        def sb(name, shape):
            return ctx.enter_context(k.sbuf(name, shape))

        x_c = sb("x_c", [P, 3 * T, P])
        small = sb("small", [P, 4, H])
        g_wide = sb("g_wide", [P, H, HD])
        v_beta, k_beta, k_end = sb("v_beta", [P, H, HD]), sb("k_beta", [P, H, HD]), sb("k_end", [P, H, HD])
        steps = sb("steps", [P, H, P])
        decay, decay_t = sb("decay", [P, H, P]), sb("decay_t", [P, H, P])
        run = sb("run", [P, T, P])
        low, low_t = sb("low", [P, H, P]), sb("low_t", [P, H, P])
        part = sb("part", [P, H, P])
        attn_t = sb("attn_t", [P, H, P])
        inv, inv_t, y = sb("inv", [P, H, P]), sb("inv_t", [P, H, P]), sb("lt_inv", [P, H, P])
        u, w_t, q_run = sb("u", [P, H, HD]), sb("w_t", [P, T, P]), sb("q_run", [P, T, P])
        v_new = sb("v_new", [P, H, HD])
        state = sb("gdn_state", [P, T, HD])
        banks = ctx.enter_context(k.psum("banks", [P, 8, S]))

        def wide(b, n=P):
            return banks[:, b:b + 2, 0:T * n].rearrange("p b (t n) -> p t b n", t=T)

        def paired(x):
            return x.rearrange("p (t b) n -> p t b n", b=2)

        turned_k, turned_v = (banks[:, b, 0:H * HD].rearrange("p (h n) -> p h n", h=H) for b in (0, 1))
        kk_ps, low_t_ps, y_ps = wide(0), wide(0), wide(0)
        decay_ps, kq_ps, ty_ps = wide(2), wide(2), wide(2)
        decay_t_ps, yt_ps = wide(4), wide(4)
        run_ps = banks[:, 6, 0:T * P].rearrange("p (t n) -> p t n", t=T)
        w_ps = run_ps
        u_ps = banks[:, 7, 0:H * HD].rearrange("p (h n) -> p h n", h=H)
        new_ps = wide(0, HD)
        inter_ps, intra_ps = (banks[:, b, 0:T * P].rearrange("p (t n) -> p t n", t=T) for b in (3, 4))
        grow_ps = banks[:, 2, 0:T * HD].rearrange("p (t n) -> p t n", t=T)

        (block, admitted, zeroed, staged, turn_done, rows_done, steps_done, decay_done, run_done, exp_done, kk_done, kq_done, masked,
         low_done, attn_done, low_turned, low_t_out, part_done, y_done, y_out, ty_done, yt_done, inv_done, inv_t_done, qrun_done,
         uw_done, uw_out, vn_done, vn_out, grow_done, state_done, inter_done, inter_out, intra_done, pass_out, first_done) = ctx.enter_context(stage(nc, (
             "admitted zeroed staged turn_done rows_done steps_done decay_done run_done exp_done kk_done kq_done masked low_done attn_done "
             "low_turned low_t_out part_done y_done y_out ty_done yt_done inv_done inv_t_done qrun_done uw_done uw_out vn_done "
             "vn_out grow_done state_done inter_done inter_out intra_done pass_out first_done")))

        def per_head(col, width):
            return col.unsqueeze(2).to_broadcast([P, H, width])

        def each_head(m):
            return m.unsqueeze(1).to_broadcast([P, H, P])

        @block.gpsimd
        def _(pool):
            nc.gpsimd.memset(state[:, :, :], 0.0).then_inc(zeroed, 1)
            with pool.Fori(0, TC) as c:
                pool.wait_ge(pass_out, c + 1)
                for i, src in enumerate((g, beta, beta_eg, to_end)):
                    nc.gpsimd.tensor_copy(small[:, i, :], src[:, bass.ds(c * H, H)]).then_inc(staged, 1)
                nc.gpsimd.tensor_copy(g_wide[:, :, :], per_head(g[:, bass.ds(c * H, H)], HD)).then_inc(staged, 1)
                pool.wait_ge(exp_done, c * 3 + 1)
                nc.gpsimd.tensor_tensor(decay[:, :, :], decay[:, :, :], each_head(k.at["after_64"]), ALU.mult).then_inc(masked, 1)
                pool.wait_ge(masked, c * 3 + 1)
                pool.wait_ge(staged, c * 6 + 6)
                nc.gpsimd.tensor_tensor(decay[:, :, :], decay[:, :, :], per_head(small[:, 1, :], P), ALU.mult).then_inc(masked, 1)
                pool.wait_ge(exp_done, c * 3 + 2)
                nc.gpsimd.tensor_tensor(decay_t[:, :, :], decay_t[:, :, :], each_head(k.at["upto_64"]), ALU.mult).then_inc(masked, 1)
                pool.wait_ge(exp_done, c * 3 + 3)
                nc.gpsimd.tensor_tensor(q_run[:, :, :], x_c[:, 0:T, :], run[:, :, :], ALU.mult).then_inc(qrun_done, 1)
                pool.wait_ge(low_t_out, c + 1)
                for n in range(LEVELS):
                    pool.wait_ge(y_done, c * LEVELS + n + 1)
                    nc.gpsimd.tensor_tensor(part[:, :, :], low_t[:, :, :], each_head(k.level_masks[n + 1]), ALU.mult).then_inc(part_done, 1)

        @block.scalar
        def _(act):
            with act.Fori(0, TC) as c:
                act.wait_ge(pass_out, c + 1)
                nc.scalar.activation(x_c[:, :, :], qkv[:, :, bass.ds(c * P + (CONV - 1), P)], ACT.Copy).then_inc(staged, 1)
                act.wait_ge(decay_done, c * 2 + 1)
                nc.scalar.activation(paired(decay[:, :, :]), decay_ps, ACT.Exp).then_inc(exp_done, 1)
                act.wait_ge(decay_done, c * 2 + 2)
                nc.scalar.activation(paired(decay_t[:, :, :]), decay_t_ps, ACT.Exp).then_inc(exp_done, 1)
                act.wait_ge(run_done, c + 1)
                nc.scalar.activation(run[:, :, :], run_ps, ACT.Exp).then_inc(exp_done, 1)
                act.wait_ge(low_turned, c + 1)
                nc.scalar.activation(paired(low_t[:, :, :]), low_t_ps, ACT.Copy).then_inc(low_t_out, 1)
                for n in range(LEVELS):
                    act.wait_ge(y_done, c * LEVELS + n + 2)
                    nc.scalar.activation(paired(y[:, :, :]), y_ps, ACT.Copy).then_inc(y_out, 1)
                act.wait_ge(uw_done, c + 1)
                nc.scalar.activation(u[:, :, :], u_ps, ACT.Copy).then_inc(uw_out, 1)
                nc.scalar.activation(w_t[:, :, :], w_ps, ACT.Copy).then_inc(uw_out, 1)
                act.wait_ge(inter_done, c * 2 + 2)
                nc.scalar.activation(mixT[:, 0:T, bass.ds(c * P, P)], inter_ps, ACT.Copy).then_inc(inter_out, 1)

        @block.tensor
        def _(pe):
            pe.sem_inc(y_done, 1)
            pe.wait_ge(zeroed, 1)
            with pe.Fori(0, TC) as c:
                pe.wait_ge(staged, c * 6 + 6)
                for t in range(T):
                    nc.tensor.transpose(banks[:, 0, t * P:(t + 1) * P], x_c[:, T + t, :], k.at["ident"])
                for t in range(T):
                    last = nc.tensor.transpose(banks[:, 1, t * P:(t + 1) * P], x_c[:, 2 * T + t, :], k.at["ident"])
                last.then_inc(turn_done, 1)
                pe.wait_ge(steps_done, c + 1)
                pe.wait_ge(state_done, c * 2 * T + 1)
                for b in range(2):
                    last = nc.tensor.matmul(decay_ps[:, :, b, :], k.at["upto_64"], paired(steps[:, :, :])[:, :, b, :], start=True, stop=True)
                last.then_inc(decay_done, 1)
                for h in range(H):
                    last = nc.tensor.matmul(decay_t_ps[:, h // 2, h % 2, :], steps[:, h, :], k.at["upto_64"], start=True, stop=True)
                last.then_inc(decay_done, 1)
                for t in range(T):
                    last = nc.tensor.matmul(run_ps[:, t, :], g_wide[:, 2 * t:2 * t + 2, :].rearrange("p h n -> p (h n)"), k.at["upto_64"], start=True, stop=True)
                last.then_inc(run_done, 1)
                pe.wait_ge(rows_done, c * 3 + 3)
                for h in range(H):
                    at = slice(HD * (h % 2), HD * (h % 2) + HD)
                    last = nc.tensor.matmul(kk_ps[:, h // 2, h % 2, :], x_c[at, T + h // 2, :], x_c[at, T + h // 2, :], start=True, stop=True)
                last.then_inc(kk_done, 1)
                pe.wait_ge(exp_done, c * 3 + 1)
                for h in range(H):
                    at = slice(HD * (h % 2), HD * (h % 2) + HD)
                    last = nc.tensor.matmul(kq_ps[:, h // 2, h % 2, :], x_c[at, T + h // 2, :], x_c[at, h // 2, :], start=True, stop=True)
                last.then_inc(kq_done, 1)
                pe.wait_ge(low_done, c + 1)
                for h in range(H):
                    last = nc.tensor.transpose(low_t_ps[:, h // 2, h % 2, :], low[:, h, :], k.at["ident"])
                last.then_inc(low_turned, 1)
                pe.wait_ge(attn_done, c + 1)
                pe.wait_ge(exp_done, c * 3 + 3)
                for n in range(LEVELS):
                    pe.wait_ge(part_done, c * LEVELS + n + 1)
                    pe.wait_ge(inv_done, c * LEVELS + n + 1)
                    for h in range(H):
                        last = nc.tensor.matmul(y_ps[:, h // 2, h % 2, :], part[:, h, :], inv[:, h, :], start=True, stop=True)
                    last.then_inc(y_done, 1)
                    pe.wait_ge(inv_t_done, c * (LEVELS + 1) + n + 1)
                    pe.wait_ge(y_out, c * LEVELS + n + 1)
                    if n < LEVELS - 1:
                        for h in range(H):
                            last = nc.tensor.matmul(ty_ps[:, h // 2, h % 2, :], inv_t[:, h, :], y[:, h, :], start=True, stop=True)
                        last.then_inc(ty_done, 1)
                    for h in range(H):
                        last = nc.tensor.matmul(yt_ps[:, h // 2, h % 2, :], y[:, h, :], inv_t[:, h, :], start=True, stop=True)
                    last.then_inc(yt_done, 1)
                pe.wait_ge(inv_t_done, c * (LEVELS + 1) + LEVELS + 1)
                for h in range(H):
                    at = slice(HD * (h % 2), HD * (h % 2) + HD)
                    nc.tensor.matmul(u_ps[:, h, :], inv_t[:, h, :], v_beta[:, h, :], start=True, stop=True)
                    last = nc.tensor.matmul(w_ps[at, h // 2, :], k_beta[:, h, :], inv_t[:, h, :], start=True, stop=True)
                last.then_inc(uw_done, 1)
                pe.wait_ge(uw_out, c * 2 + 2)
                pe.wait_ge(qrun_done, c + 1)
                for i in range(2):
                    rows = slice(HD * i, HD * i + HD)
                    pe.wait_ge(state_done, c * (2 * T) + i * T + 1)
                    pe.sem_inc(admitted, 1)
                    for h in range(H):
                        at = slice(HD * (h % 2), HD * (h % 2) + HD)
                        last = nc.tensor.matmul(new_ps[rows, h // 2, h % 2, :], w_t[at, h // 2, rows], state[at, h // 2, :], start=True, stop=True)
                    last.then_inc(vn_done, 1)
                    for h in range(H):
                        at = slice(HD * (h % 2), HD * (h % 2) + HD)
                        last = nc.tensor.matmul(inter_ps[at, h // 2, rows], state[at, h // 2, :], q_run[at, h // 2, rows], start=True, stop=True)
                    last.then_inc(inter_done, 1)
                    pe.wait_ge(vn_out, c * 2 + i + 1)
                    pe.sem_inc(admitted, 1)
                    for h in range(H):
                        at = slice(HD * (h % 2), HD * (h % 2) + HD)
                        last = nc.tensor.matmul(grow_ps[at, h // 2, :], k_end[rows, h, :], v_new[rows, h, :], start=True, stop=True)
                    last.then_inc(grow_done, 1)
                for h in range(H):
                    at = slice(HD * (h % 2), HD * (h % 2) + HD)
                    last = nc.tensor.matmul(intra_ps[at, h // 2, :], v_new[:, h, :], attn_t[:, h, :], start=True, stop=True)
                last.then_inc(intra_done, 1)

        @block.vector
        def _(dve):
            dve.sem_inc(state_done, 1)
            dve.sem_inc(pass_out, 1)
            dve.wait_ge(zeroed, 1)
            with dve.Fori(0, TC) as c:
                dve.wait_ge(staged, c * 6 + 6)
                nc.vector.tensor_tensor(steps[:, :, :], each_head(k.at["after_64"]), per_head(small[:, 0, :], P), ALU.mult).then_inc(steps_done, 1)
                dve.wait_ge(turn_done, c + 1)
                nc.vector.tensor_tensor(v_beta[:, :, :], turned_v, per_head(small[:, 1, :], HD), ALU.mult).then_inc(rows_done, 1)
                nc.vector.tensor_tensor(k_beta[:, :, :], turned_k, per_head(small[:, 2, :], HD), ALU.mult).then_inc(rows_done, 1)
                nc.vector.tensor_tensor(k_end[:, :, :], turned_k, per_head(small[:, 3, :], HD), ALU.mult).then_inc(rows_done, 1)
                dve.wait_ge(kk_done, c + 1)
                dve.wait_ge(masked, c * 3 + 2)
                nc.vector.tensor_tensor(paired(low[:, :, :]), kk_ps, paired(decay[:, :, :]), ALU.mult).then_inc(low_done, 1)
                dve.wait_ge(kq_done, c + 1)
                dve.wait_ge(masked, c * 3 + 3)
                nc.vector.tensor_tensor(paired(attn_t[:, :, :]), kq_ps, paired(decay_t[:, :, :]), ALU.mult).then_inc(attn_done, 1)
                dve.wait_ge(low_done, c + 1)
                nc.vector.tensor_tensor(inv[:, :, :], low[:, :, :], each_head(k.at["first_mask"]), ALU.mult).then_inc(first_done, 1)
                dve.wait_ge(low_t_out, c + 1)
                nc.vector.tensor_tensor(inv_t[:, :, :], low_t[:, :, :], each_head(k.level_masks[0]), ALU.mult).then_inc(first_done, 1)
                dve.wait_ge(first_done, c * 2 + 2)
                nc.vector.tensor_tensor(inv[:, :, :], each_head(k.at["ident"]), inv[:, :, :], ALU.subtract).then_inc(inv_done, 1)
                nc.vector.tensor_tensor(inv_t[:, :, :], each_head(k.at["ident"]), inv_t[:, :, :], ALU.subtract).then_inc(inv_t_done, 1)
                for n in range(LEVELS):
                    if n < LEVELS - 1:
                        dve.wait_ge(ty_done, c * (LEVELS - 1) + n + 1)
                        dve.wait_ge(inv_done, c * LEVELS + n + 1)
                        nc.vector.tensor_tensor(paired(inv[:, :, :]), paired(inv[:, :, :]), ty_ps, ALU.subtract).then_inc(inv_done, 1)
                    dve.wait_ge(yt_done, c * LEVELS + n + 1)
                    dve.wait_ge(inv_t_done, c * (LEVELS + 1) + n + 1)
                    nc.vector.tensor_tensor(paired(inv_t[:, :, :]), paired(inv_t[:, :, :]), yt_ps, ALU.subtract).then_inc(inv_t_done, 1)
                dve.wait_ge(uw_out, c * 2 + 2)
                for i in range(2):
                    rows = slice(HD * i, HD * i + HD)
                    dve.wait_ge(vn_done, c * 2 + i + 1)
                    nc.vector.tensor_tensor(paired(v_new[rows, :, :]), paired(u[rows, :, :]), new_ps[rows, :, :, :], ALU.subtract).then_inc(vn_out, 1)
                    dve.wait_ge(grow_done, c * 2 + i + 1)
                    dve.wait_ge(inter_done, c * 2 + i + 1)
                    dve.wait_ge(state_done, c * (2 * T) + i * T + 1)
                    for t in range(T):
                        nc.vector.scalar_tensor_tensor(state[:, t, :], state[:, t, :], run[:, t, HD * i + HD - 1:HD * i + HD],
                                                       grow_ps[:, t, :], ALU.mult, ALU.add).then_inc(state_done, 1)
                dve.wait_ge(inter_out, c + 1)
                dve.wait_ge(intra_done, c + 1)
                nc.vector.tensor_tensor(mixT[:, 0:T, bass.ds(c * P, P)], mixT[:, 0:T, bass.ds(c * P, P)], intra_ps, ALU.add).then_inc(pass_out, 1)



def compress_keys(k, a, l, k2, v2, kc_dup, vc_rows):
    nc = k.nc
    M = CMP_LEN // 2
    G = 2
    n = G * N_CMP
    HID = P
    with ExitStack() as ctx:
        def sb(name, shape):
            return ctx.enter_context(k.sbuf(name, shape))

        w1 = sb("cmp_w1", [P, 2, M, HID])
        w2 = sb("cmp_w2", [P, 3, HD])
        pairs_of = sb("token_pairs", [P, 2, G, S])
        hid = sb("hid", [P, 2, n])
        pe_cols = sb("pe_cols", [P, 2])
        ps = ctx.enter_context(k.psum("cmp_ps", [P, 5, S]))
        (block, w_in, shifted, hid_done, pe_out, act_done, out_done) = ctx.enter_context(stage(
            nc, "w_in shifted hid_done pe_out act_done out_done"))

        @block.sync
        def _(sp):
            for i, name in enumerate(("k", "v")):
                rows = layer_of(a[f"nsa_cmp_{name}_w1_2"], l).rearrange("(m p) c -> p m c", p=P)
                for half in (slice(0, M // 2), slice(M // 2, M)):
                    sp.dma_start(w1[:, i, half, :], rows[:, half, :]).then_inc(w_in, 16)
            for i, name in enumerate(("k", "k", "v")):
                sp.dma_start(w2[:, i, :], layer_of(a[f"nsa_cmp_{name}_w2_2"], l)).then_inc(w_in, 16)

        @block.gpsimd
        def _(pool):
            for i, x in enumerate((k2, v2)):
                for g in range(G):
                    nc.gpsimd.tensor_copy(pairs_of[0:HD, i, g, :], x[0:HD, g, :]).then_inc(shifted, 1)
                    nc.gpsimd.tensor_copy(pairs_of[HD:P, i, g, 0:S - 1], x[HD:P, 1 - g, 1:S]).then_inc(shifted, 1)

        @block.tensor
        def _(pe):
            pe.wait_ge(w_in, 16 * 7)
            for i in range(2):
                pe.wait_ge(shifted, 4 * i + 4)
                for m in range(M):
                    nc.tensor.matmul(ps[:, i, 0:n].rearrange("p (g n) -> p g n", g=G), w1[:, i, m, :],
                                     pairs_of[:, i, :, 2 * m:2 * m + CMP_STRIDE * (N_CMP - 1) + 1:CMP_STRIDE],
                                     start=(m == 0), stop=(m == M - 1))
                at = (V_PEK, V_PEV)[i]
                for m in range(M):
                    last = nc.tensor.matmul(ps[:, 2, i:i + 1], w1[:, i, m, :], k.vec2[:, at + m:at + m + 1],
                                            start=(m == 0), stop=(m == M - 1))
                last.then_inc(hid_done, 1)
            pe.wait_ge(act_done, 2)
            nc.tensor.matmul(ps[:, 3, 0:n], w2[:, 0:2, :], hid[:, 0, :], start=True, stop=True).then_inc(out_done, 1)
            for g in range(G):
                last = nc.tensor.matmul(ps[0:N_CMP, 4, g * HD:(g + 1) * HD], hid[:, 1, g * N_CMP:(g + 1) * N_CMP], w2[:, 2, :],
                                        start=True, stop=True)
            last.then_inc(out_done, 1)

        @block.vector
        def _(dve):
            dve.wait_ge(hid_done, 2)
            nc.vector.tensor_copy(pe_cols[:, :], ps[:, 2, 0:2]).then_inc(pe_out, 1)
            dve.wait_ge(out_done, 1)
            nc.vector.tensor_copy(kc_dup[:, :], ps[:, 3, 0:n])
            dve.wait_ge(out_done, 2)
            nc.vector.tensor_copy(vc_rows[0:N_CMP, :, :], ps[0:N_CMP, 4, 0:G * HD].rearrange("p (g n) -> p g n", g=G))

        @block.scalar
        def _(act):
            act.wait_ge(pe_out, 1)
            for i in range(2):
                nc.scalar.activation(hid[:, i, :], ps[:, i, 0:n], ACT.Silu, bias=pe_cols[:, i:i + 1]).then_inc(act_done, 1)


def sparse_attention(k, qT, ks2, kw2, vs_rows, vw_rows, kc_dup, vc_rows, gates, mixT, mix_at):
    nc = k.nc
    UNITS = 2 * TC
    T = NSA_T
    with ExitStack() as ctx:
        def sb(name, shape):
            return ctx.enter_context(k.sbuf(name, shape))

        q_pair, k_pair = sb("q_pair", [P, S]), sb("k_pair", [P, 2, S])
        v_pair = sb("v_pair", [P, 2, TC, 2, HD])
        kc_pair, vc_pair = sb("kc_pair", [P, N_CMP]), sb("vc_pair", [P, 2, HD])
        gate_pair = sb("gate_pair", [P, 3, 2, TC])
        probs, probs_t = sb("probs", [P, 2, 2, S]), sb("probs_t", [P, 9, P])
        neg_max, sums = sb("neg_max", [P, 2, 2]), sb("sums", [P, 2, 2])
        cmp_p, cmp_col = sb("cmp_p", [P, UNITS, N_CMP]), sb("cmp_col", [P, 2, UNITS])
        banks = ctx.enter_context(k.psum("banks", [P, 8, S]))
        logits = banks[:, 0:4, :].rearrange("p (u m) n -> p u m n", m=2)
        turned = banks[:, 4:7, :].rearrange("p b (t n) -> p (b t) n", n=P)
        cmp_ps = banks[:, 4:6, 0:TC * N_CMP].rearrange("p u (c i) -> p u c i", c=TC)
        out_ps = banks[:, 7, :]
        (block, admitted, staged, cmp_done, cmp_step, cmp_exp, cmp_ready, logit_done, shifted, exp_done, recip_done, gated, scaled,
         turn_done, turn_out, pv_done, tile_out) = ctx.enter_context(stage(nc, (
             "admitted staged cmp_done cmp_step cmp_exp cmp_ready logit_done shifted exp_done recip_done gated scaled turn_done turn_out "
             "pv_done tile_out")))
        STAGED = 14

        def unit(n):
            u, qb = divmod(n, TC)
            return u, qb, (qb + 1) * P

        def by_unit(col):
            return col.unsqueeze(2).to_broadcast([P, UNITS, N_CMP])

        @block.gpsimd
        def _(pool):
            for t in range(T):
                if t:
                    pool.wait_ge(pv_done, t * UNITS + 1)
                    pool.wait_ge(gated, t * UNITS)
                nc.gpsimd.tensor_copy(q_pair[:, :], qT[:, t, :]).then_inc(staged, 1)
                for u in range(2):
                    g = (2 * t + u) // 3
                    for i, vx in enumerate((vs_rows, vw_rows)):
                        nc.gpsimd.tensor_copy(v_pair[:, i, :, u, :], vx[:, :, g * HD:(g + 1) * HD]).then_inc(staged, 1)
                    nc.gpsimd.tensor_copy(vc_pair[0:N_CMP, u, :], vc_rows[0:N_CMP, g, :]).then_inc(staged, 1)
                nc.gpsimd.tensor_copy(gate_pair[:, :, :, :].rearrange("p b u c -> p c b u"),
                                      gates.rearrange("p c (b h) -> p c b h", b=3)[:, :, :, 2 * t:2 * t + 2]).then_inc(staged, 1)
                for u in range(2):
                    g = (2 * t + u) // 3
                    at = slice(HD * u, HD * u + HD)
                    pool.wait_ge(staged, t * STAGED + 8 + 3 * u)
                    for i, kx in enumerate((ks2, kw2)):
                        nc.gpsimd.tensor_copy(k_pair[at, i, :], kx[at, int(g != u), :]).then_inc(staged, 1)
                    nc.gpsimd.tensor_copy(kc_pair[at, :], kc_dup[at, g * N_CMP:(g + 1) * N_CMP]).then_inc(staged, 1)
                pool.wait_ge(staged, t * STAGED + STAGED)

        @block.tensor
        def _(pe):
            pe.sem_inc(pv_done, 1)
            pe.sem_inc(turn_done, 1)
            with pe.Fori(0, T) as i:
                def score(n):
                    u, qb, keys = unit(n)
                    at = slice(HD * u, HD * u + HD)
                    if n >= 2:
                        pe.wait_ge(shifted, i * (2 * UNITS) + 2 * n - 1)
                    for m in range(2):
                        last = nc.tensor.matmul(logits[:, n % 2, m, 0:keys], q_pair[at, qb * P:(qb + 1) * P], k_pair[at, m, 0:keys],
                                                start=True, stop=True)
                    last.then_inc(logit_done, 1)

                pe.wait_ge(turn_out, i * (2 * UNITS) + 1)
                pe.wait_ge(staged, i * STAGED + STAGED)
                for n in range(UNITS):
                    u, qb, _ = unit(n)
                    at = slice(HD * u, HD * u + HD)
                    last = nc.tensor.matmul(cmp_ps[:, u, qb, :], q_pair[at, qb * P:(qb + 1) * P], kc_pair[at, :], start=True, stop=True)
                last.then_inc(cmp_done, 1)
                pe.wait_ge(shifted, i * (2 * UNITS) + 1)
                score(0)
                for n in range(UNITS):
                    u, qb, keys = unit(n)
                    at = slice(HD * u, HD * u + HD)
                    blocks = [(m * 4 + b, probs[:, n % 2, m, b * P:(b + 1) * P], v_pair[:, m, b, u, :])
                              for m in range(2) for b in range(qb + 1)]
                    if n + 1 < UNITS:
                        score(n + 1)
                    pe.wait_ge(scaled, i * (2 * UNITS) + 2 * n + 3)
                    pe.wait_ge(cmp_ready, i + 1)
                    pe.wait_ge(turn_out, i * (2 * UNITS) + 2 * n + 1)
                    for b, src, _ in blocks:
                        nc.tensor.transpose(turned[:, b, :], src, k.at["ident"])
                    nc.tensor.transpose(turned[0:N_CMP, 8, :], cmp_p[:, n, :], k.at["ident"]).then_inc(turn_done, 1)
                    pe.wait_ge(turn_out, i * (2 * UNITS) + 2 * n + 3)
                    if n == 0:
                        pe.wait_ge(tile_out, i + 1)
                    to = out_ps[at, qb * P:(qb + 1) * P]
                    for j, (b, _, v) in enumerate(blocks):
                        nc.tensor.matmul(to, v, probs_t[:, b, :], start=(j == 0), stop=False)
                    nc.tensor.matmul(to, vc_pair[0:N_CMP, u, :], probs_t[0:N_CMP, 8, :], start=False, stop=True).then_inc(pv_done, 1)

        @block.vector
        def _(dve):
            dve.sem_inc(scaled, 1)
            dve.sem_inc(tile_out, 1)
            dve.sem_inc(shifted, 1)
            with dve.Fori(0, T) as i:
                def shift(n):
                    u, qb, keys = unit(n)
                    p = n % 2
                    dve.wait_ge(logit_done, i * UNITS + n + 1)
                    dve.wait_ge(turn_done, i * UNITS + max(n, 1))
                    dve.sem_inc(admitted, 1)
                    for m in range(2):
                        nc.vector.tensor_tensor_reduce(probs[:, p, m, 0:keys], logits[:, p, m, 0:keys], k.at["causal_row"][:, S - keys:S],
                                                       -1.0, 3e38, ALU.add, ALU.min, neg_max[:, p, m:m + 1]).then_inc(shifted, 1)

                col, col2 = cmp_col[:, 0, :], cmp_col[:, 1, :]
                halves = cmp_p[:, :, :].rearrange("p (u c) i -> p u c i", u=2)
                dve.wait_ge(cmp_done, i + 1)
                dve.wait_ge(turn_done, i * UNITS + 1)
                for u in range(2):
                    nc.vector.tensor_tensor(halves[:, u], cmp_ps[:, u], k.at["cmp_add"].rearrange("p (c i) -> p c i", c=TC),
                                            ALU.add).then_inc(cmp_step, 1)
                dve.wait_ge(cmp_step, i * 9 + 2)
                nc.vector.tensor_reduce(col, cmp_p[:, :, :], AX, ALU.max).then_inc(cmp_step, 1)
                dve.wait_ge(cmp_step, i * 9 + 3)
                nc.vector.tensor_tensor(cmp_p[:, :, :], cmp_p[:, :, :], by_unit(col), ALU.subtract).then_inc(cmp_step, 1)
                dve.wait_ge(cmp_exp, i + 1)
                for u in range(2):
                    nc.vector.tensor_tensor(halves[:, u], halves[:, u], k.at["cmp_keep"].rearrange("p (c i) -> p c i", c=TC),
                                            ALU.mult).then_inc(cmp_step, 1)
                dve.wait_ge(cmp_step, i * 9 + 6)
                nc.vector.tensor_reduce(col2, cmp_p[:, :, :], AX, ALU.add).then_inc(cmp_step, 1)
                dve.wait_ge(cmp_step, i * 9 + 7)
                nc.vector.tensor_scalar(col2, col2, 1e-30, None, ALU.max).then_inc(cmp_step, 1)
                dve.wait_ge(cmp_step, i * 9 + 8)
                nc.vector.reciprocal(col2, col2).then_inc(cmp_step, 1)
                dve.wait_ge(cmp_step, i * 9 + 9)
                dve.wait_ge(staged, i * STAGED + STAGED)
                nc.vector.tensor_tensor(col, col2, gate_pair[:, 0, :, :].rearrange("p u c -> p (u c)"), ALU.mult).then_inc(recip_done, 1)
                dve.wait_ge(recip_done, i * (UNITS + 1) + 1)
                nc.vector.tensor_tensor(cmp_p[:, :, :], cmp_p[:, :, :], by_unit(col), ALU.mult).then_inc(cmp_ready, 1)
                shift(0)
                for n in range(UNITS):
                    u, qb, keys = unit(n)
                    p = n % 2
                    if n + 1 < UNITS:
                        shift(n + 1)
                    dve.wait_ge(exp_done, i * (2 * UNITS) + 2 * n + 2)
                    nc.vector.reciprocal(sums[:, p, :], sums[:, p, :]).then_inc(recip_done, 1)
                    dve.wait_ge(recip_done, i * (UNITS + 1) + n + 2)
                    nc.vector.tensor_tensor(sums[:, p, :], sums[:, p, :], gate_pair[:, 1:3, u, qb], ALU.mult).then_inc(gated, 1)
                    dve.wait_ge(gated, i * UNITS + n + 1)
                    for m in range(2):
                        nc.vector.tensor_scalar(probs[:, p, m, 0:keys], probs[:, p, m, 0:keys], sums[:, p, m:m + 1], None,
                                                ALU.mult).then_inc(scaled, 1)
                dve.wait_ge(pv_done, i * UNITS + UNITS + 1)
                nc.vector.tensor_copy(tile_of(mixT, i + mix_at), out_ps).then_inc(tile_out, 1)

        @block.scalar
        def _(act):
            act.sem_inc(turn_out, 1)
            with act.Fori(0, T) as i:
                def exps(n):
                    u, qb, keys = unit(n)
                    p = n % 2
                    act.wait_ge(scaled, i * (2 * UNITS) + max(2 * n - 1, 1))
                    for m in range(2):
                        act.wait_ge(shifted, i * (2 * UNITS) + 2 * n + m + 2)
                        nc.scalar.activation(probs[:, p, m, 0:keys], probs[:, p, m, 0:keys], ACT.Exp, scale=-1.0,
                                             bias=neg_max[:, p, m:m + 1], accum_out=sums[:, p, m:m + 1]).then_inc(exp_done, 1)

                act.wait_ge(cmp_step, i * 9 + 4)
                nc.scalar.activation(cmp_p[:, :, :], cmp_p[:, :, :], ACT.Exp).then_inc(cmp_exp, 1)
                exps(0)
                for n in range(UNITS):
                    u, qb, keys = unit(n)
                    if n + 1 < UNITS:
                        exps(n + 1)
                    act.wait_ge(turn_done, i * UNITS + n + 2)
                    act.wait_ge(pv_done, i * UNITS + n + 1)
                    nc.scalar.activation(probs_t[:, 0:8, :].rearrange("p (m b) q -> p m b q", m=2)[:, :, 0:qb + 1, :],
                                         turned[:, 0:8, :].rearrange("p (m b) q -> p m b q", m=2)[:, :, 0:qb + 1, :],
                                         ACT.Copy).then_inc(turn_out, 1)
                    nc.scalar.activation(probs_t[0:N_CMP, 8, :], turned[0:N_CMP, 8, :], ACT.Copy).then_inc(turn_out, 1)



def stick_breaking(k, qT, kT, v_rows, mixT, mix_at):
    nc = k.nc
    WIDTH = [S - b * P for b in range(TC)]
    AT = [sum(WIDTH[:b]) for b in range(TC + 1)]
    N = AT[TC]
    with ExitStack() as ctx:
        def sb(name, shape):
            return ctx.enter_context(k.sbuf(name, shape))

        q_pair, k_pair, v_pair = sb("q_pair", [P, S]), sb("k_pair", [P, S]), sb("v_pair", [P, TC, P])
        z, soft, tmp = sb("z", [P, N]), sb("soft", [P, N]), sb("tmp", [P, N])
        banks = ctx.enter_context(k.psum("banks", [P, 8, S]))
        z_ps, sum_ps, out_ps = banks[:, 0:4, :], banks[:, 4:8, :], banks[:, 0, :]
        (block, staged, z_done, z_out, abs_done, exp_done, log_done, soft_done, sum_done, arg_done, weight_done, pv_done,
         head_out) = ctx.enter_context(stage(nc, (
             "staged z_done z_out abs_done exp_done log_done soft_done sum_done arg_done weight_done pv_done head_out")))

        @block.gpsimd
        def _(pool):
            with pool.Fori(0, SB_T) as i:
                pool.wait_ge(pv_done, i * 2 + 1)
                nc.gpsimd.tensor_copy(q_pair[:, :], tile_of(qT, i)).then_inc(staged, 1)
                nc.gpsimd.tensor_copy(k_pair[:, :], tile_of(kT, i)).then_inc(staged, 1)
                nc.gpsimd.tensor_copy(v_pair[:, :, :], v_rows[:, :, bass.ds(i * P, P)]).then_inc(staged, 1)

        @block.tensor
        def _(pe):
            pe.sem_inc(pv_done, 1)
            with pe.Fori(0, SB_T) as i:
                pe.wait_ge(staged, i * 3 + 3)
                for u in range(2):
                    at = slice(HD * u, HD * u + HD)
                    pe.wait_ge(head_out, i * 2 + u + 1)
                    for b in range(TC):
                        nc.tensor.matmul(z_ps[:, b, 0:WIDTH[b]], k_pair[at, b * P:(b + 1) * P], q_pair[at, b * P:S],
                                         start=True, stop=True).then_inc(z_done, 1)
                    pe.wait_ge(soft_done, i * 2 + u + 1)
                    for b in range(TC):
                        for later in range(b, TC):
                            last = nc.tensor.matmul(sum_ps[:, b, (later - b) * P:WIDTH[b]], k.at["from_here"] if later == b else k.at["ones"],
                                                    soft[:, AT[later]:AT[later + 1]], start=(later == b), stop=(later == TC - 1))
                        last.then_inc(sum_done, 1)
                    pe.wait_ge(weight_done, i * 2 + u + 1)
                    for b in range(TC):
                        last = nc.tensor.matmul(out_ps[at, b * P:S], v_pair[:, b, at], z[:, AT[b]:AT[b + 1]],
                                                start=(b == 0), stop=(b == TC - 1))
                    last.then_inc(pv_done, 1)

        @block.vector
        def _(dve):
            dve.sem_inc(head_out, 1)
            with dve.Fori(0, SB_T) as i:
                for u in range(2):
                    at = slice(HD * u, HD * u + HD)
                    n = i * 2 + u
                    for b in range(TC):
                        dve.wait_ge(z_done, i * (2 * TC) + u * TC + b + 1)
                        nc.vector.tensor_tensor(z[:, AT[b]:AT[b + 1]], z_ps[:, b, 0:WIDTH[b]], k.at["strict_row"][:, 0:WIDTH[b]],
                                                ALU.add).then_inc(z_out, 1)
                    dve.wait_ge(log_done, n + 1)
                    nc.vector.scalar_tensor_tensor(soft[:, :], z[:, :], 0.0, tmp[:, :], ALU.max, ALU.add).then_inc(soft_done, 1)
                    for b in range(TC):
                        dve.wait_ge(sum_done, i * (2 * TC) + u * TC + b + 1)
                        nc.vector.tensor_tensor(z[:, AT[b]:AT[b + 1]], z[:, AT[b]:AT[b + 1]], sum_ps[:, b, 0:WIDTH[b]],
                                                ALU.subtract).then_inc(arg_done, 1)
                    dve.wait_ge(pv_done, n + 2)
                    nc.vector.tensor_copy(tile_of(mixT, i + mix_at)[at, :], out_ps[at, :]).then_inc(head_out, 1)

        @block.scalar
        def _(act):
            with act.Fori(0, SB_T) as i:
                for u in range(2):
                    n = i * 2 + u
                    act.wait_ge(z_out, i * (2 * TC) + u * TC + TC)
                    nc.scalar.activation(tmp[:, :], z[:, :], ACT.Abs).then_inc(abs_done, 1)
                    act.wait_ge(abs_done, n + 1)
                    nc.scalar.activation(tmp[:, :], tmp[:, :], ACT.Exp, scale=-1.0).then_inc(exp_done, 1)
                    act.wait_ge(exp_done, n + 1)
                    nc.scalar.activation(tmp[:, :], tmp[:, :], ACT.Ln, bias=1.0).then_inc(log_done, 1)
                    act.wait_ge(arg_done, i * (2 * TC) + u * TC + TC)
                    nc.scalar.activation(z[:, :], z[:, :], ACT.Exp).then_inc(weight_done, 1)



def second_mixer(k, a, l, mixT):
    nc = k.nc
    w = layer_of(a["w_in_2"], l)
    with ExitStack() as ctx:
        def sb(name, shape):
            return ctx.enter_context(k.sbuf(name, shape))

        qkv = sb("gdn_qkv", [P, 3 * GDN_T, CONV - 1 + S])
        gz = sb("gdn_z", [P, GDN_T, S])
        ab = sb("ab_rows", [P, TC, 30])
        nq = sb("nsa_q", [P, NSA_T, S])
        kc2, vc2, ks2, kw2 = (sb(f"nsa_{n}", [P, 2, S]) for n in ("kc", "vc", "ks", "kw"))
        vs_rows, vw_rows = sb("vs_rows", [P, TC, P]), sb("vw_rows", [P, TC, P])
        sq, sk, sv_rows = sb("sb_q", [P, SB_T, S]), sb("sb_k", [P, SB_T, S]), sb("sb_v", [P, TC, N_SB * HD])
        cols = sb("gdn_cols", [P, 4, TC * N_GDN])
        gates = sb("nsa_gates", [P, TC, 3 * N_NSA])

        def feat(at, dst, scale=None):
            return ("feat", at, P, lambda e, ps: copy_out(nc, e, dst, ps, scale))

        def rows(at, width, dst):
            return ("rows", at, width, lambda e, ps: copy_out(nc, e, dst, ps))

        def gdn_tile(j):
            return qkv[:, j, CONV - 1:] if j < 3 * GDN_T else gz[:, j - 3 * GDN_T, :]

        project_items(k, w, [([(W_GDN + t * COLS, COLS)], [feat(j * P, gdn_tile(4 * t + j)) for j in range(4)]) for t in range(3)] + [
            ([(W_AB, 12), (W_GATE, 18)], [rows(0, 30, ab[:, :, :])]),
            ([(W_NQ, 384)], [feat(j * P, nq[:, j, :], HD ** -0.5) for j in range(NSA_T)]),
            ([(W_KC, 512)], [feat(0, kc2[:, 0, :]), feat(P, vc2[:, 0, :]), feat(2 * P, ks2[:, 0, :]), rows(3 * P, P, vs_rows[:, :, :])]),
            ([(W_KW, 256)], [feat(0, kw2[:, 0, :]), rows(P, P, vw_rows[:, :, :])]),
            ([(W_SQ, 512)], [feat(j * P, sq[:, j, :], HD ** -0.5) for j in range(SB_T)] + [feat((2 + j) * P, sk[:, j, :]) for j in range(SB_T)]),
            ([(W_SV, 256)], [rows(j * P, P, sv_rows[:, :, j * P:(j + 1) * P]) for j in range(2)]),
        ])
        g, beta, beta_eg, to_end = (cols[:, i, :] for i in range(4))
        gdn_steps(k, a, l, ab, g, beta, beta_eg, to_end, gates[:, :, :])
        conv_silu(k, qkv, 3 * GDN_T, CONV, S, lambda t, j: k.vec2[:, bass.ds(t + (V_GCONV + 9 * j), 1)], None)
        norm_heads(k, [(qkv[:, t, CONV - 1:], HD ** -0.5 if t < GDN_T else 1.0, None) for t in range(2 * GDN_T)], 1.0)
        delta_rule(k, qkv, g, beta, beta_eg, to_end, mixT)
        rotate(k, [nq[:, j, :] for j in range(NSA_T)] + [x[:, 0, :] for x in (kc2, ks2, kw2)], k.at["swap_32"], k.cos, k.sin)
        swap_halves(k, [(x[:, 0, :], x[:, 1, :]) for x in (kc2, vc2, ks2, kw2)])
        with k.sbuf("kc_dup", [P, 2 * N_CMP]) as kc_dup, k.sbuf("vc_rows", [P, 2, HD]) as vc_rows:
            compress_keys(k, a, l, kc2, vc2, kc_dup, vc_rows)
            sparse_attention(k, nq, ks2, kw2, vs_rows, vw_rows, kc_dup, vc_rows, gates[:, :, :], mixT, GDN_T)
        stick_breaking(k, sq, sk, sv_rows, mixT, GDN_T + NSA_T)
        norm_heads(k, [(mixT[:, j, :], k.vec2[:, V_GN:V_GN + 1], gz[:, j, :]) for j in range(GDN_T)]
                   + [(mixT[:, GDN_T + j, :], k.vec2[:, V_NN:V_NN + 1], None) for j in range(NSA_T)]
                   + [(mixT[:, GDN_T + NSA_T + j, :], k.vec2[:, V_SN:V_SN + 1], None) for j in range(SB_T)], 1.0 / HD)


def conv_ffn(k, a, l):
    nc = k.nc
    taps = 3
    pad = taps - 1
    v = layer_of(a["w_up_2"], l).rearrange("(k p) n -> p k n", p=P)
    half = FF_T * P
    with k.sbuf("ff", [P, 2 * FF_T, pad + S]) as ff:
        def tile(t, j):
            return ff[:, bass.ds(2 * t + (j if j < 2 else FF_T + j - 2), 1), pad:].rearrange("p a n -> p (a n)")

        def slot(t, part):
            return v[:, :, bass.ds(t * (2 * P) + part * half, 2 * P)]

        project(k, FF_T // 2, slot, lambda e, t, j, ps: copy_out(nc, e, tile(t, j), ps), parts=2)
        with (
            k.sbuf("conv_acc", [P, 2, S]) as acc,
            stage(nc, "padded tap_done silu_done tile_done") as (block, padded, tap_done, silu_done, tile_done),
        ):
            @block.vector
            def _(dve):
                nc.vector.memset(ff[:, :, 0:pad], 0.0).then_inc(padded, 1)
                dve.wait_ge(padded, 1)
                with dve.Fori(0, FF_T) as t:
                    for u in range(2):
                        dve.wait_ge(tile_done, t + 1)
                        for j in range(taps):
                            x = ff[:, bass.ds(t + u * FF_T, 1), j:j + S].rearrange("p a n -> p (a n)")
                            tap = k.vec2[:, bass.ds(t + (V_FCONV + 2 * FF_T * j + u * FF_T), 1)]
                            if j == 0:
                                step = nc.vector.tensor_scalar(acc[:, u, :], x, tap, None, ALU.mult)
                            else:
                                dve.wait_ge(tap_done, t * (2 * taps) + u * taps + j)
                                step = nc.vector.scalar_tensor_tensor(acc[:, u, :], x, tap, acc[:, u, :], ALU.mult, ALU.add)
                            step.then_inc(tap_done, 1)

            @block.scalar
            def _(act):
                with act.Fori(0, FF_T) as t:
                    act.wait_ge(tap_done, t * (2 * taps) + taps)
                    nc.scalar.activation(ff[:, bass.ds(t, 1), pad:].rearrange("p a n -> p (a n)"), acc[:, 0, :], ACT.Silu).then_inc(silu_done, 1)

            @block.gpsimd
            def _(pool):
                pool.sem_inc(tile_done, 1)
                with pool.Fori(0, FF_T) as t:
                    pool.wait_ge(silu_done, t + 1)
                    pool.wait_ge(tap_done, t * (2 * taps) + 2 * taps)
                    x = ff[:, bass.ds(t, 1), pad:].rearrange("p a n -> p (a n)")
                    nc.gpsimd.tensor_tensor(x, x, acc[:, 1, :], ALU.mult).then_inc(tile_done, 1)
        down_project(k, layer_of(a["w_down_2"], l), ff[:, :, pad:], 2)


def layer_input(k, a, l):
    nc = k.nc
    K = 2
    with k.sbuf("ple_gate", [P, DT, S]) as gate, k.sbuf("pT", [P, K, S]) as pT, k.sbuf("p_rows", [P, TC, K * P]) as p_rows:
        with (
            k.psum("turned", [P, K, S]) as turned,
            stage(nc, "p_in turn_done") as (block, p_in, turn_done),
        ):
            @block.sync
            def _(sp):
                sp.dma_start(p_rows[:, :, :], layer_of(a["p_2"], l)[0].rearrange("(c p) n -> p c n", p=P)).then_inc(p_in, 16)

            @block.tensor
            def _(pe):
                pe.wait_ge(p_in, 16)
                for f in range(K):
                    for c in range(TC):
                        last = nc.tensor.transpose(turned[:, f, c * P:(c + 1) * P], p_rows[:, c, f * P:(f + 1) * P], k.at["ident"])
                    last.then_inc(turn_done, 1)

            @block.vector
            def _(dve):
                for f in range(K):
                    dve.wait_ge(turn_done, f + 1)
                    nc.vector.tensor_copy(pT[:, f, :], turned[:, f, :])

        project(k, 2, weight_tiles(layer_of(a["w_ple_gate_2"], l), 0),
                lambda e, t, j, ps: copy_out(nc, e, tile_of(gate, 4 * t + j), ps))
        with stage(nc, "none") as (block, _none):
            @block.scalar
            def _(act):
                nc.scalar.activation(gate[:, :, :], gate[:, :, :], ACT.Sigmoid)
        down_project(k, layer_of(a["w_ple_2"], l), pT, K, post=lambda f: k.vec2[:, V_PLEN + f:V_PLEN + f + 1], gate=gate)


def store_output(k, a):
    nc = k.nc
    with (
        k.sbuf("y_rows", [P, TC, D]) as y_rows, k.psum("turned", [P, TC, 2, S]) as turned,
        stage(nc, "turn_done out_done stored") as (block, turn_done, out_done, stored),
    ):
        @block.tensor
        def _(pe):
            for c in range(TC):
                for f in range(DT):
                    last = nc.tensor.transpose(turned[:, c, f // 4, (f % 4) * P:(f % 4 + 1) * P], k.hT[:, f, c * P:(c + 1) * P], k.at["ident"])
                last.then_inc(turn_done, 1)

        @block.vector
        def _(dve):
            for c in range(TC):
                dve.wait_ge(turn_done, c + 1)
                nc.vector.tensor_copy(y_rows[:, c, :], turned[:, c, :, :].rearrange("p b n -> p (b n)")).then_inc(out_done, 1)

        @block.sync
        def _(sp):
            for c in range(TC):
                sp.wait_ge(out_done, c + 1)
                sp.dma_start(a["y"][0, c * P:(c + 1) * P, :], y_rows[:, c, :]).then_inc(stored, 16)
            sp.wait_ge(stored, 16 * TC)


def place(k, buf, arrays):
    at = 0
    for name, array in arrays.items():
        k.at[name] = buf[:, at:at + array.shape[1]]
        at += array.shape[1]


def first_blocks(k, a):
    with ExitStack() as ctx:
        def sb(name, shape):
            return ctx.enter_context(k.sbuf(name, shape))

        k.vec = sb("vec", [P, 2 * P + 1])
        k.c_act = sb("c_act", [P, DT])[:, :]
        k.mod = sb("mod", [P, 96])
        k.pre_gain = sb("pre_gain", [P, 4, DT])
        k.post_gain = sb("post_gain", [P, 4, DT])
        k.ssd_d = sb("ssd_d", [P, SSD_HEADS])[:, :]
        k.band = sb("band", [P, HEADS, BAND])
        k.far = sb("far", [P, HEADS])[:, :]
        load_inputs(k, a)
        modulation(k, a)
        relative_bias(k, a)
        pre_norm(k, 0)
        with k.sbuf("mixT", [P, 16, S]) as mixT:
            even_ssd(k, a, mixT)
            even_diff(k, a, mixT)
            down_project(k, a["e_w_out"][0], mixT, 4, post=lambda f: k.post_gain[:, 0, f:f + 1])
        pre_norm(k, 1)
        squared_relu_mlp(k, a, 0, 1)
        pre_norm(k, 2)
        with k.sbuf("mixT", [P, 12, S]) as mixT:
            odd_mixer(k, a, mixT)
            down_project(k, a["o_w_out"][0], mixT, 4, post=lambda f: k.post_gain[:, 2, f:f + 1])
        pre_norm(k, 3)
        squared_relu_mlp(k, a, 1, 3)


def second_blocks(k, a):
    with k.sbuf("const2_sb", list(a["const2"].shape)) as const2, k.sbuf("vec2", [P, V_FCONV + 3 * 2 * FF_T]) as k.vec2, \
            k.sbuf("cos", [P, S]) as cos, k.sbuf("sin", [P, S]) as sin:
        place(k, const2, second_constants())
        k.level_masks = [k.at[f"level_{n}"] for n in range(6)]
        k.cos, k.sin = cos[:, :], sin[:, :]
        with stage(k.nc, "const_in") as (block, const_in):
            @block.sync
            def _(sp):
                sp.dma_start(const2[:, :], a["const2"]).then_inc(const_in, 16)
                sp.wait_ge(const_in, 16)
        rotary_tables(k, a)
        with k.nc.Fori(0, 2) as l:
            def gain(at):
                return lambda f: k.vec2[:, at + f:at + f + 1]

            layer_vectors(k, a, l)
            norm_into(k, gain(V_MIX))
            second_mixer(k, a, l, k.hT)
            down_project(k, layer_of(a["w_out_2"], l), k.hT, 4)
            norm_into(k, gain(V_FFN))
            conv_ffn(k, a, l)
            norm_into(k, gain(V_PLE))
            layer_input(k, a, l)
        norm_into(k, gain(V_FIN))


def build(nc, a):
    k = Kit(nc)
    with ExitStack() as ctx:
        def sb(name, shape):
            return ctx.enter_context(k.sbuf(name, shape))

        k.const = sb("const_sb", list(a["const"].shape))
        place(k, k.const, constants())
        k.xT = sb("xT", [P, DT, S])
        k.hT = sb("hT", [P, DT, S])
        k.ring = sb("ring", [P, SLOTS, DT, COLS])
        first_blocks(k, a)
        second_blocks(k, a)
        store_output(k, a)


INS = ["x", "c", "rel_bias", "norm_gains", "mod_w", "mod_b", "mlp_w1", "mlp_w2", "e_w_in", "e_conv_w", "e_conv_b",
       "e_dt_bias", "e_A_log", "e_D", "e_ssd_norm", "e_lambda", "e_diff_norm", "e_w_out", "o_w_in", "o_sinks", "o_w_out",
       "p_2", "positions_2", "ln_mix_2", "w_in_2", "gdn_conv_2", "gdn_a_log_2", "gdn_dt_bias_2", "gdn_norm_2", "nsa_pe_k_2",
       "nsa_pe_v_2", "nsa_cmp_k_w1_2", "nsa_cmp_k_w2_2", "nsa_cmp_v_w1_2", "nsa_cmp_v_w2_2", "nsa_norm_2", "sb_norm_2",
       "w_out_2", "ln_ffn_2", "w_up_2", "ffn_conv_2", "w_down_2", "ln_ple_2", "w_ple_gate_2", "w_ple_2", "ple_norm_2",
       "ln_final_2"]


def kernel(**inputs):
    import concourse.bacc as bacc
    from concourse.bass_utils import run_bass_kernel_spmd as run

    nc = bacc.Bacc("TRN2", target_bir_lowering=False, num_devices=1)
    arrays, args = {}, {}

    def declare(name, array):
        arrays[f"in_{name}"] = array
        args[name] = nc.dram_tensor(f"in_{name}", array.shape, mybir.dt.from_np(array.dtype), kind="ExternalInput").ap()

    for name in INS:
        declare(name, np.ascontiguousarray(inputs[name]))
    for name, arrays_of in (("const", constants()), ("const2", second_constants())):
        declare(name, np.concatenate([v.astype(np.float32) for v in arrays_of.values()], axis=1))
    declare("one_hot", (np.arange(REL_BUCKETS)[:, None] == bucket_of(BAND - 1 - np.arange(3 * P))[None, :]).astype(np.float32))
    declare("ret_table", retention_constants()[0])
    args["y"] = nc.dram_tensor("out_y", (1, S, D), F32, kind="ExternalOutput").ap()
    build(nc, args)
    r = run(nc, [arrays], core_ids=[0])
    return r.results[0]["out_y"]
```

```python
from contextlib import ExitStack, contextmanager

import numpy as np

import concourse.bass as bass
from concourse import mybir

P = 128
F32 = mybir.dt.float32
F32R = mybir.dt.float32r
I32 = mybir.dt.int32
ACT = mybir.ActivationFunctionType
ALU = mybir.AluOpType
AX = mybir.AxisListType.X

D = 1024
DT = D // P
S = 512
TC = S // P
EPS = 1e-6
NEG = -1e30
COLS = 512
SLOTS = 2
DEEP = 4


@contextmanager
def stage(nc, names):
    with ExitStack() as ctx:
        sems = [ctx.enter_context(nc.semaphore(n)) for n in names.split()]
        with nc.Block() as block:
            yield (block, *sems)
        for s in sems:
            nc.gpsimd.sem_clear(s)
        nc.all_engine_barrier()


def constants():
    i = np.arange(P)
    c = {}
    c["ident"] = np.eye(P)
    c["ones"] = np.ones((P, P))
    c["upto"] = i[:, None] <= i[None, :]
    c["after"] = i[:, None] > i[None, :]
    c["flip"] = np.eye(P)[::-1]
    c["causal"] = np.where(i[None, :] > i[:, None], NEG, 0.0)
    dist = i[:, None] - np.arange(BAND)[None, :] + P
    c["window"] = np.where((dist >= 0) & (dist < P), 0.0, NEG)
    c["swap_128"] = np.eye(P)[(i + 64) % P]
    c["eps"] = np.full((P, 1), EPS)
    return c


def second_constants():
    i = np.arange(P)
    same = (i[:, None] // 64) == (i[None, :] // 64)
    causal = np.where(i[None, :] > i[:, None], NEG, 0.0)
    c = {}
    c["causal_row"] = np.concatenate([np.zeros((P, S - P)), causal], axis=1)
    c["strict_row"] = np.concatenate([np.where(i[None, :] <= i[:, None], NEG, 0.0), np.zeros((P, S - P))], axis=1)
    c["from_here"] = i[:, None] >= i[None, :]
    c["upto_64"] = (i[:, None] <= i[None, :]) & same
    c["after_64"] = (i[:, None] > i[None, :]) & same
    c["ones_64"] = same
    c["swap_32"] = np.eye(P)[i ^ 32]
    for level in range(6):
        n = 1 << level
        c[f"level_{level}"] = ((i[:, None] // (2 * n) == i[None, :] // (2 * n)) & (i[:, None] // n % 2 == 0) & (i[None, :] // n % 2 == 1))
    c["first_mask"] = c["level_0"].T
    inv = np.float32(10000.0) ** (-np.arange(32, dtype=np.float32) / 32)
    c["inv_freq"] = inv[i % 32][:, None]
    c["half_sign"] = np.where(i % 64 < 32, -1.0, 1.0)[:, None]
    ends = np.arange(N_CMP) * CMP_STRIDE + CMP_LEN - 1
    seen = ends[None, None, :] <= (np.arange(TC)[None, :, None] * P + i[:, None, None])
    c["cmp_keep"] = seen.reshape(P, -1)
    c["cmp_add"] = np.where(seen, 0.0, NEG).reshape(P, -1)
    return c


class Kit:

    def __init__(self, nc):
        self.nc = nc
        self.named = {}
        self.at = {}

    def unique(self, name):
        self.named[name] = self.named.get(name, 0) + 1
        return name if self.named[name] == 1 else f"{name}_{self.named[name]}"

    def sbuf(self, name, shape, dtype=F32):
        return self.nc.sbuf_tensor(self.unique(name), shape, dtype)

    def psum(self, name, shape):
        return self.nc.psum_tensor(self.unique(name), shape, F32)


def load_inputs(k, a):
    nc = k.nc
    with (
        k.sbuf("x_rows", [P, TC, D]) as x_rows,
        k.sbuf("vec_rows", [P, 3, P]) as vec_rows,
        k.psum("turned", [P, 8, S]) as turned,
        stage(nc, "const_in x_in rows_in x_turned x_out vec_turned vec_out_a") as
        (block, const_in, x_in, rows_in, x_turned, x_out, vec_turned, vec_out),
    ):
        rows = [
            (0, 0, 64, a["norm_gains"].rearrange("l n (f p) -> (l n f) p", p=P)),
            (0, 64, 64, a["e_conv_w"].rearrange("a t (f p) -> (a t f) p", p=P)),
            (1, 0, 96, a["mod_b"].rearrange("l s (f p) -> (l s f) p", p=P)),
            (1, 96, 16, a["e_conv_b"].rearrange("a (f p) -> (a f) p", p=P)),
            (1, 112, 8, a["e_ssd_norm"].rearrange("a (f p) -> (a f) p", p=P)),
            (1, 120, 8, a["c"].rearrange("a (f p) -> (a f) p", p=P)),
            (2, 0, 1, a["e_diff_norm"]),
        ]
        used = (P, P, 1)

        @block.sync
        def _(sp):
            sp.dma_start(k.const[:, :], a["const"]).then_inc(const_in, 16)
            for c in range(TC):
                sp.dma_start(x_rows[:, c, :], a["x"][0, c * P:(c + 1) * P, :]).then_inc(x_in, 16)
            for g, at, n, src in rows:
                sp.dma_start(vec_rows[at:at + n, g, :], src).then_inc(rows_in, 16)

        @block.tensor
        def _(pe):
            pe.wait_ge(const_in, 16)
            pe.wait_ge(x_in, 16 * TC)
            for f in range(DT):
                for c in range(TC):
                    last = nc.tensor.transpose(turned[:, f, c * P:(c + 1) * P],
                                               x_rows[:, c, f * P:(f + 1) * P], k.at["ident"])
                last.then_inc(x_turned, 1)
            pe.wait_ge(rows_in, 16 * len(rows))
            for g in range(3):
                pe.wait_ge(x_out, g + 1)
                n = used[g]
                nc.tensor.transpose(turned[:, g, 0:n], vec_rows[0:n, g, :],
                                    k.at["ident"][0:n, 0:n]).then_inc(vec_turned, 1)

        @block.vector
        def _(dve):
            for f in range(DT):
                dve.wait_ge(x_turned, f + 1)
                nc.vector.tensor_copy(k.xT[:, f, :], turned[:, f, :]).then_inc(x_out, 1)
            for g in range(3):
                dve.wait_ge(vec_turned, g + 1)
                nc.vector.tensor_copy(k.vec[:, g * P:g * P + used[g]], turned[:, g, 0:used[g]]).then_inc(vec_out, 1)

        @block.scalar
        def _(act):
            act.wait_ge(vec_out, 2)
            nc.scalar.activation(k.c_act, k.vec[:, P + 120:P + 128], ACT.Silu)


def modulation(k, a):
    nc = k.nc
    tiles = 3 * D // COLS
    w = a["mod_w"].rearrange("l s (k p) n -> (l s) p k n", p=P)
    with (
        k.sbuf("ring", [P, SLOTS, DT, COLS]) as ring, k.sbuf("acc", [P, 2, 2, COLS]) as acc,
        k.psum("mod_cols", [P, 96]) as mod_cols,
        stage(nc, "landed0 landed1 summed freed cols_done mod_ready") as
        (block, landed0, landed1, summed, freed, cols_done, mod_ready),
    ):
        landed = (landed0, landed1)

        @block.sync
        def _(sp):
            with sp.Fori(0, 4) as s:
                for j in range(tiles):
                    sp.wait_ge(freed, s * tiles + j + 1)
                    sp.dma_start(ring[:, j % 2, :, :],
                                 w[bass.ds(s, 1), :, :, j * COLS:(j + 1) * COLS].rearrange("a p k n -> p (a k) n")
                                 ).then_inc(landed[j % 2], 16)

        @block.vector
        def _(dve):
            dve.sem_inc(freed, 2)
            with dve.Fori(0, 4) as s:
                for j in range(tiles):
                    dve.wait_ge(landed[j % 2], s * (8 * tiles) + 16 * (j // 2) + 16)
                    dve.wait_ge(cols_done, s * tiles + j + 1)
                    for c in range(DT):
                        if c < 2:
                            step = nc.vector.tensor_scalar(acc[:, j % 2, c, :], ring[:, j % 2, c, :],
                                                           k.c_act[:, c:c + 1], None, ALU.mult)
                        else:
                            dve.wait_ge(summed, s * (tiles * DT) + j * DT + c - 1)
                            step = nc.vector.scalar_tensor_tensor(acc[:, j % 2, c % 2, :], ring[:, j % 2, c, :],
                                                                  k.c_act[:, c:c + 1], acc[:, j % 2, c % 2, :],
                                                                  ALU.mult, ALU.add)
                        step.then_inc(summed, 1)
                    dve.wait_ge(summed, s * (tiles * DT) + (j + 1) * DT)
                    dve.sem_inc(freed, 1)
            dve.wait_ge(cols_done, 4 * tiles + 2)
            nc.vector.tensor_tensor(k.mod[:, :], mod_cols[:, :], k.vec[:, P:P + 96], ALU.add).then_inc(mod_ready, 1)
            dve.wait_ge(mod_ready, 1)
            for s in range(4):
                pre = k.vec[:, (2 * s) * DT:(2 * s + 1) * DT]
                post = k.vec[:, (2 * s + 1) * DT:(2 * s + 2) * DT]
                nc.vector.scalar_tensor_tensor(k.pre_gain[:, s, :], k.mod[:, s * 24 + DT:s * 24 + 2 * DT], 1.0, pre,
                                               ALU.add, ALU.mult)
                nc.vector.tensor_tensor(k.post_gain[:, s, :], k.mod[:, s * 24 + 2 * DT:s * 24 + 3 * DT], post, ALU.mult)

        @block.tensor
        def _(pe):
            pe.sem_inc(cols_done, 2)
            with pe.Fori(0, 4) as s:
                for j in range(tiles):
                    pe.wait_ge(summed, s * (tiles * DT) + (j + 1) * DT)
                    for q in range(4):
                        for e in range(2):
                            last = nc.tensor.matmul(mod_cols[:, bass.ds(s * 24 + (j * 4 + q), 1)], acc[:, j % 2, e, q * P:(q + 1) * P],
                                                    k.at["ones"][:, 0:1], start=(e == 0), stop=(e == 1))
                    last.then_inc(cols_done, 1)


def keep_hi(nc, hi, x):
    return nc.scalar.activation(hi.bitcast(F32R), x, ACT.Copy)


def keep_lo(nc, lo, x, hi):
    return nc.vector.tensor_tensor(lo.bitcast(F32R), x, hi, ALU.subtract)


def three_products(nc, out, weights, moving, start, stop, **kw):
    (wh, wl), (xh, xl) = ((hi.bitcast(F32R), lo.bitcast(F32R)) for hi, lo in (weights, moving))
    nc.tensor.matmul(out, wh, xl, start=start, stop=False, **kw)
    nc.tensor.matmul(out, wh, xh, start=False, stop=False, **kw)
    return nc.tensor.matmul(out, wl, xh, start=False, stop=stop, **kw)


def norm_into(k, gain, shift=None, whole=None):
    nc = k.nc
    with (
        k.sbuf("normed", [P, DT, S]) as normed,
        k.sbuf("log_ms", [P, S]) as log_ms,
        k.sbuf("rstd", [P, S]) as rstd,
        k.psum("stat", [P, S]) as stat,
        stage(nc, "squared stat_done log_done rstd_done scaled moved hi_done") as
        (block, squared, stat_done, log_done, rstd_done, scaled, moved, hi_done),
    ):
        hT = normed if whole is None else whole

        @block.scalar
        def _(act):
            for f in range(DT):
                nc.scalar.activation(hT[:, f, :], k.xT[:, f, :], ACT.Square).then_inc(squared, 1)
            act.wait_ge(stat_done, 1)
            inverse_root(k, act, rstd[:, :], log_ms[:, :], stat[:, :], 1.0 / D, log_done).then_inc(rstd_done, 1)
            if shift is not None:
                for f in range(DT):
                    act.wait_ge(scaled, f + 1)
                    nc.scalar.activation(hT[:, f, :], hT[:, f, :], ACT.Identity, bias=shift(f)).then_inc(moved, 1)
            if whole is None:
                for f in range(DT):
                    act.wait_ge(scaled if shift is None else moved, f + 1)
                    keep_hi(nc, k.h_hi[:, f, :], hT[:, f, :]).then_inc(hi_done, 1)

        @block.tensor
        def _(pe):
            for f in range(DT):
                pe.wait_ge(squared, f + 1)
                last = nc.tensor.matmul(stat[:, :], k.at["ones"], hT[:, f, :], start=(f == 0), stop=(f == DT - 1))
            last.then_inc(stat_done, 1)

        @block.vector
        def _(dve):
            dve.wait_ge(rstd_done, 1)
            for f in range(DT):
                nc.vector.scalar_tensor_tensor(hT[:, f, :], k.xT[:, f, :], gain(f), rstd[:, :],
                                               ALU.mult, ALU.mult).then_inc(scaled, 1)
            if whole is None:
                for f in range(DT):
                    dve.wait_ge(hi_done, f + 1)
                    keep_lo(nc, k.h_lo[:, f, :], hT[:, f, :], k.h_hi[:, f, :])


def inverse_root(k, act, out, log, total, scale, log_done, nth=1):
    nc = k.nc
    nc.scalar.activation(log, total, ACT.Ln, bias=k.at["eps"][0:log.shape[0], :], scale=scale).then_inc(log_done, 1)
    act.wait_ge(log_done, nth)
    return nc.scalar.activation(out, log, ACT.Exp, scale=-0.5)


def project(k, runs, conv=None):
    nc = k.nc
    h_hi, h_lo = k.h_hi, k.h_lo
    with (
        k.sbuf("ring", [P, SLOTS, DT, COLS]) as ring, k.sbuf("w_hi", [P, DT, COLS]) as w_hi, k.sbuf("w_lo", [P, DT, COLS]) as w_lo,
        k.psum("out", [P, 2, 4, S]) as out,
        k.sbuf("conv_acc", [P, 2, 4, S if conv else 1]) as acc,
        stage(nc, "first0 first1 first2 first3 landed0 landed1 hi_done lo_done used bank_done even_freed odd_freed tap_done second_done silu_done tile_done") as
        (block, *first, landed0, landed1, hi_done, lo_done, used, bank_done, even_freed, odd_freed,
         tap_done, second_done, silu_done, tile_done),
    ):
        landed = (landed0, landed1)
        loads = 16 * runs[0][5]

        def each_tile(eng, body):
            base = 0
            for r, run in enumerate(runs):
                def one(i, u, end):
                    following = run if not end else runs[r + 1] if r + 1 < len(runs) else None
                    body(run, 2 * i + u, 2 * i + (base + u), i + base // 2, u, following)
                pairs(eng, run[0], one)
                base += run[0]

        def columns(j):
            return slice(j * P, j * P + P)

        def quarter(q):
            return slice(2 * q, 2 * q + 2)

        @block.sync
        def _(sp):
            def load(run, t, n, i, u, following):
                _, w_tile, _, _, _, parts = run
                sp.wait_ge(lo_done, n * 4 + 4)
                for part in range(parts):
                    width = COLS // parts
                    at = slice(part * width, (part + 1) * width)
                    src = w_tile(t) if parts == 1 else w_tile(t, part)
                    if isinstance(n, int) and n == 0:
                        for q in range(4):
                            sp.dma_start(ring[:, 0, quarter(q), at], src[:, quarter(q), :]).then_inc(first[q], 16)
                    else:
                        sp.dma_start(ring[:, u, :, at], src).then_inc(landed[u], 16)
            each_tile(sp, load)

        @block.tensor
        def _(pe):
            def multiply(run, t, n, i, u, following):
                pe.wait_ge(even_freed, n * 2 + 2)
                pe.wait_ge(odd_freed, n * 2 + 2)
                for q in range(4):
                    pe.wait_ge(lo_done, n * 4 + (q + 9))
                    for j in range(4):
                        for c in (2 * q, 2 * q + 1):
                            if run[3]:
                                last = three_products(nc, out[:, u, j, :], (h_hi[:, c, columns(j)], h_lo[:, c, columns(j)]),
                                                      (w_hi[:, c, :], w_lo[:, c, :]), c == 0, c == DT - 1)
                            else:
                                last = three_products(nc, out[:, u, j, :], (w_hi[:, c, columns(j)], w_lo[:, c, columns(j)]),
                                                      (h_hi[:, c, :], h_lo[:, c, :]), c == 0, c == DT - 1)
                        if q == 3:
                            last.then_inc(bank_done, 1)
                    if q < 3:
                        last.then_inc(used, 1)
            each_tile(pe, multiply)

        @block.scalar
        def _(act):
            act.sem_inc(even_freed, 4)

            def keep(u, q):
                keep_hi(nc, w_hi[:, quarter(q), :], ring[:, u, quarter(q), :]).then_inc(hi_done, 1)

            def empty(run, t, n, i, u, following):
                for q in range(3) if following else ():
                    act.wait_ge(landed[1 - u], i * loads + loads)
                    act.wait_ge(used, n * 3 + (q + 1))
                    keep(1 - u, q)
                for j in (0, 2) if conv is None else ():
                    act.wait_ge(bank_done, n * 4 + (j + 1))
                    run[2]("act", t, j, out[:, u, j, :]).then_inc(even_freed, 1)
                for j in range(4) if conv else ():
                    act.wait_ge(tile_done, n * 2 + 2)
                    act.wait_ge(bank_done, n * 4 + (j + 1))
                    nc.scalar.activation(acc[:, u, j, :], out[:, u, j, :], ACT.Copy, scale=conv[0](t, j, 2)).then_inc(tap_done, 1)
                    if j in (1, 2):
                        act.wait_ge((even_freed, odd_freed)[j - 1], n * 2 + 5)
                        nc.scalar.activation(acc[:, u, j - 1, :], acc[:, u, j - 1, :], ACT.Silu).then_inc(silu_done, 1)
                if following:
                    act.wait_ge(bank_done, n * 4 + 4)
                    keep(1 - u, 3)
            for q in range(4):
                act.wait_ge(first[q], loads)
                keep(0, q)
            each_tile(act, empty)

        @block.vector
        def _(dve):
            dve.sem_inc(odd_freed, 4)

            dve.sem_inc(lo_done, 8)

            def split(n, u, q):
                dve.wait_ge(hi_done, n * 4 + (q + 1))
                keep_lo(nc, w_lo[:, quarter(q), :], ring[:, u, quarter(q), :], w_hi[:, quarter(q), :]).then_inc(lo_done, 1)

            def empty(run, t, n, i, u, following):
                for q in range(3) if following else ():
                    split(n + 1, 1 - u, q)
                for j in (1, 3) if conv is None else ():
                    dve.wait_ge(bank_done, n * 4 + (j + 1))
                    run[2]("dve", t, j, out[:, u, j, :]).then_inc(odd_freed, 1)
                for j in range(4) if conv else ():
                    dve.wait_ge(tap_done, n * 4 + (j + 1))
                    nc.vector.scalar_tensor_tensor(acc[:, u, j, 1:], out[:, u, j, 0:S - 1], conv[0](t, j, 1), acc[:, u, j, 1:],
                                                   ALU.mult, ALU.add).then_inc(second_done, 1)
                    dve.wait_ge(second_done, n * 4 + (j + 1))
                    nc.vector.scalar_tensor_tensor(acc[:, u, j, 2:], out[:, u, j, 0:S - 2], conv[0](t, j, 0), acc[:, u, j, 2:],
                                                   ALU.mult, ALU.add).then_inc((even_freed, odd_freed)[j % 2], 1)
                if following:
                    split(n + 1, 1 - u, 3)
            for q in range(4):
                split(0, 0, q)
            each_tile(dve, empty)

        @block.gpsimd
        def _(pool):
            def finish(run, t, n, i, u, following):
                for j in range(4):
                    pool.wait_ge((even_freed, odd_freed)[j % 2], n * 2 + (j // 2 + 5))
                    run[4](t, j)
            if runs[0][4] is not None:
                each_tile(pool, finish)

            def gate(run, t, n, i, u, following):
                for j in range(2):
                    pool.wait_ge(silu_done, n * 2 + (j + 1))
                    pool.wait_ge((even_freed, odd_freed)[j], n * 2 + 6)
                    nc.gpsimd.tensor_tensor(conv[1](t, j), acc[:, u, j, :], acc[:, u, 2 + j, :], ALU.mult).then_inc(tile_done, 1)
            if conv:
                pool.sem_inc(tile_done, 4)
                each_tile(pool, gate)


def run(n_tiles, w_tile, evac, rows=False, after=None, parts=1):
    return n_tiles, w_tile, evac, rows, after, parts


def pairs(eng, n_tiles, body):
    looped = (n_tiles - 1) // 2
    if looped < 3:
        looped = 1
    for t in range(min(2, n_tiles)):
        body(0, t, t == n_tiles - 1)
    if looped >= 3:
        with eng.Fori(1, looped) as i:
            for u in range(2):
                body(i, u, False)
    for t in range(2 * looped, n_tiles):
        body(t // 2, t % 2, t == n_tiles - 1)


def copy_out(nc, engine, dst, src, scale=None):
    if engine == "act":
        return nc.scalar.activation(dst, src, ACT.Copy, scale=1.0 if scale is None else scale)
    if scale is None:
        return nc.vector.tensor_copy(dst, src)
    return nc.vector.tensor_scalar(dst, src, scale, None, ALU.mult)



SSD_HEADS, SSD_P, SSD_G = 16, 64, 4
CONV = 4
XBC_T = 16
E_Z, E_XBC, E_DT, E_Q, E_K, E_V = 0, 1024, 3072, 3088, 4112, 5136


def weight_tiles(w, col):
    v = w.rearrange("(k p) n -> p k n", p=P)
    return lambda t: v[:, :, bass.ds(t * COLS + col, COLS)]


def conv_silu(k, raw, n_tiles, taps, width, tap_col, bias_col):
    nc = k.nc
    pad = taps - 1
    with (
        k.sbuf("conv_acc", [P, 2, width]) as acc,
        stage(nc, "padded tap_done silu_done") as (block, padded, tap_done, silu_done),
    ):
        @block.vector
        def _(dve):
            nc.vector.memset(raw[:, :, 0:pad], 0.0).then_inc(padded, 1)
            dve.wait_ge(padded, 1)

            def taps_of(i, u, _end):
                t = 2 * i + u
                dve.wait_ge(silu_done, 2 * i + u + 1)
                for j in range(taps):
                    x = raw[:, bass.ds(t, 1), j:j + width].rearrange("p a n -> p (a n)")
                    if j == 0:
                        step = nc.vector.tensor_scalar(acc[:, u, :], x, tap_col(t, j), None, ALU.mult)
                    else:
                        dve.wait_ge(tap_done, (2 * i + u) * taps + j)
                        step = nc.vector.scalar_tensor_tensor(acc[:, u, :], x, tap_col(t, j), acc[:, u, :],
                                                              ALU.mult, ALU.add)
                    step.then_inc(tap_done, 1)
            pairs(dve, n_tiles, taps_of)

        @block.scalar
        def _(act):
            act.sem_inc(silu_done, 2)

            def finish(i, u, _end):
                t = 2 * i + u
                act.wait_ge(tap_done, (2 * i + u) * taps + taps)
                out = raw[:, bass.ds(t, 1), pad:pad + width].rearrange("p a n -> p (a n)")
                if bias_col is None:
                    step = nc.scalar.activation(out, acc[:, u, :], ACT.Silu)
                else:
                    step = nc.scalar.activation(out, acc[:, u, :], ACT.Silu, bias=bias_col(t))
                step.then_inc(silu_done, 1)
            pairs(act, n_tiles, finish)


def ssd_steps(k, a, dt, dt_a, eacs, to_end, total):
    nc = k.nc
    H = SSD_HEADS
    n = TC * H
    w = a["e_w_in"][0].rearrange("(k p) n -> p k n", p=P)
    with (
        k.sbuf("w_dt", [P, DT, H]) as w_dt,
        k.sbuf("rows", [P, 3, H]) as rows,
        k.sbuf("tmp", [P, 6, n]) as tmp,
        k.psum("dt_ps", [P, n]) as dt_ps,
        k.psum("sums", [P, 3, S]) as sums,
        stage(nc, "w_in rows_in dt_done step neg_a exp_done log_done sum_done") as
        (block, w_in, rows_in, dt_done, step, neg_a, exp_done, log_done, sum_done),
    ):
        v, mag, u, w1, corr, neg = (tmp[:, i, :] for i in range(6))

        @block.sync
        def _(sp):
            sp.dma_start(w_dt[:, :, :], w[:, :, E_DT:E_DT + H]).then_inc(w_in, 16)
            for i, name in enumerate(("e_dt_bias", "e_A_log", "e_D")):
                sp.dma_start(rows[:, i, :], a[name][0].partition_broadcast(P)).then_inc(rows_in, 16)

        @block.tensor
        def _(pe):
            pe.wait_ge(w_in, 16)
            for c in range(TC):
                for f in range(DT):
                    for i, part in enumerate((k.h_lo, k.h_hi)):
                        last = nc.tensor.matmul(dt_ps[:, c * H:(c + 1) * H], part[:, f, c * P:(c + 1) * P], w_dt[:, f, :],
                                                start=(f == 0 and i == 0), stop=(f == DT - 1 and i == 1))
            last.then_inc(dt_done, 1)
            pe.wait_ge(step, 9)
            for i, m in enumerate((k.at["upto"], k.at["after"], k.at["ones"])):
                last = nc.tensor.matmul(sums[:, i, 0:n], m, dt_a, start=True, stop=True)
            last.then_inc(sum_done, 1)

        @block.scalar
        def _(act):
            act.wait_ge(rows_in, 48)
            nc.scalar.activation(k.ssd_d, rows[:, 2, :], ACT.Copy)
            nc.scalar.activation(neg[:, 0:H], rows[:, 1, :], ACT.Exp).then_inc(neg_a, 1)
            act.wait_ge(step, 2)
            nc.scalar.activation(u, mag, ACT.Exp, scale=-1.0).then_inc(exp_done, 1)
            act.wait_ge(step, 3)
            nc.scalar.activation(mag, w1, ACT.Ln).then_inc(log_done, 1)
            act.wait_ge(sum_done, 1)
            for i, out in enumerate((eacs, to_end, total)):
                nc.scalar.activation(out, sums[:, i, 0:n], ACT.Exp)

        @block.vector
        def _(dve):
            def per_head(row):
                return row.unsqueeze(1).to_broadcast([P, TC, H])

            def by_chunk(x):
                return x.rearrange("p (c h) -> p c h", h=H)

            dve.wait_ge(dt_done, 1)
            dve.wait_ge(rows_in, 48)
            nc.vector.tensor_tensor(by_chunk(v), by_chunk(dt_ps[:, :]), per_head(rows[:, 0, :]), ALU.add).then_inc(step, 1)
            dve.wait_ge(step, 1)
            nc.vector.scalar_tensor_tensor(mag, v, -1.0, v, ALU.mult, ALU.max).then_inc(step, 1)
            dve.wait_ge(exp_done, 1)
            nc.vector.tensor_scalar(w1, u, 1.0, None, ALU.add).then_inc(step, 1)
            dve.wait_ge(step, 3)
            nc.vector.tensor_scalar(corr, w1, -1.0, 1e-30, ALU.add, ALU.max).then_inc(step, 1)
            dve.wait_ge(step, 4)
            nc.vector.reciprocal(corr, corr).then_inc(step, 1)
            dve.wait_ge(step, 5)
            nc.vector.tensor_tensor(corr, corr, u, ALU.mult).then_inc(step, 1)
            dve.wait_ge(log_done, 1)
            dve.wait_ge(step, 6)
            nc.vector.tensor_tensor(corr, corr, mag, ALU.mult).then_inc(step, 1)
            nc.vector.scalar_tensor_tensor(u, w1, 1.0, u, ALU.is_equal, ALU.mult).then_inc(log_done, 1)
            dve.wait_ge(step, 7)
            nc.vector.scalar_tensor_tensor(v, v, 0.0, corr, ALU.max, ALU.add).then_inc(step, 1)
            dve.wait_ge(step, 8)
            dve.wait_ge(log_done, 2)
            nc.vector.tensor_tensor(dt, v, u, ALU.add).then_inc(log_done, 1)
            dve.wait_ge(log_done, 3)
            dve.wait_ge(neg_a, 1)
            nc.vector.scalar_tensor_tensor(by_chunk(dt_a), by_chunk(dt), -1.0, per_head(neg[:, 0:H]),
                                           ALU.mult, ALU.mult).then_inc(step, 1)


def ssd_scan(k, raw, z, dt, dt_a, eacs, to_end, total, mixT):
    nc = k.nc
    H, G, R = SSD_HEADS, SSD_G, SSD_HEADS // SSD_G
    N = SSD_HEADS * SSD_P
    with ExitStack() as ctx:
        def sb(name, shape):
            return ctx.enter_context(k.sbuf(name, shape))

        xc = sb("xc", [P, XBC_T, P])
        small = sb("small", [P, 4, H])
        dta_c = sb("dta_c", [P, H])
        x_rows = sb("xs_rows", [P, H, SSD_P])
        b_rows = sb("b_rows", [P, G, P])
        x_dt = sb("x_dt", [P, H, SSD_P])
        x_end = sb("x_end", [P, H, SSD_P])
        steps = sb("steps", [P, H, P])
        weights = sb("weights", [P, H, P])
        cb = sb("cb", [P, G, P])
        state = sb("state", [P, H, SSD_P])
        y = steps[:, N // P:2 * N // P, :].rearrange("p a (b d) -> p (a b) d", d=SSD_P)
        zs = steps[:, 0:N // P, :].rearrange("p h n -> p (h n)")
        stat = sb("stat", [P, 4])
        banks = ctx.enter_context(k.psum("banks", [P, 8, S]))

        def two(b):
            return banks[:, b:b + 2, :].rearrange("p b n -> p (b n)")

        def heads(x):
            return x.rearrange("p (h d) -> p h d", h=H)

        turned_x, turned_b, cb_ps = two(0), banks[:, 2, :], banks[:, 3, :]
        segs = banks[:, 4:8, :].rearrange("p b n -> p (b n)")
        y_diag, new_state, y_off, turned_y = two(4), two(6), two(0), two(0)

        (block, staged, x_turned, x_copied, b_copied, xdt_done, steps_done, seg_done, cb_done, cb_masked, exp_done,
         weighted, xend_done, diag_done, off_done, new_done, y_step, state_step, z_done, sq_done, log_done, rstd_done,
         y_normed, y_turned, chunk_done, state_zero) = ctx.enter_context(stage(nc, (
             "staged x_turned x_copied b_copied xdt_done steps_done seg_done cb_done cb_masked exp_done weighted xend_done "
             "diag_done off_done new_done y_step state_step z_done sq_done log_done rstd_done y_normed y_turned chunk_done "
             "state_zero")))

        def per_head(col):
            return col.unsqueeze(2).to_broadcast([P, H, SSD_P])

        @block.gpsimd
        def _(pool):
            nc.gpsimd.memset(state[:, :, :], 0.0).then_inc(state_zero, 1)
            pool.sem_inc(chunk_done, 1)
            with pool.Fori(0, TC) as c:
                pool.wait_ge(chunk_done, c + 1)
                pool.wait_ge(state_step, c * 2 + 1)
                for i, src in enumerate((dt, eacs, to_end, total)):
                    nc.gpsimd.tensor_copy(small[:, i, :], src[:, bass.ds(c * H, H)]).then_inc(staged, 1)
                nc.gpsimd.tensor_copy(dta_c[:, :], dt_a[:, bass.ds(c * H, H)]).then_inc(staged, 1)
                pool.wait_ge(y_step, c * 4 + 2)
                pool.wait_ge(x_copied, c + 1)
                pool.wait_ge(xend_done, c + 1)
                pool.wait_ge(diag_done, c + 1)
                nc.gpsimd.tensor_tensor(x_dt[:, :, :], x_rows[:, :, :], per_head(k.ssd_d), ALU.mult).then_inc(y_step, 1)
                pool.wait_ge(y_step, c * 4 + 3)
                nc.gpsimd.tensor_tensor(y[:, :, :], y[:, :, :], x_dt[:, :, :], ALU.add).then_inc(y_step, 1)
                pool.wait_ge(y_step, c * 4 + 4)
                pool.wait_ge(z_done, c + 1)
                nc.gpsimd.tensor_tensor(y[:, :, :], y[:, :, :], heads(zs), ALU.mult).then_inc(sq_done, 1)

        @block.scalar
        def _(act):
            with act.Fori(0, TC) as c:
                act.wait_ge(chunk_done, c + 1)
                act.wait_ge(state_step, c * 2 + 1)
                nc.scalar.activation(xc[:, :, :], raw[:, :, bass.ds(c * P + (CONV - 1), P)], ACT.Copy).then_inc(staged, 1)
                act.wait_ge(x_turned, c * 2 + 1)
                nc.scalar.activation(x_rows[:, :, :], heads(turned_x), ACT.Copy).then_inc(x_copied, 1)
                act.wait_ge(x_turned, c * 2 + 2)
                nc.scalar.activation(b_rows[:, :, :], turned_b.rearrange("p (g n) -> p g n", g=G), ACT.Copy).then_inc(b_copied, 1)
                for g in range(G):
                    act.wait_ge(seg_done, c * G + g + 1)
                    nc.scalar.activation(weights[:, g * R:(g + 1) * R, :],
                                         segs[:, g * S:(g + 1) * S].rearrange("p (r n) -> p r n", r=R),
                                         ACT.Exp).then_inc(exp_done, 1)
                nc.scalar.activation(zs, z[:, bass.ds(c, 1), :].rearrange("p a n -> p (a n)"),
                                     ACT.Silu).then_inc(z_done, 1)
                act.wait_ge(sq_done, c * 2 + 1)
                nc.scalar.activation(zs, y[:, :, :].rearrange("p h d -> p (h d)"), ACT.Square,
                                     accum_out=stat[:, 0:1]).then_inc(sq_done, 1)
                act.wait_ge(sq_done, c * 2 + 2)
                inverse_root(k, act, stat[:, 2:3], stat[:, 1:2], stat[:, 0:1], 1.0 / N, log_done, c + 1).then_inc(rstd_done, 1)
                act.wait_ge(rstd_done, c + 1)
                nc.scalar.activation(y[:, :, :], y[:, :, :], ACT.Copy, scale=stat[:, 2:3]).then_inc(y_normed, 1)

        @block.tensor
        def _(pe):
            with pe.Fori(0, TC) as c:
                pe.wait_ge(staged, c * 6 + 6)
                for f in range(DT):
                    last = nc.tensor.transpose(turned_x[:, f * P:(f + 1) * P], xc[:, f, :], k.at["ident"])
                last.then_inc(x_turned, 1)
                for g in range(G):
                    last = nc.tensor.transpose(turned_b[:, g * P:(g + 1) * P], xc[:, DT + g, :], k.at["ident"])
                last.then_inc(x_turned, 1)
                for g in range(G):
                    last = nc.tensor.matmul(cb_ps[:, g * P:(g + 1) * P], xc[:, DT + g, :], xc[:, DT + G + g, :],
                                            start=True, stop=True)
                last.then_inc(cb_done, 1)
                pe.wait_ge(steps_done, c + 1)
                for h in range(H):
                    last = nc.tensor.matmul(segs[:, h * P:(h + 1) * P], steps[:, h, :], k.at["upto"], start=True, stop=True)
                    if h % R == R - 1:
                        last.then_inc(seg_done, 1)
                pe.wait_ge(x_copied, c + 1)
                pe.wait_ge(xdt_done, c + 1)
                pe.wait_ge(state_zero, 1)
                for g in range(G):
                    last = nc.tensor.matmul(y_off[:, g * R * SSD_P:(g + 1) * R * SSD_P], xc[:, DT + G + g, :],
                                            state[:, g * R:(g + 1) * R, :], start=True, stop=True)
                last.then_inc(off_done, 1)
                pe.wait_ge(xend_done, c + 1)
                pe.wait_ge(b_copied, c + 1)
                pe.wait_ge(exp_done, c * G + G)
                for g in range(G):
                    last = nc.tensor.matmul(new_state[:, g * R * SSD_P:(g + 1) * R * SSD_P], b_rows[:, g, :],
                                            x_end[:, g * R:(g + 1) * R, :], start=True, stop=True)
                last.then_inc(new_done, 1)
                pe.wait_ge(weighted, c * G + G)
                for h in range(H):
                    last = nc.tensor.matmul(y_diag[:, h * SSD_P:(h + 1) * SSD_P], weights[:, h, :], x_dt[:, h, :],
                                            start=True, stop=True)
                last.then_inc(diag_done, 1)
                pe.wait_ge(y_normed, c + 1)
                for f in range(DT):
                    last = nc.tensor.transpose(turned_y[:, f * P:(f + 1) * P],
                                               y[:, 2 * f:2 * f + 2, :].rearrange("p h d -> p (h d)"), k.at["ident"])
                last.then_inc(y_turned, 1)

        @block.vector
        def _(dve):
            dve.sem_inc(state_step, 1)
            with dve.Fori(0, TC) as c:
                dve.wait_ge(staged, c * 6 + 6)
                nc.vector.tensor_tensor(steps[:, :, :], k.at["after"].unsqueeze(1).to_broadcast([P, H, P]),
                                        dta_c[:, :].unsqueeze(2).to_broadcast([P, H, P]), ALU.mult).then_inc(steps_done, 1)
                dve.wait_ge(x_turned, c * 2 + 1)
                dve.wait_ge(x_copied, c + 1)
                nc.vector.tensor_tensor(x_dt[:, :, :], x_rows[:, :, :], per_head(small[:, 0, :]), ALU.mult).then_inc(xdt_done, 1)
                dve.wait_ge(xdt_done, c + 1)
                nc.vector.tensor_tensor(x_end[:, :, :], x_dt[:, :, :], per_head(small[:, 2, :]), ALU.mult).then_inc(xend_done, 1)
                dve.wait_ge(cb_done, c + 1)
                nc.vector.tensor_tensor(cb[:, :, :], cb_ps.rearrange("p (g n) -> p g n", g=G),
                                        k.at["upto"].unsqueeze(1).to_broadcast([P, G, P]), ALU.mult).then_inc(cb_masked, 1)
                dve.wait_ge(cb_masked, c + 1)
                for g in range(G):
                    dve.wait_ge(exp_done, c * G + g + 1)
                    w = weights[:, g * R:(g + 1) * R, :]
                    nc.vector.tensor_tensor(w, w, cb[:, g, :].unsqueeze(1).to_broadcast([P, R, P]), ALU.mult).then_inc(weighted, 1)
                dve.wait_ge(off_done, c + 1)
                nc.vector.tensor_tensor(y[:, :, :], heads(y_off), per_head(small[:, 1, :]), ALU.mult).then_inc(y_step, 1)
                nc.vector.tensor_tensor(state[:, :, :], state[:, :, :], per_head(small[:, 3, :]), ALU.mult).then_inc(state_step, 1)
                dve.wait_ge(new_done, c + 1)
                dve.wait_ge(state_step, c * 2 + 2)
                nc.vector.tensor_tensor(state[:, :, :], heads(new_state), state[:, :, :], ALU.add).then_inc(state_step, 1)
                dve.wait_ge(diag_done, c + 1)
                dve.wait_ge(y_step, c * 4 + 1)
                nc.vector.tensor_tensor(y[:, :, :], heads(y_diag), y[:, :, :], ALU.add).then_inc(y_step, 1)
                dve.wait_ge(y_turned, c + 1)
                nc.vector.tensor_tensor(mixT[:, 0:DT, bass.ds(c * P, P)], turned_y.rearrange("p (f n) -> p f n", f=DT),
                                        k.vec[:, P + 112:P + 120].unsqueeze(2).to_broadcast([P, DT, P]),
                                        ALU.mult).then_inc(chunk_done, 1)


def even_ssd(k, a, mixT):
    nc = k.nc
    w = a["e_w_in"][0]
    with (
        k.sbuf("z_rows", [P, TC, D]) as z,
        k.sbuf("xbc", [P, XBC_T, CONV - 1 + S]) as raw,
        k.sbuf("decays", [P, 5, TC * SSD_HEADS]) as decays,
    ):
        dt, dt_a, eacs, to_end, total = (decays[:, i, :] for i in range(5))
        project(k, [run(2, weight_tiles(w, E_Z), lambda e, t, j, ps: copy_out(nc, e, z[:, j, bass.ds(t * COLS, COLS)], ps), rows=True),
                    run(4, weight_tiles(w, E_XBC), lambda e, t, j, ps: copy_out(
                        nc, e, raw[:, bass.ds(4 * t + j, 1), CONV - 1:].rearrange("p a n -> p (a n)"), ps))])
        ssd_steps(k, a, dt, dt_a, eacs, to_end, total)
        conv_silu(k, raw, XBC_T, CONV, S, lambda t, j: k.vec[:, bass.ds(t + (64 + 16 * j), 1)],
                  lambda t: k.vec[:, bass.ds(t + (P + 96), 1)])
        ssd_scan(k, raw, z, dt, dt_a, eacs, to_end, total, mixT)



REL_BUCKETS, REL_MAX_DIST = 32, 128
HEADS = 8
BAND = 2 * P
LAM_INIT = 0.8 - 0.6 * float(np.exp(-0.3 * 0))


def bucket_of(dist):
    dist = np.maximum(dist, 0)
    exact = REL_BUCKETS // 2
    logd = np.log(np.maximum(dist, 1).astype(np.float32) / np.float32(exact))
    large = exact + (logd / np.float32(np.log(REL_MAX_DIST / exact)) * np.float32(REL_BUCKETS - exact)).astype(np.int32)
    return np.where(dist < exact, dist, np.minimum(large, REL_BUCKETS - 1))


def relative_bias(k, a):
    nc = k.nc
    n = 3 * P
    rows = nc.dram_tensor("bias_rows", [HEADS, n], F32)
    with (
        k.sbuf("bias_in", [REL_BUCKETS, HEADS + n]) as bias_in,
        k.sbuf("bias_sb", [HEADS, n]) as bias_sb,
        k.sbuf("flipped", [P, HEADS, BAND]) as flipped,
        k.psum("bias_ps", [P, 5, S]) as ps,
        stage(nc, "tab_in far_in list_done list_out list_kept band_in turned") as
        (block, tab_in, far_in, list_done, list_out, list_kept, band_in, turned),
    ):
        @block.sync
        def _(sp):
            sp.dma_start(bias_in[:, 0:HEADS], a["rel_bias"]).then_inc(tab_in, 16)
            sp.dma_start(bias_in[:, HEADS:], a["one_hot"]).then_inc(tab_in, 16)
            sp.dma_start(k.far, a["rel_bias"][REL_BUCKETS - 1].partition_broadcast(P)).then_inc(far_in, 16)
            sp.wait_ge(list_out, 1)
            sp.dma_start(rows.ap(), bias_sb[:, :]).then_inc(list_kept, 16)
            sp.wait_ge(list_kept, 16)
            sp.dma_start(flipped[:, :, :], bass.AP(rows, 0, [[1, P], [n, HEADS], [1, BAND]])).then_inc(band_in, 16)
            sp.wait_ge(far_in, 16)

        @block.tensor
        def _(pe):
            pe.wait_ge(tab_in, 32)
            nc.tensor.matmul(ps[0:HEADS, 4, 0:n], bias_in[:, 0:HEADS], bias_in[:, HEADS:], start=True, stop=True).then_inc(list_done, 1)
            pe.wait_ge(band_in, 16)
            for i in range(4):
                nc.tensor.matmul(ps[:, i, :], k.at["flip"], flipped[:, 2 * i:2 * i + 2, :], start=True, stop=True).then_inc(turned, 1)

        @block.vector
        def _(dve):
            dve.wait_ge(list_done, 1)
            nc.vector.tensor_copy(bias_sb[:, :], ps[0:HEADS, 4, 0:n]).then_inc(list_out, 1)
            for i in range(4):
                dve.wait_ge(turned, i + 1)
                nc.vector.tensor_copy(k.band[:, 2 * i:2 * i + 2, :], ps[:, i, :].rearrange("p (h n) -> p h n", h=2))


def lambda_stage(k, a, neg_lam, out_gain):
    nc = k.nc
    d = 64
    with (
        k.sbuf("lam", [P, 4, d]) as lam,
        k.sbuf("lam_tmp", [P, d]) as tmp,
        k.sbuf("dots", [P, 4]) as dots,
        stage(nc, "lam_in dot_done exp_done neg_done") as (block, lam_in, dot_done, exp_done, neg_done),
    ):
        @block.sync
        def _(sp):
            sp.dma_start(lam[:, :, :], a["e_lambda"][0].partition_broadcast(P)).then_inc(lam_in, 16)

        @block.vector
        def _(dve):
            dve.wait_ge(lam_in, 16)
            for i in range(2):
                if i:
                    dve.wait_ge(dot_done, i)
                nc.vector.tensor_tensor_reduce(tmp[:, :], lam[:, 2 * i, :], lam[:, 2 * i + 1, :], 1.0, 0.0, ALU.mult, ALU.add,
                                               dots[:, i:i + 1]).then_inc(dot_done, 1)
            nc.vector.tensor_scalar(out_gain, k.vec[:, 2 * P:2 * P + 1], 1.0 - LAM_INIT, None, ALU.mult)
            dve.wait_ge(exp_done, 1)
            nc.vector.scalar_tensor_tensor(neg_lam, dots[:, 2:3], -1.0, dots[:, 3:4], ALU.mult, ALU.add).then_inc(neg_done, 1)
            dve.wait_ge(neg_done, 1)
            nc.vector.tensor_scalar(neg_lam, neg_lam, -LAM_INIT, None, ALU.add)

        @block.scalar
        def _(act):
            act.wait_ge(dot_done, 2)
            nc.scalar.activation(dots[:, 2:4], dots[:, 0:2], ACT.Exp).then_inc(exp_done, 1)


def diff_attention(k, qT, kT, v_rows, neg_lam, out_gain, mixT, mix_at):
    nc = k.nc
    UNITS = 2 * TC
    with ExitStack() as ctx:
        def sb(name, shape):
            return ctx.enter_context(k.sbuf(name, shape))

        q_pair, k_pair, v_pair = sb("q_pair", [P, 2, S]), sb("k_pair", [P, 2, S]), sb("v_pair", [P, TC, 2 * P])
        bias = sb("bias", [P, 2, S])
        probs = sb("probs", [P, DEEP, 2, S])
        attn_t = sb("attn_t", [P, 2, S])
        neg_max, sums, weight = (sb(name, [P, DEEP, 2]) for name in ("neg_max", "sums", "weight"))
        sq, log_ms, rstd = sb("sq", [P, S]), sb("log_ms", [P, S]), sb("rstd", [P, S])
        banks = ctx.enter_context(k.psum("banks", [P, 8, S]))
        logits = banks[:, 0:4, :].rearrange("p (u m) n -> p u m n", m=2)
        turned, out_ps, stat = banks[:, 4, :], banks[:, 5:7, :], banks[:, 7, :]
        (block, admitted, staged, logit_done, shifted, exp_done, recip_done, lam_done, scaled, mixed, turn_done, turn_out, pv_done,
         sq_done, stat_done, log_done, rstd_done, head_done) = ctx.enter_context(stage(nc, (
             "admitted staged logit_done shifted exp_done recip_done lam_done scaled mixed turn_done turn_out pv_done sq_done "
             "stat_done log_done rstd_done head_done")))

        def unit(n):
            u, qb = divmod(n, TC)
            return u, qb, (qb + 1) * P, S - (qb + 1) * P

        @block.gpsimd
        def _(pool):
            with pool.Fori(0, HEADS // 2) as i:
                pool.wait_ge(logit_done, i * UNITS + 1)
                nc.gpsimd.tensor_copy(q_pair[:, :, :], qT[:, bass.ds(i * 2, 2), :]).then_inc(staged, 1)
                nc.gpsimd.tensor_copy(k_pair[:, :, :], kT[:, bass.ds(i * 2, 2), :]).then_inc(staged, 1)
                pool.wait_ge(shifted, i * (2 * UNITS) + 1)
                nc.gpsimd.tensor_copy(bias[:, :, BAND:S], k.band[:, bass.ds(i * 2, 2), :]).then_inc(staged, 1)
                nc.gpsimd.tensor_copy(bias[:, :, 0:BAND], k.far[:, bass.ds(i * 2, 2)].unsqueeze(2).to_broadcast([P, 2, BAND])
                                      ).then_inc(staged, 1)
                pool.wait_ge(staged, i * 6 + 3)
                nc.gpsimd.tensor_tensor(bias[:, :, S - P:S], bias[:, :, S - P:S],
                                        k.at["causal"].unsqueeze(1).to_broadcast([P, 2, P]), ALU.add).then_inc(staged, 1)
                pool.wait_ge(pv_done, i * UNITS + 1)
                nc.gpsimd.tensor_copy(v_pair[:, :, :], v_rows[:, :, bass.ds(i * (2 * P), 2 * P)]).then_inc(staged, 1)

        @block.tensor
        def _(pe):
            pe.sem_inc(stat_done, 1)
            pe.sem_inc(turn_done, 1)
            pe.sem_inc(pv_done, 1)
            pe.sem_inc(logit_done, 1)
            with pe.Fori(0, HEADS // 2) as i:
                def score(n):
                    u, qb, keys, _ = unit(n)
                    if n >= 2:
                        pe.wait_ge(shifted, i * (2 * UNITS) + 2 * n - 1)
                    for m in range(2):
                        at = slice(64 * m, 64 * m + 64)
                        last = nc.tensor.matmul(logits[:, n % 2, m, 0:keys], q_pair[at, u, qb * P:(qb + 1) * P],
                                                k_pair[at, u, 0:keys], start=True, stop=True)
                    last.then_inc(logit_done, 1)

                def norm(u):
                    pe.wait_ge(sq_done, i * 2 + u + 1)
                    nc.tensor.matmul(stat, k.at["ones"], sq[:, :], start=True, stop=True).then_inc(stat_done, 1)

                pe.wait_ge(staged, i * 6 + 2)
                pe.wait_ge(shifted, i * (2 * UNITS) + 1)
                score(0)
                score(1)
                for n in range(UNITS + 1):
                    if n + 2 < UNITS:
                        score(n + 2)
                    if n < UNITS:
                        _, qb, _, _ = unit(n)
                        pe.wait_ge(mixed, i * UNITS + n + 1)
                        pe.wait_ge(turn_out, i * UNITS + n + 1)
                        for b in range(qb + 1):
                            last = nc.tensor.transpose(turned[:, b * P:(b + 1) * P], probs[:, n % DEEP, 0, b * P:(b + 1) * P], k.at["ident"])
                        last.then_inc(turn_done, 1)
                    if n >= 1:
                        if n == TC + 1:
                            norm(0)
                        m = n - 1
                        u, qb, _, _ = unit(m)
                        pe.wait_ge(turn_out, i * UNITS + m + 2)
                        pe.wait_ge(staged, i * 6 + 6)
                        if qb == 0:
                            pe.wait_ge(head_done, i * 2 + u + 1)
                        for b in range(qb + 1):
                            last = nc.tensor.matmul(out_ps[:, u, qb * P:(qb + 1) * P], v_pair[:, b, u * P:(u + 1) * P],
                                                    attn_t[:, m % 2, b * P:(b + 1) * P], start=(b == 0), stop=(b == qb))
                        last.then_inc(pv_done, 1)
                norm(1)

        @block.vector
        def _(dve):
            dve.sem_inc(head_done, 2)
            dve.sem_inc(shifted, 1)
            with dve.Fori(0, HEADS // 2) as i:
                def shift(n):
                    u, qb, keys, at = unit(n)
                    dve.wait_ge(logit_done, i * UNITS + n + 2)
                    dve.wait_ge(staged, i * 6 + 5)
                    dve.wait_ge(turn_done, i * UNITS + max(n - 2, 1))
                    dve.sem_inc(admitted, 1)
                    for m in range(2):
                        nc.vector.tensor_tensor_reduce(probs[:, n % DEEP, m, 0:keys], logits[:, n % 2, m, 0:keys], bias[:, u, at:S],
                                                       -1.0, 3e38, ALU.add, ALU.min, neg_max[:, n % DEEP, m:m + 1]).then_inc(shifted, 1)

                def leave(u):
                    dve.wait_ge(rstd_done, i * 2 + u + 1)
                    nc.vector.scalar_tensor_tensor(mixT[:, bass.ds(i * 2 + (mix_at + u), 1), :].rearrange("p a n -> p (a n)"), out_ps[:, u, :],
                                                   out_gain, rstd[:, :], ALU.mult, ALU.mult).then_inc(head_done, 1)

                shift(0)
                shift(1)
                for n in range(UNITS):
                    u, qb, keys, _ = unit(n)
                    p = n % DEEP
                    dve.wait_ge(exp_done, i * (2 * UNITS) + 2 * n + 2)
                    nc.vector.reciprocal(weight[:, p, :], sums[:, p, :]).then_inc(recip_done, 1)
                    dve.wait_ge(recip_done, i * UNITS + n + 1)
                    nc.vector.tensor_scalar(weight[:, p, 1:2], weight[:, p, 1:2], neg_lam, None, ALU.mult).then_inc(lam_done, 1)
                    dve.wait_ge(lam_done, i * UNITS + n + 1)
                    nc.vector.tensor_scalar(probs[:, p, 1, 0:keys], probs[:, p, 1, 0:keys], weight[:, p, 1:2], None,
                                            ALU.mult).then_inc(scaled, 1)
                    dve.wait_ge(scaled, i * UNITS + n + 1)
                    nc.vector.scalar_tensor_tensor(probs[:, p, 0, 0:keys], probs[:, p, 0, 0:keys], weight[:, p, 0:1],
                                                   probs[:, p, 1, 0:keys], ALU.mult, ALU.add).then_inc(mixed, 1)
                    if n + 2 < UNITS:
                        shift(n + 2)
                    if n == TC + 2:
                        leave(0)
                leave(1)

        @block.scalar
        def _(act):
            act.sem_inc(turn_out, 1)
            with act.Fori(0, HEADS // 2) as i:
                def exps(n):
                    u, qb, keys, _ = unit(n)
                    p = n % DEEP
                    for m in range(2):
                        act.wait_ge(shifted, i * (2 * UNITS) + 2 * n + m + 2)
                        nc.scalar.activation(probs[:, p, m, 0:keys], probs[:, p, m, 0:keys], ACT.Exp, scale=-1.0,
                                             bias=neg_max[:, p, m:m + 1], accum_out=sums[:, p, m:m + 1]).then_inc(exp_done, 1)

                def square(u):
                    act.wait_ge(pv_done, i * UNITS + (u + 1) * TC + 1)
                    act.wait_ge(stat_done, i * 2 + u + 1)
                    nc.scalar.activation(sq[:, :], out_ps[:, u, :], ACT.Square).then_inc(sq_done, 1)

                def root(u):
                    act.wait_ge(stat_done, i * 2 + u + 2)
                    act.wait_ge(head_done, i * 2 + u + 2)
                    inverse_root(k, act, rstd[:, :], log_ms[:, :], stat, 1.0 / P, log_done, i * 2 + u + 1).then_inc(rstd_done, 1)

                exps(0)
                for n in range(UNITS):
                    u, qb, keys, _ = unit(n)
                    if n + 1 < UNITS:
                        exps(n + 1)
                    act.wait_ge(turn_done, i * UNITS + n + 2)
                    act.wait_ge(pv_done, i * UNITS + max(n, 1))
                    nc.scalar.activation(attn_t[:, n % 2, 0:keys], turned[:, 0:keys], ACT.Copy).then_inc(turn_out, 1)
                    if n == TC + 1:
                        square(0)
                    if n == TC + 2:
                        root(0)
                square(1)
                root(1)


def even_diff(k, a, mixT):
    nc = k.nc
    w = a["e_w_in"][0]
    with (
        k.sbuf("qT", [P, HEADS, S]) as qT, k.sbuf("kT", [P, HEADS, S]) as kT, k.sbuf("v_rows", [P, TC, D]) as v_rows,
        k.sbuf("lam_cols", [P, 2]) as lam_cols,
    ):
        neg_lam, out_gain = lam_cols[:, 0:1], lam_cols[:, 1:2]

        def to(dst, scale=None):
            return lambda e, t, j, ps: copy_out(nc, e, dst[:, bass.ds(4 * t + j, 1), :].rearrange("p a n -> p (a n)"), ps, scale)

        project(k, [run(2, weight_tiles(w, E_Q), to(qT, 64 ** -0.5)), run(2, weight_tiles(w, E_K), to(kT)),
                    run(2, weight_tiles(w, E_V), lambda e, t, j, ps: copy_out(nc, e, v_rows[:, j, bass.ds(t * COLS, COLS)], ps), rows=True)])
        lambda_stage(k, a, neg_lam, out_gain)
        diff_attention(k, qT, kT, v_rows, neg_lam, out_gain, mixT, DT)



def down_project(k, w, moving, per, post=None, gate=None):
    nc = k.nc
    n_tiles = w.shape[0] // (P * per)
    v = w.rearrange("(t c p) n -> t p c n", c=per, p=P)
    moving_hi, moving_lo = (h[:, :, :].rearrange("p (u c) n -> p u c n", u=2) for h in (k.h_hi, k.h_lo))

    def moving_of(t):
        return moving[:, bass.ds(t * per, per), :]

    def columns(j):
        return slice(j * 2 * P, (j + 1) * 2 * P)

    with (
        k.sbuf("ring", [P, SLOTS, per, D]) as slot, k.sbuf("w_hi", [P, per, D]) as w_hi, k.sbuf("w_lo", [P, per, D]) as w_lo,
        k.sbuf("y0", [P, S]) as y0, k.sbuf("log_ms", [P, S]) as log_ms, k.sbuf("rstd", [P, S]) as rstd,
        k.psum("y", [P, DT, S]) as y,
        stage(nc, "zeroed first0 first1 first2 first3 landed0 landed1 hi_done lo_done bank_done y0_kept squared stat_done log_done rstd_done scaled gate_done") as
        (block, zeroed, *first, landed0, landed1, hi_done, lo_done, bank_done, y0_kept, squared, stat_done, log_done, rstd_done, scaled, gate_done),
    ):
        landed = (landed0, landed1)
        done = 8 * (n_tiles - 1) + 16
        built = slot[:, :, :, :].rearrange("p u c n -> p (u c n)")[:, 0:DT * S].rearrange("p (f n) -> p f n", f=DT)

        @block.sync
        def _(sp):
            def load(i, u, end):
                sp.wait_ge(lo_done, (2 * i + u) * 5 + 5)
                src = v[bass.ds(2 * i + u, 1)].rearrange("a p c n -> p (a c) n")
                if isinstance(i, int) and i == u == 0:
                    for j in range(4):
                        sp.dma_start(slot[:, 0, :, columns(j)], src[:, :, columns(j)]).then_inc(first[j], 16)
                else:
                    sp.dma_start(slot[:, u, :, :], src).then_inc(landed[u], 16)
            pairs(sp, n_tiles, load)

        @block.tensor
        def _(pe):
            pe.sem_inc(bank_done, 16)
            pe.wait_ge(zeroed, 1)

            def multiply(i, u, end):
                for f in range(DT):
                    pe.wait_ge(lo_done, (2 * i + u) * 5 + (f // 2 + 12))
                    for c in range(per):
                        last = three_products(nc, y[:, f, :], (w_hi[:, c, f * P:(f + 1) * P], w_lo[:, c, f * P:(f + 1) * P]),
                                              (moving_hi[:, u, c, :], moving_lo[:, u, c, :]),
                                              False, False, skip_group_check=True)
                    if f < DT - 1:
                        last.then_inc(bank_done, 1)
                last.then_inc(bank_done, 1)
            pairs(pe, n_tiles, multiply)
            if post is not None:
                pe.wait_ge(y0_kept, 1)
                for f in range(DT):
                    pe.wait_ge(squared, f + 1)
                    last = nc.tensor.matmul(y[:, 0, :], k.at["ones"], built[:, f, :], start=(f == 0), stop=(f == DT - 1))
                last.then_inc(stat_done, 1)

        @block.vector
        def _(dve):
            nc.vector.memset(y[:, :, :], 0.0).then_inc(zeroed, 1)

            dve.sem_inc(lo_done, 10)

            def split(i, u, end):
                t = 2 * i + u
                dve.wait_ge(hi_done, t * 5 + 1)
                keep_lo(nc, moving_lo[:, u, 0:per, :], moving_of(t), moving_hi[:, u, 0:per, :]).then_inc(lo_done, 1)
                for j in range(4):
                    dve.wait_ge(hi_done, t * 5 + (j + 2))
                    keep_lo(nc, w_lo[:, :, columns(j)], slot[:, u, :, columns(j)], w_hi[:, :, columns(j)]).then_inc(lo_done, 1)
            pairs(dve, n_tiles, split)
            if post is None:
                for f in range(DT):
                    dve.wait_ge(bank_done, done + f + 1)
                    nc.vector.tensor_tensor(k.xT[:, f, :], y[:, f, :], k.xT[:, f, :], ALU.add)
            else:
                dve.wait_ge(bank_done, done + 1)
                nc.vector.tensor_copy(y0[:, :], y[:, 0, :]).then_inc(y0_kept, 1)
                dve.wait_ge(rstd_done, 1)
                dve.wait_ge(y0_kept, 1)
                for f in range(DT):
                    nc.vector.scalar_tensor_tensor(built[:, f, :], y0[:, :] if f == 0 else y[:, f, :], post(f), rstd[:, :],
                                                   ALU.mult, ALU.mult).then_inc(scaled, 1)
                for f in range(DT // 2, DT) if gate is not None else ():
                    dve.wait_ge(scaled, f + 1)
                    nc.vector.tensor_tensor(built[:, f, :], built[:, f, :], gate[:, f, :], ALU.mult).then_inc(scaled, 1)
                for f in range(DT // 2, DT):
                    dve.wait_ge(scaled, f + 1 + (DT // 2 if gate is not None else 0))
                    nc.vector.tensor_tensor(k.xT[:, f, :], k.xT[:, f, :], built[:, f, :], ALU.add)

        @block.scalar
        def _(act):
            def keep(i, u, end):
                t = 2 * i + u
                act.wait_ge(bank_done, t * 8 + 8)
                keep_hi(nc, moving_hi[:, u, 0:per, :], moving_of(t)).then_inc(hi_done, 1)
                if isinstance(i, int) and i == u == 0:
                    for j in range(4):
                        act.wait_ge(first[j], 16)
                        keep_hi(nc, w_hi[:, :, columns(j)], slot[:, 0, :, columns(j)]).then_inc(hi_done, 1)
                    return
                act.wait_ge(landed[u], i * 16 + 16 * u)
                for j in range(4):
                    act.wait_ge(bank_done, t * 8 + (2 * j + 10))
                    keep_hi(nc, w_hi[:, :, columns(j)], slot[:, u, :, columns(j)]).then_inc(hi_done, 1)
            pairs(act, n_tiles, keep)
            if post is not None:
                for f in range(DT):
                    act.wait_ge(bank_done, done + f + 1)
                    if f == 0:
                        act.wait_ge(y0_kept, 1)
                    nc.scalar.activation(built[:, f, :], y0[:, :] if f == 0 else y[:, f, :], ACT.Square).then_inc(squared, 1)
                act.wait_ge(stat_done, 1)
                inverse_root(k, act, rstd[:, :], log_ms[:, :], y[:, 0, :], 1.0 / D, log_done).then_inc(rstd_done, 1)

        @block.gpsimd
        def _(pool):
            for f in range(DT // 2 if post is not None else 0):
                pool.wait_ge(scaled, f + 1)
                if gate is not None:
                    nc.gpsimd.tensor_tensor(built[:, f, :], built[:, f, :], gate[:, f, :], ALU.mult).then_inc(gate_done, 1)
                    pool.wait_ge(gate_done, f + 1)
                nc.gpsimd.tensor_tensor(k.xT[:, f, :], k.xT[:, f, :], built[:, f, :], ALU.add)


def squared_relu_mlp(k, a, layer, sub):
    nc = k.nc
    F = 4 * D // P
    with k.sbuf("hidden", [P, F, S]) as hidden:
        def tile(t, j):
            return hidden[:, bass.ds(4 * t + j, 1), :].rearrange("p a n -> p (a n)")

        def relu(e, t, j, ps):
            if e == "act":
                return nc.scalar.activation(tile(t, j), ps, ACT.Relu)
            return nc.vector.tensor_scalar(tile(t, j), ps, 0.0, None, ALU.max)

        project(k, [run(8, weight_tiles(a["mlp_w1"][layer], 0), relu,
                        after=lambda t, j: nc.gpsimd.tensor_tensor(tile(t, j), tile(t, j), tile(t, j), ALU.mult))])
        down_project(k, a["mlp_w2"][layer], hidden, 4, post=lambda f: k.post_gain[:, sub, f:f + 1])


def pre_norm(k, sub):
    norm_into(k, lambda f: k.pre_gain[:, sub, f:f + 1], lambda f: k.mod[:, sub * 24 + f:sub * 24 + f + 1])



def project_items(k, w, loads):
    nc = k.nc
    v = w.rearrange("(k p) n -> p k n", p=P)
    items = [(n, *item, None)[:6] for n, (_, its) in enumerate(loads) for item in its]
    widths = [sum(width for _, width in ranges) for ranges, _ in loads]
    n_parts = [-(-width // P) for width in widths]
    parts_before = [sum(n_parts[:n]) for n in range(len(loads))]
    with (
        k.sbuf("ring", [P, SLOTS, DT, COLS]) as ring, k.sbuf("w_hi", [P, DT, COLS]) as w_hi, k.sbuf("w_lo", [P, DT, COLS]) as w_lo,
        k.psum("item_out", [P, 8, S]) as out,
        stage(nc, "first0 first1 first2 first3 landed0 landed1 hi_done lo_done item_done act_freed dve_freed") as
        (block, *first, landed0, landed1, hi_done, lo_done, item_done, act_freed, dve_freed),
    ):
        landed = (landed0, landed1)
        def arrived(n):
            return 16 * sum(len(ranges) for ranges, _ in loads[n % 2 or 2:n + 1:2])

        def view(m):
            _, kind, _, width, _, chunks = items[m]
            if kind == "rows":
                return out[:, m % 8, 0:len(chunks) * width].rearrange("p (c n) -> p c n", c=len(chunks))
            return out[:, m % 8, :]

        def columns(n, j):
            return slice(j * P, min(j * P + P, widths[n]))

        def last_user(n, j):
            return max(m for m, (of, _, at, *_) in enumerate(items) if of == n and at < j * P + P)

        def each_item(empty, split):
            for j in range(n_parts[0]):
                split(0, j)
            for n in range(len(loads)):
                free = range(n_parts[n + 1]) if n + 1 < len(loads) else ()
                for m in range(len(items)):
                    if items[m][0] == n:
                        empty(m)
                        for j in free:
                            if last_user(n, j) == m:
                                split(n + 1, j)

        @block.sync
        def _(sp):
            for n, (ranges, _) in enumerate(loads):
                if n >= 2:
                    sp.wait_ge(lo_done, parts_before[n - 1])
                at = 0
                for j in range(n_parts[0]) if n == 0 else ():
                    sp.dma_start(ring[:, 0, :, columns(0, j)], v[:, :, bass.ds(ranges[0][0] + j * P, P)]).then_inc(first[j], 16)
                for col, width in ranges if n else ():
                    sp.dma_start(ring[:, n % 2, :, at:at + width], v[:, :, bass.ds(col, width)]).then_inc(landed[n % 2], 16)
                    at += width

        @block.tensor
        def _(pe):
            for m, (n, kind, at, width, _, chunks) in enumerate(items):
                pe.wait_ge(lo_done, parts_before[n] + -(-(at + width) // P))
                if m >= 8:
                    pe.wait_ge((act_freed, dve_freed)[m % 2], (m - 8) // 2 + 1)
                hi, lo = (part[:, :, at:at + width] for part in (w_hi, w_lo))
                if kind == "rows":
                    for i, c in enumerate(chunks):
                        tokens = slice(c * P, c * P + P)
                        for f in range(DT):
                            last = three_products(nc, view(m)[:, i, :], (k.h_hi[:, f, tokens], k.h_lo[:, f, tokens]),
                                                  (hi[:, f, :], lo[:, f, :]), f == 0, f == DT - 1)
                else:
                    for f in range(DT):
                        last = three_products(nc, view(m), (hi[:, f, :], lo[:, f, :]), (k.h_hi[:, f, :], k.h_lo[:, f, :]), f == 0, f == DT - 1)
                last.then_inc(item_done, 1)

        @block.scalar
        def _(act):
            def empty(m):
                if m % 2 == 0:
                    act.wait_ge(item_done, m + 1)
                    items[m][4]("act", view(m)).then_inc(act_freed, 1)

            def keep(n, j):
                if n == 0:
                    act.wait_ge(first[j], 16)
                else:
                    act.wait_ge(landed[n % 2], arrived(n))
                    act.wait_ge(item_done, last_user(n - 1, j) + 1)
                keep_hi(nc, w_hi[:, :, columns(n, j)], ring[:, n % 2, :, columns(n, j)]).then_inc(hi_done, 1)
            each_item(empty, keep)

        @block.vector
        def _(dve):
            def empty(m):
                if m % 2 == 1:
                    dve.wait_ge(item_done, m + 1)
                    items[m][4]("dve", view(m)).then_inc(dve_freed, 1)

            def split(n, j):
                dve.wait_ge(hi_done, parts_before[n] + j + 1)
                keep_lo(nc, w_lo[:, :, columns(n, j)], ring[:, n % 2, :, columns(n, j)], w_hi[:, :, columns(n, j)]).then_inc(lo_done, 1)
            each_item(empty, split)


def rotate(k, tiles, swap, cos, sin):
    nc = k.nc
    n = len(tiles)
    with (
        k.sbuf("crossed", [P, 2, S]) as crossed,
        k.psum("swapped", [P, 2, S]) as swapped,
        stage(nc, "swap_done cross_done cos_done added") as (block, swap_done, cross_done, cos_done, added),
    ):
        @block.tensor
        def _(pe):
            for j in range(n):
                if j >= 2:
                    pe.wait_ge(cross_done, j - 1)
                nc.tensor.matmul(swapped[:, j % 2, :], swap, tiles[j], start=True, stop=True).then_inc(swap_done, 1)

        @block.gpsimd
        def _(pool):
            for j in range(n):
                pool.wait_ge(swap_done, j + 1)
                nc.gpsimd.tensor_tensor(tiles[j], tiles[j], cos, ALU.mult).then_inc(cos_done, 1)

        @block.vector
        def _(dve):
            for j in range(n):
                dve.wait_ge(swap_done, j + 1)
                if j >= 2:
                    dve.wait_ge(added, j - 1)
                nc.vector.tensor_tensor(crossed[:, j % 2, :], swapped[:, j % 2, :], sin, ALU.mult).then_inc(cross_done, 1)
                dve.wait_ge(cross_done, j + 1)
                dve.wait_ge(cos_done, j + 1)
                nc.vector.tensor_tensor(tiles[j], tiles[j], crossed[:, j % 2, :], ALU.add).then_inc(added, 1)



RET_H, RET_QK, RET_V = 4, 128, 256
O_RQ, O_RV, O_RG, O_SQ, O_SK = 0, 1024, 2048, 3072, 3584


def retention_constants():
    half = RET_QK // 2
    inv = np.float32(10000.0) ** (-np.arange(half, dtype=np.float32) / half)
    ang = np.arange(S, dtype=np.float32)[None, :] * inv[:, None]
    log_gamma = np.log(1.0 - 2.0 ** (-5.0 - np.arange(RET_H)))
    i = np.arange(P)
    rel = i[None, :] - i[:, None]
    decay = [np.where(rel >= 0, np.exp(np.maximum(rel, 0) * g), 0.0) for g in log_gamma]
    xi = [np.broadcast_to(np.exp((i + 1.0) * g), (P, P)) for g in log_gamma]
    zeta = [np.exp((P - 1 - i) * g)[:, None] for g in log_gamma]
    table = np.concatenate([np.concatenate([np.cos(ang)] * 2), np.concatenate([-np.sin(ang), np.sin(ang)])]
                           + [np.concatenate(x, axis=1) for x in (decay, xi, zeta)], axis=1)
    return table.astype(np.float32), [float(np.exp(P * g)) for g in log_gamma]


def retention(k, qkT, v_rows, table, gammas, outT):
    nc = k.nc
    H = RET_H
    decay = table[:, 2 * S:2 * S + H * P].rearrange("p (h n) -> p h n", h=H)
    xi = table[:, 2 * S + H * P:2 * S + 2 * H * P].rearrange("p (h n) -> p h n", h=H)
    zeta = table[:, 2 * S + 2 * H * P:2 * S + 2 * H * P + H]
    with ExitStack() as ctx:
        def sb(name, shape):
            return ctx.enter_context(k.sbuf(name, shape))

        qk_c = sb("qk_c", [P, 2 * H, P])
        v_c = sb("v_c", [P, H, RET_V])
        q_xi = sb("q_xi", [P, H, P])
        scores = sb("scores", [P, H, P])
        k_zeta = sb("k_zeta", [P, H, P])
        state = sb("ret_state", [P, H, RET_V])
        banks = ctx.enter_context(k.psum("banks", [P, 6, S]))
        score_ps, turned = banks[:, 0, :], banks[:, 1, :]
        out_ps = banks[:, 2:4, :].rearrange("p b (t n) -> p (b t) n", n=P)
        new_ps = banks[:, 4:6, :].rearrange("p b (t n) -> p (b t) n", n=RET_V)
        (block, staged, xi_done, score_done, scored, turn_done, kz_done, out_done, new_done, state_done, chunk_out,
         zeroed) = ctx.enter_context(stage(nc, (
             "staged xi_done score_done scored turn_done kz_done out_done new_done state_done chunk_out zeroed")))

        @block.gpsimd
        def _(pool):
            nc.gpsimd.memset(state[:, :, :], 0.0).then_inc(zeroed, 1)
            with pool.Fori(0, TC) as c:
                pool.wait_ge(chunk_out, c + 1)
                pool.wait_ge(state_done, c * H + 1)
                nc.gpsimd.tensor_copy(v_c[:, :, :], v_rows[:, bass.ds(c, 1), :].rearrange("p a (h n) -> p (a h) n", h=H)).then_inc(staged, 1)
                pool.wait_ge(staged, c * 2 + 2)
                nc.gpsimd.tensor_tensor(q_xi[:, :, :], qk_c[:, 0:H, :], xi, ALU.mult).then_inc(xi_done, 1)

        @block.scalar
        def _(act):
            act.sem_inc(chunk_out, 1)
            with act.Fori(0, TC) as c:
                act.wait_ge(out_done, c + 1)
                act.wait_ge(new_done, c + 1)
                nc.scalar.activation(qk_c[:, :, :], qkT[:, :, bass.ds(c * P, P)], ACT.Copy).then_inc(staged, 1)
                act.wait_ge(out_done, c + 2)
                nc.scalar.activation(outT[:, :, bass.ds(c * P, P)], out_ps, ACT.Copy).then_inc(chunk_out, 1)

        @block.tensor
        def _(pe):
            pe.sem_inc(new_done, 1)
            pe.sem_inc(out_done, 1)
            pe.wait_ge(zeroed, 1)
            with pe.Fori(0, TC) as c:
                pe.wait_ge(staged, c * 2 + 2)
                for h in range(H):
                    last = nc.tensor.matmul(score_ps[:, h * P:(h + 1) * P], qk_c[:, H + h, :], qk_c[:, h, :], start=True, stop=True)
                last.then_inc(score_done, 1)
                for h in range(H):
                    last = nc.tensor.transpose(turned[:, h * P:(h + 1) * P], qk_c[:, H + h, :], k.at["ident"])
                last.then_inc(turn_done, 1)
                pe.wait_ge(scored, c + 1)
                pe.wait_ge(xi_done, c + 1)
                pe.wait_ge(chunk_out, c + 1)
                for h in range(H):
                    for e in range(2):
                        to = out_ps[:, 2 * h + e, :]
                        nc.tensor.matmul(to, v_c[:, h, e * P:(e + 1) * P], scores[:, h, :], start=True, stop=False)
                        last = nc.tensor.matmul(to, state[:, h, e * P:(e + 1) * P], q_xi[:, h, :], start=False, stop=True)
                last.then_inc(out_done, 1)
                pe.wait_ge(kz_done, c + 1)
                for h in range(H):
                    last = nc.tensor.matmul(new_ps[:, h, :], k_zeta[:, h, :], v_c[:, h, :], start=True, stop=True)
                last.then_inc(new_done, 1)

        @block.vector
        def _(dve):
            dve.sem_inc(state_done, 1)
            dve.wait_ge(zeroed, 1)
            with dve.Fori(0, TC) as c:
                dve.wait_ge(score_done, c + 1)
                nc.vector.tensor_tensor(scores[:, :, :], score_ps.rearrange("p (h n) -> p h n", h=H), decay, ALU.mult).then_inc(scored, 1)
                dve.wait_ge(turn_done, c + 1)
                nc.vector.tensor_tensor(k_zeta[:, :, :], turned.rearrange("p (h n) -> p h n", h=H),
                                        zeta.unsqueeze(2).to_broadcast([P, H, P]), ALU.mult).then_inc(kz_done, 1)
                dve.wait_ge(new_done, c + 2)
                dve.wait_ge(out_done, c + 2)
                for h in range(H):
                    nc.vector.scalar_tensor_tensor(state[:, h, :], state[:, h, :], gammas[h], new_ps[:, h, :],
                                                   ALU.mult, ALU.add).then_inc(state_done, 1)


def norm_gate_heads(k, x, n_heads, per, gate):
    nc = k.nc
    n = n_heads * per
    with (
        k.sbuf("squares", [P, n, S]) as sq,
        k.sbuf("log_ms", [P, 2, S]) as log_ms, k.sbuf("rstd", [P, 2, S]) as rstd,
        k.psum("stat", [P, n_heads, S]) as stat,
        stage(nc, "squared gated stat_done log_done rstd_done normed") as (block, squared, gated, stat_done, log_done, rstd_done, normed),
    ):
        @block.scalar
        def _(act):
            for f in range(n):
                nc.scalar.activation(sq[:, f, :], x[:, f, :], ACT.Square).then_inc(squared, 1)
            for f in range(n):
                nc.scalar.activation(gate[:, f, :], gate[:, f, :], ACT.Silu).then_inc(gated, 1)
            for h in range(n_heads):
                act.wait_ge(stat_done, h + 1)
                if h >= 2:
                    act.wait_ge(normed, (h - 1) * per)
                inverse_root(k, act, rstd[:, h % 2, :], log_ms[:, h % 2, :], stat[:, h, :], 1.0 / (per * P), log_done, h + 1
                             ).then_inc(rstd_done, 1)

        @block.tensor
        def _(pe):
            for h in range(n_heads):
                for e in range(per):
                    pe.wait_ge(squared, h * per + e + 1)
                    last = nc.tensor.matmul(stat[:, h, :], k.at["ones"], sq[:, h * per + e, :], start=(e == 0), stop=(e == per - 1))
                last.then_inc(stat_done, 1)

        @block.vector
        def _(dve):
            for f in range(n):
                dve.wait_ge(rstd_done, f // per + 1)
                nc.vector.tensor_tensor(x[:, f, :], x[:, f, :], rstd[:, (f // per) % 2, :], ALU.mult).then_inc(normed, 1)

        @block.gpsimd
        def _(pool):
            for f in range(n):
                pool.wait_ge(normed, f + 1)
                pool.wait_ge(gated, f + 1)
                nc.gpsimd.tensor_tensor(gate[:, f, :], x[:, f, :], gate[:, f, :], ALU.mult)



def sliding_window(k, a, qT, k_dup, v_rows, mixT, mix_at):
    nc = k.nc
    UNITS = 2 * TC
    with ExitStack() as ctx:
        def sb(name, shape):
            return ctx.enter_context(k.sbuf(name, shape))

        q_pair, k_pair, v_pair = sb("q_pair", [P, S]), sb("k_pair", [P, S]), sb("v_pair", [P, TC, 64])
        bias = sb("bias", [P, 2, BAND])
        sinks, neg_sinks, neg_sink = sb("sinks", [P, HEADS]), sb("neg_sinks", [P, HEADS]), sb("neg_sink", [P, 2])
        probs, probs_t = sb("probs", [P, DEEP, BAND]), sb("probs_t", [P, 2, BAND])
        neg_max, sums, sink_exp = sb("neg_max", [P, DEEP]), sb("sums", [P, DEEP]), sb("sink_exp", [P, DEEP])
        banks = ctx.enter_context(k.psum("banks", [P, 8, S]))
        logits, turned, out_ps = banks[:, 0:DEEP, 0:BAND], banks[:, 4:6, 0:BAND], banks[:, 6:8, :]
        (block, admitted, sinks_in, sinks_turned, staged, logit_done, shifted, max_done, exp_done, sink_done, sum_done, recip_done, scaled, turn_done,
         turn_out, pv_done, pair_out) = ctx.enter_context(stage(nc, (
             "admitted sinks_in sinks_turned staged logit_done shifted max_done exp_done sink_done sum_done recip_done scaled turn_done turn_out "
             "pv_done pair_out")))

        def unit(n):
            u, qb = divmod(n, TC)
            first = max(qb - 1, 0)
            return u, qb, first, (qb + 1 - first) * P, 0 if qb else P

        @block.sync
        def _(sp):
            sp.dma_start(sinks[:, :], a["o_sinks"][0].partition_broadcast(P)).then_inc(sinks_in, 16)

        @block.gpsimd
        def _(pool):
            pool.wait_ge(sinks_in, 16)
            nc.gpsimd.tensor_scalar(neg_sinks[:, :], sinks[:, :], -1.0, None, ALU.mult).then_inc(sinks_turned, 1)
            pool.wait_ge(sinks_turned, 1)
            with pool.Fori(0, 2) as g:
                for w in range(2):
                    i = g * 2 + w
                    pool.wait_ge(pv_done, g * (2 * UNITS) + w * UNITS + 1)
                    nc.gpsimd.tensor_copy(q_pair[:, :], qT[:, bass.ds(i, 1), :].rearrange("p a n -> p (a n)")).then_inc(staged, 1)
                    nc.gpsimd.tensor_copy(k_pair[:, :], k_dup[:, bass.ds(g, 1), :].rearrange("p a n -> p (a n)")).then_inc(staged, 1)
                    nc.gpsimd.tensor_tensor(bias[:, :, :], k.band[:, bass.ds(i * 2, 2), :],
                                            k.at["window"].unsqueeze(1).to_broadcast([P, 2, BAND]), ALU.add).then_inc(staged, 1)
                    nc.gpsimd.tensor_copy(neg_sink[:, :], neg_sinks[:, bass.ds(i * 2, 2)]).then_inc(staged, 1)
                    nc.gpsimd.tensor_copy(v_pair[:, :, :], v_rows[:, :, bass.ds(g * 64, 64)]).then_inc(staged, 1)

        @block.tensor
        def _(pe):
            pe.sem_inc(turn_done, 1)
            pe.sem_inc(pv_done, 1)
            with pe.Fori(0, HEADS // 2) as i:
                def score(n):
                    u, qb, first, keys, _ = unit(n)
                    if n >= DEEP:
                        pe.wait_ge(shifted, i * UNITS + n - 2)
                    nc.tensor.matmul(logits[:, n % DEEP, 0:keys], q_pair[64 * u:64 * u + 64, qb * P:(qb + 1) * P],
                                     k_pair[64 * u:64 * u + 64, first * P:first * P + keys], start=True, stop=True).then_inc(logit_done, 1)

                pe.wait_ge(staged, i * 5 + 5)
                pe.wait_ge(shifted, i * UNITS + 1)
                score(0)
                score(1)
                for n in range(UNITS + 1):
                    if n + 2 < UNITS:
                        score(n + 2)
                    if n < UNITS:
                        _, _, _, keys, _ = unit(n)
                        pe.wait_ge(scaled, i * UNITS + n + 2)
                        pe.wait_ge(turn_out, i * UNITS + max(n, 1))
                        for b in range(keys // P):
                            last = nc.tensor.transpose(turned[:, n % 2, b * P:(b + 1) * P], probs[:, n % DEEP, b * P:(b + 1) * P], k.at["ident"])
                        last.then_inc(turn_done, 1)
                    if n >= 1:
                        m = n - 1
                        u, qb, first, keys, _ = unit(m)
                        pe.wait_ge(turn_out, i * UNITS + m + 2)
                        pe.wait_ge(pair_out, i * 2 + u + 1)
                        for b in range(keys // P):
                            last = nc.tensor.matmul(out_ps[64 * u:64 * u + 64, u, qb * P:(qb + 1) * P], v_pair[:, first + b, :],
                                                    probs_t[:, m % 2, b * P:(b + 1) * P], start=(b == 0), stop=(b == keys // P - 1))
                        last.then_inc(pv_done, 1)

        @block.vector
        def _(dve):
            dve.sem_inc(scaled, 1)
            dve.sem_inc(sum_done, 1)
            dve.sem_inc(pair_out, 2)
            dve.sem_inc(shifted, 1)
            with dve.Fori(0, HEADS // 2) as i:
                def shift(n):
                    u, qb, first, keys, at = unit(n)
                    p = n % DEEP
                    dve.wait_ge(logit_done, i * UNITS + n + 1)
                    dve.wait_ge(staged, i * 5 + 5)
                    dve.wait_ge(turn_done, i * UNITS + max(n - 2, 1))
                    dve.wait_ge(sum_done, i * UNITS + max(n - 2, 1))
                    dve.sem_inc(admitted, 1)
                    nc.vector.tensor_tensor_reduce(probs[:, p, 0:keys], logits[:, p, 0:keys], bias[:, u, at:at + keys],
                                                   -1.0, 3e38, ALU.add, ALU.min, neg_max[:, p:p + 1]).then_inc(shifted, 1)
                    dve.wait_ge(shifted, i * UNITS + n + 2)
                    nc.vector.tensor_tensor(neg_max[:, p:p + 1], neg_max[:, p:p + 1], neg_sink[:, u:u + 1], ALU.min).then_inc(max_done, 1)

                def leave(u):
                    half = slice(64 * u, 64 * u + 64)
                    dve.wait_ge(pv_done, i * UNITS + (u + 1) * TC + 1)
                    nc.vector.tensor_copy(mixT[half, bass.ds(i + mix_at, 1), :].rearrange("p a n -> p (a n)"),
                                          out_ps[half, u, :]).then_inc(pair_out, 1)

                shift(0)
                shift(1)
                for n in range(UNITS):
                    _, _, _, keys, _ = unit(n)
                    p = n % DEEP
                    dve.wait_ge(exp_done, i * UNITS + n + 1)
                    dve.wait_ge(sink_done, i * UNITS + n + 1)
                    nc.vector.tensor_tensor(sums[:, p:p + 1], sums[:, p:p + 1], sink_exp[:, p:p + 1], ALU.add).then_inc(sum_done, 1)
                    dve.wait_ge(sum_done, i * UNITS + n + 2)
                    nc.vector.reciprocal(sums[:, p:p + 1], sums[:, p:p + 1]).then_inc(recip_done, 1)
                    dve.wait_ge(recip_done, i * UNITS + n + 1)
                    nc.vector.tensor_scalar(probs[:, p, 0:keys], probs[:, p, 0:keys], sums[:, p:p + 1], None, ALU.mult).then_inc(scaled, 1)
                    if n + 2 < UNITS:
                        shift(n + 2)
                    if n == TC + 2:
                        leave(0)
                leave(1)

        @block.scalar
        def _(act):
            act.sem_inc(turn_out, 1)
            with act.Fori(0, HEADS // 2) as i:
                def exps(n):
                    u, qb, first, keys, _ = unit(n)
                    p = n % DEEP
                    act.wait_ge(max_done, i * UNITS + n + 1)
                    act.wait_ge(scaled, i * UNITS + max(n - 2, 1))
                    nc.scalar.activation(probs[:, p, 0:keys], probs[:, p, 0:keys], ACT.Exp, scale=-1.0,
                                         bias=neg_max[:, p:p + 1], accum_out=sums[:, p:p + 1]).then_inc(exp_done, 1)
                    nc.scalar.activation(sink_exp[:, p:p + 1], neg_sink[:, u:u + 1], ACT.Exp, scale=-1.0,
                                         bias=neg_max[:, p:p + 1]).then_inc(sink_done, 1)

                exps(0)
                for n in range(UNITS):
                    u, qb, first, keys, _ = unit(n)
                    if n + 1 < UNITS:
                        exps(n + 1)
                    act.wait_ge(turn_done, i * UNITS + n + 2)
                    act.wait_ge(pv_done, i * UNITS + max(n, 1))
                    nc.scalar.activation(probs_t[:, n % 2, 0:keys], turned[:, n % 2, 0:keys], ACT.Copy).then_inc(turn_out, 1)


def tile_of(buf, index):
    return buf[:, bass.ds(index, 1), :].rearrange("p a n -> p (a n)")


def double_halves(k, src, dst):
    nc = k.nc
    with stage(nc, "none") as (block, _none):
        @block.scalar
        def _(act):
            for half in (0, 64):
                nc.scalar.activation(dst[half:half + 64, 0, :], src[0:64, :], ACT.Copy)

        @block.vector
        def _(dve):
            for half in (0, 64):
                nc.vector.tensor_copy(dst[half:half + 64, 1, :], src[64:P, :])


def odd_mixer(k, a, mixT):
    nc = k.nc
    w = a["o_w_in"][0]

    def feat(dst, scale=None, at=0):
        return lambda e, t, j, ps: copy_out(nc, e, tile_of(dst, 4 * t + (j + at)), ps, scale)

    with k.sbuf("sqT", [P, 4, S]) as sqT, k.sbuf("sk_dup", [P, 2, S]) as sk_dup, k.sbuf("sv_rows", [P, TC, P]) as sv_rows:
        with k.sbuf("rqkT", [P, 2 * RET_H, S]) as qkT, k.sbuf("rv_rows", [P, TC, D]) as v_rows, k.sbuf("skT", [P, S]) as skT:
            project(k, [
                run(2, weight_tiles(w, O_RQ), lambda e, t, j, ps: copy_out(nc, e, tile_of(qkT, 4 * t + j), ps, RET_QK ** -0.5 if t else None)),
                run(2, weight_tiles(w, O_RV), lambda e, t, j, ps: copy_out(nc, e, v_rows[:, j, bass.ds(t * COLS, COLS)], ps), rows=True),
                run(2, weight_tiles(w, O_RG), feat(mixT)),
                run(1, weight_tiles(w, O_SQ), feat(sqT, 64 ** -0.5))])
            project_items(k, w, [([(O_SK, BAND)], [
                ("feat", 0, P, lambda e, ps: copy_out(nc, e, skT[:, :], ps)),
                ("rows", 0, 2 * P, lambda e, ps: copy_out(nc, e, sv_rows[:, 0:2, :], ps[:, :, P:]), (0, 1)),
                ("rows", 0, 2 * P, lambda e, ps: copy_out(nc, e, sv_rows[:, 2:4, :], ps[:, :, P:]), (2, 3))])])
            double_halves(k, skT, sk_dup)
            with k.sbuf("ret_table", [P, a["ret_table"].shape[1]]) as table, k.sbuf("retT", [P, DT, S]) as retT:
                with stage(nc, "table_in") as (block, table_in):
                    @block.sync
                    def _(sp):
                        sp.dma_start(table[:, :], a["ret_table"]).then_inc(table_in, 16)
                        sp.wait_ge(table_in, 16)
                rotate(k, [qkT[:, j, :] for j in range(2 * RET_H)], k.at["swap_128"], table[:, 0:S], table[:, S:2 * S])
                retention(k, qkT, v_rows, table, retention_constants()[1], retT)
                norm_gate_heads(k, retT, RET_H, 2, mixT)
        sliding_window(k, a, sqT, sk_dup, sv_rows, mixT, DT)



N_GDN, N_NSA, N_SB, HD = 6, 6, 4, 64
GDN_T, NSA_T, SB_T = N_GDN // 2, N_NSA // 2, N_SB // 2
FF_T = 22
CMP_LEN, CMP_STRIDE = 32, 16
N_CMP = (S - CMP_LEN) // CMP_STRIDE + 1
V_MIX, V_GCONV, V_FFN, V_PLE, V_PLEN, V_PEK, V_PEV, V_GN, V_NN, V_SN, V_FIN, V_FCONV = 0, 8, 44, 52, 60, 68, 84, 100, 101, 102, 103, 111
W_GDN, W_AB, W_NQ, W_KC, W_KW, W_GATE, W_SQ, W_SV = 0, 1536, 1548, 1932, 2444, 2700, 2718, 3230


def layer_of(ap, l):
    names = " ".join(f"d{i}" for i in range(len(ap.shape) - 1))
    first, *rest = names.split()
    return ap[bass.ds(l, 1)].rearrange(f"a {names} -> (a {first}) {' '.join(rest)}".rstrip())


def layer_vectors(k, a, l):
    nc = k.nc
    rows = [
        (0, V_MIX, 8, 0, P, layer_of(a["ln_mix_2"], l).rearrange("(f p) -> f p", p=P)),
        (0, V_GCONV, 36, 0, P, layer_of(a["gdn_conv_2"], l).rearrange("t (f p) -> (t f) p", p=P)),
        (0, V_FFN, 8, 0, P, layer_of(a["ln_ffn_2"], l).rearrange("(f p) -> f p", p=P)),
        (0, V_PLE, 8, 0, P, layer_of(a["ln_ple_2"], l).rearrange("(f p) -> f p", p=P)),
        (0, V_PLEN, 8, 0, P, layer_of(a["ple_norm_2"], l).rearrange("(f p) -> f p", p=P)),
        (0, V_PEK, 16, 0, P, layer_of(a["nsa_pe_k_2"], l).rearrange("(m j) d -> m (j d)", j=2)),
        (0, V_PEV, 16, 0, P, layer_of(a["nsa_pe_v_2"], l).rearrange("(m j) d -> m (j d)", j=2)),
        (0, V_FIN, 8, 0, P, a["ln_final_2"].rearrange("(f p) -> f p", p=P)),
        (1, 0, 88, 0, P, layer_of(a["ffn_conv_2"], l)[0:2].rearrange("t (f p) -> (t f) p", p=P)),
        (2, 0, 44, 0, P, layer_of(a["ffn_conv_2"], l)[2:3].rearrange("t (f p) -> (t f) p", p=P)),
    ]
    for at, name in ((V_GN, "gdn_norm_2"), (V_NN, "nsa_norm_2"), (V_SN, "sb_norm_2")):
        for half in (0, HD):
            rows.append((0, at, 1, half, HD, a[name][bass.ds(l, 1)]))
    used = (V_FCONV, 88, 44)
    with (
        k.sbuf("vec_rows", [P, 3, P]) as vec_rows, k.psum("turned", [P, 3, S]) as turned,
        stage(nc, "rows_in vec_turned") as (block, rows_in, vec_turned),
    ):
        @block.sync
        def _(sp):
            for g, at, n, col, width, src in rows:
                sp.dma_start(vec_rows[at:at + n, g, col:col + width], src).then_inc(rows_in, 16)

        @block.tensor
        def _(pe):
            pe.wait_ge(rows_in, 16 * len(rows))
            for g in range(3):
                n = used[g]
                nc.tensor.transpose(turned[:, g, 0:n], vec_rows[0:n, g, :], k.at["ident"][0:n, 0:n]).then_inc(vec_turned, 1)

        @block.vector
        def _(dve):
            at = 0
            for g in range(3):
                dve.wait_ge(vec_turned, g + 1)
                nc.vector.tensor_copy(k.vec2[:, at:at + used[g]], turned[:, g, 0:used[g]])
                at += used[g]


def rotary_tables(k, a):
    nc = k.nc
    turn = 2 * np.pi
    c1 = 6.28125
    c2 = float(np.float32(np.round((turn - c1) * 2 ** 21) / 2 ** 21))
    c3 = float(np.float32(turn - c1 - c2))
    magic = 1.5 * 2.0 ** 23
    edge = 3.1415925
    with (
        k.sbuf("pos_int", [P, S], I32) as pos_int, k.sbuf("ang", [P, S]) as ang, k.sbuf("turns", [P, S]) as turns,
        k.sbuf("over", [P, S]) as over,
        stage(nc, "pos_in step sin_done") as (block, pos_in, step, sin_done),
    ):
        @block.sync
        def _(sp):
            sp.dma_start(pos_int[:, :], a["positions_2"][0].partition_broadcast(P)).then_inc(pos_in, 16)

        @block.vector
        def _(dve):
            dve.wait_ge(pos_in, 16)
            nc.vector.tensor_copy(ang[:, :], pos_int[:, :]).then_inc(step, 1)
            dve.wait_ge(step, 1)
            nc.vector.tensor_scalar(ang[:, :], ang[:, :], k.at["inv_freq"], None, ALU.mult).then_inc(step, 1)
            dve.wait_ge(step, 2)
            nc.vector.tensor_scalar(turns[:, :], ang[:, :], 1.0 / turn, magic, ALU.mult, ALU.add).then_inc(step, 1)
            dve.wait_ge(step, 3)
            nc.vector.tensor_scalar(turns[:, :], turns[:, :], -magic, None, ALU.add).then_inc(step, 1)
            for n, c in enumerate((c1, c2, c3)):
                dve.wait_ge(step, 4 + n)
                nc.vector.scalar_tensor_tensor(ang[:, :], turns[:, :], -c, ang[:, :], ALU.mult, ALU.add).then_inc(step, 1)
            dve.wait_ge(step, 7)
            nc.vector.tensor_scalar(turns[:, :], ang[:, :], np.pi / 2, None, ALU.add).then_inc(step, 1)
            dve.wait_ge(step, 8)
            nc.vector.tensor_scalar(over[:, :], turns[:, :], edge, -turn, ALU.is_gt, ALU.mult).then_inc(step, 1)
            dve.wait_ge(step, 9)
            nc.vector.tensor_tensor(turns[:, :], turns[:, :], over[:, :], ALU.add).then_inc(step, 1)
            dve.wait_ge(step, 10)
            nc.vector.tensor_scalar(turns[:, :], turns[:, :], edge, -edge, ALU.min, ALU.max).then_inc(step, 1)
            nc.vector.tensor_scalar(ang[:, :], ang[:, :], edge, -edge, ALU.min, ALU.max).then_inc(step, 1)
            dve.wait_ge(sin_done, 1)
            nc.vector.tensor_scalar(k.sin, k.sin, k.at["half_sign"], None, ALU.mult)

        @block.scalar
        def _(act):
            act.wait_ge(step, 12)
            nc.scalar.activation(k.sin, ang[:, :], ACT.Sin).then_inc(sin_done, 1)
            nc.scalar.activation(k.cos, turns[:, :], ACT.Sin)


def swap_halves(k, tiles):
    nc = k.nc
    with (
        k.psum("swapped", [P, len(tiles), S]) as swapped,
        stage(nc, "swap_done") as (block, swap_done),
    ):
        @block.tensor
        def _(pe):
            for j, (orig, _) in enumerate(tiles):
                nc.tensor.matmul(swapped[:, j, :], k.at["swap_128"], orig, start=True, stop=True).then_inc(swap_done, 1)

        @block.vector
        def _(dve):
            for j in range(0, len(tiles), 2):
                dve.wait_ge(swap_done, j + 1)
                nc.vector.tensor_copy(tiles[j][1], swapped[:, j, :])

        @block.scalar
        def _(act):
            for j in range(1, len(tiles), 2):
                act.wait_ge(swap_done, j + 1)
                nc.scalar.activation(tiles[j][1], swapped[:, j, :], ACT.Copy)



def gdn_steps(k, a, l, ab, g, beta, beta_eg, to_end, gates):
    nc = k.nc
    H = N_GDN
    n = TC * H
    with (
        k.sbuf("rows", [P, 2, H]) as rows, k.sbuf("tmp", [P, 4, n]) as tmp, k.psum("sums", [P, 2, S]) as sums,
        stage(nc, "rows_in step exp_done act_done sum_done") as (block, rows_in, step, exp_done, act_done, sum_done),
    ):
        v, mag, eg, rate = (tmp[:, i, :] for i in range(4))

        def by_pair(x):
            return x.rearrange("p (c h) -> p c h", h=H)

        def per_head(row):
            return row.unsqueeze(1).to_broadcast([P, TC, H])

        @block.sync
        def _(sp):
            sp.dma_start(rows[:, 0, :], layer_of(a["gdn_dt_bias_2"], l).partition_broadcast(P)).then_inc(rows_in, 16)
            sp.dma_start(rows[:, 1, :], layer_of(a["gdn_a_log_2"], l).partition_broadcast(P)).then_inc(rows_in, 16)

        @block.scalar
        def _(act):
            nc.scalar.activation(by_pair(beta), ab[:, :, H:2 * H], ACT.Sigmoid).then_inc(act_done, 1)
            nc.scalar.activation(gates, ab[:, :, 2 * H:2 * H + 3 * N_NSA], ACT.Sigmoid)
            act.wait_ge(rows_in, 32)
            nc.scalar.activation(rate[:, 0:H], rows[:, 1, :], ACT.Exp).then_inc(act_done, 1)
            act.wait_ge(step, 2)
            nc.scalar.activation(mag, mag, ACT.Exp, scale=-1.0).then_inc(exp_done, 1)
            act.wait_ge(exp_done, 1)
            nc.scalar.activation(mag, mag, ACT.Ln, bias=1.0).then_inc(exp_done, 1)
            act.wait_ge(sum_done, 1)
            nc.scalar.activation(eg, sums[:, 0, 0:n], ACT.Exp).then_inc(exp_done, 1)
            nc.scalar.activation(to_end, sums[:, 1, 0:n], ACT.Exp)

        @block.vector
        def _(dve):
            dve.wait_ge(rows_in, 32)
            nc.vector.tensor_tensor(by_pair(v), ab[:, :, 0:H], per_head(rows[:, 0, :]), ALU.add).then_inc(step, 1)
            dve.wait_ge(step, 1)
            nc.vector.scalar_tensor_tensor(mag, v, -1.0, v, ALU.mult, ALU.max).then_inc(step, 1)
            dve.wait_ge(exp_done, 2)
            nc.vector.scalar_tensor_tensor(v, v, 0.0, mag, ALU.max, ALU.add).then_inc(step, 1)
            dve.wait_ge(step, 3)
            dve.wait_ge(act_done, 2)
            nc.vector.scalar_tensor_tensor(by_pair(g), by_pair(v), -1.0, per_head(rate[:, 0:H]), ALU.mult, ALU.mult).then_inc(step, 1)
            dve.wait_ge(exp_done, 3)
            nc.vector.tensor_tensor(beta_eg, eg, beta, ALU.mult)

        @block.tensor
        def _(pe):
            pe.wait_ge(step, 4)
            nc.tensor.matmul(sums[:, 0, 0:n], k.at["upto_64"], g, start=True, stop=True)
            nc.tensor.matmul(sums[:, 1, 0:n], k.at["after_64"], g, start=True, stop=True).then_inc(sum_done, 1)


def norm_heads(k, tiles, total_scale):
    nc = k.nc
    n = len(tiles)
    gated = [j for j in range(n) if tiles[j][2] is not None]
    with (
        k.sbuf("squares", [P, n, S]) as squares,
        k.sbuf("log_ms", [P, 2, S]) as log_ms, k.sbuf("rstd", [P, 2, S]) as rstd, k.psum("stat", [P, n, S]) as stat,
        stage(nc, "squared gate_done stat_done log_done rstd_done normed") as
        (block, squared, gate_done, stat_done, log_done, rstd_done, normed),
    ):
        @block.scalar
        def _(act):
            for j, (x, _, _) in enumerate(tiles):
                nc.scalar.activation(squares[:, j, :], x, ACT.Square).then_inc(squared, 1)
            for j in gated:
                nc.scalar.activation(tiles[j][2], tiles[j][2], ACT.Silu).then_inc(gate_done, 1)
            for j in range(n):
                act.wait_ge(stat_done, j + 1)
                if j >= 2:
                    act.wait_ge(normed, j - 1)
                inverse_root(k, act, rstd[:, j % 2, :], log_ms[:, j % 2, :], stat[:, j, :], total_scale, log_done, j + 1
                             ).then_inc(rstd_done, 1)

        @block.tensor
        def _(pe):
            for j in range(n):
                pe.wait_ge(squared, j + 1)
                nc.tensor.matmul(stat[:, j, :], k.at["ones_64"], squares[:, j, :], start=True, stop=True).then_inc(stat_done, 1)

        @block.vector
        def _(dve):
            for j, (x, gain, _) in enumerate(tiles):
                dve.wait_ge(rstd_done, j + 1)
                nc.vector.scalar_tensor_tensor(x, x, gain, rstd[:, j % 2, :], ALU.mult, ALU.mult).then_inc(normed, 1)

        @block.gpsimd
        def _(pool):
            for m, j in enumerate(gated):
                pool.wait_ge(normed, j + 1)
                pool.wait_ge(gate_done, m + 1)
                nc.gpsimd.tensor_tensor(tiles[j][0], tiles[j][0], tiles[j][2], ALU.mult)


def delta_rule(k, qkv, g, beta, beta_eg, to_end, mixT):
    nc = k.nc
    H, T = N_GDN, GDN_T
    LEVELS = 5
    with ExitStack() as ctx:
        def sb(name, shape):
            return ctx.enter_context(k.sbuf(name, shape))

        x_c = sb("x_c", [P, 3 * T, P])
        small = sb("small", [P, 4, H])
        g_wide = sb("g_wide", [P, H, HD])
        v_beta, k_beta, k_end = sb("v_beta", [P, H, HD]), sb("k_beta", [P, H, HD]), sb("k_end", [P, H, HD])
        steps = sb("steps", [P, H, P])
        decay, decay_t = sb("decay", [P, H, P]), sb("decay_t", [P, H, P])
        run = sb("run", [P, T, P])
        low, low_t = sb("low", [P, H, P]), sb("low_t", [P, H, P])
        part = sb("part", [P, H, P])
        attn_t = sb("attn_t", [P, H, P])
        inv, inv_t, y = sb("inv", [P, H, P]), sb("inv_t", [P, H, P]), sb("lt_inv", [P, H, P])
        u, w_t, q_run = sb("u", [P, H, HD]), sb("w_t", [P, T, P]), sb("q_run", [P, T, P])
        v_new = sb("v_new", [P, H, HD])
        state = sb("gdn_state", [P, T, HD])
        banks = ctx.enter_context(k.psum("banks", [P, 8, S]))

        def wide(b, n=P):
            return banks[:, b:b + 2, 0:T * n].rearrange("p b (t n) -> p t b n", t=T)

        def paired(x):
            return x.rearrange("p (t b) n -> p t b n", b=2)

        turned_k, turned_v = (banks[:, b, 0:H * HD].rearrange("p (h n) -> p h n", h=H) for b in (0, 1))
        kk_ps, low_t_ps, y_ps = wide(0), wide(0), wide(0)
        decay_ps, kq_ps, ty_ps = wide(2), wide(2), wide(2)
        decay_t_ps, yt_ps = wide(4), wide(4)
        run_ps = banks[:, 6, 0:T * P].rearrange("p (t n) -> p t n", t=T)
        w_ps = run_ps
        u_ps = banks[:, 7, 0:H * HD].rearrange("p (h n) -> p h n", h=H)
        new_ps = wide(0, HD)
        inter_ps, intra_ps = (banks[:, b, 0:T * P].rearrange("p (t n) -> p t n", t=T) for b in (3, 4))
        grow_ps = banks[:, 2, 0:T * HD].rearrange("p (t n) -> p t n", t=T)

        (block, admitted, zeroed, staged, turn_done, rows_done, steps_done, decay_done, run_done, exp_done, kk_done, kq_done, masked,
         low_done, attn_done, low_turned, low_t_out, part_done, y_done, y_out, ty_done, yt_done, inv_done, inv_t_done, qrun_done,
         uw_done, uw_out, vn_done, vn_out, grow_done, state_done, inter_done, inter_out, intra_done, pass_out, first_done) = ctx.enter_context(stage(nc, (
             "admitted zeroed staged turn_done rows_done steps_done decay_done run_done exp_done kk_done kq_done masked low_done attn_done "
             "low_turned low_t_out part_done y_done y_out ty_done yt_done inv_done inv_t_done qrun_done uw_done uw_out vn_done "
             "vn_out grow_done state_done inter_done inter_out intra_done pass_out first_done")))

        def per_head(col, width):
            return col.unsqueeze(2).to_broadcast([P, H, width])

        def each_head(m):
            return m.unsqueeze(1).to_broadcast([P, H, P])

        @block.gpsimd
        def _(pool):
            nc.gpsimd.memset(state[:, :, :], 0.0).then_inc(zeroed, 1)
            with pool.Fori(0, TC) as c:
                pool.wait_ge(pass_out, c + 1)
                for i, src in enumerate((g, beta, beta_eg, to_end)):
                    nc.gpsimd.tensor_copy(small[:, i, :], src[:, bass.ds(c * H, H)]).then_inc(staged, 1)
                nc.gpsimd.tensor_copy(g_wide[:, :, :], per_head(g[:, bass.ds(c * H, H)], HD)).then_inc(staged, 1)
                pool.wait_ge(exp_done, c * 3 + 1)
                nc.gpsimd.tensor_tensor(decay[:, :, :], decay[:, :, :], each_head(k.at["after_64"]), ALU.mult).then_inc(masked, 1)
                pool.wait_ge(masked, c * 3 + 1)
                pool.wait_ge(staged, c * 6 + 6)
                nc.gpsimd.tensor_tensor(decay[:, :, :], decay[:, :, :], per_head(small[:, 1, :], P), ALU.mult).then_inc(masked, 1)
                pool.wait_ge(exp_done, c * 3 + 2)
                nc.gpsimd.tensor_tensor(decay_t[:, :, :], decay_t[:, :, :], each_head(k.at["upto_64"]), ALU.mult).then_inc(masked, 1)
                pool.wait_ge(exp_done, c * 3 + 3)
                nc.gpsimd.tensor_tensor(q_run[:, :, :], x_c[:, 0:T, :], run[:, :, :], ALU.mult).then_inc(qrun_done, 1)
                pool.wait_ge(low_t_out, c + 1)
                for n in range(LEVELS):
                    pool.wait_ge(y_done, c * (2 * LEVELS) + 2 * n + 1)
                    nc.gpsimd.tensor_tensor(part[:, :, :], low_t[:, :, :], each_head(k.level_masks[n + 1]), ALU.mult).then_inc(part_done, 1)

        @block.scalar
        def _(act):
            with act.Fori(0, TC) as c:
                act.wait_ge(pass_out, c + 1)
                nc.scalar.activation(x_c[:, :, :], qkv[:, :, bass.ds(c * P + (CONV - 1), P)], ACT.Copy).then_inc(staged, 1)
                act.wait_ge(decay_done, c * 2 + 1)
                nc.scalar.activation(paired(decay[:, :, :]), decay_ps, ACT.Exp).then_inc(exp_done, 1)
                act.wait_ge(decay_done, c * 2 + 2)
                nc.scalar.activation(paired(decay_t[:, :, :]), decay_t_ps, ACT.Exp).then_inc(exp_done, 1)
                act.wait_ge(run_done, c + 1)
                nc.scalar.activation(run[:, :, :], run_ps, ACT.Exp).then_inc(exp_done, 1)
                act.wait_ge(low_turned, c + 1)
                nc.scalar.activation(paired(low_t[:, :, :]), low_t_ps, ACT.Copy).then_inc(low_t_out, 1)
                for n in range(LEVELS):
                    for b in range(2):
                        act.wait_ge(y_done, c * (2 * LEVELS) + 2 * n + b + 2)
                        nc.scalar.activation(paired(y[:, :, :])[:, :, b, :], y_ps[:, :, b, :], ACT.Copy).then_inc(y_out, 1)
                act.wait_ge(uw_done, c + 1)
                nc.scalar.activation(u[:, :, :], u_ps, ACT.Copy).then_inc(uw_out, 1)
                nc.scalar.activation(w_t[:, :, :], w_ps, ACT.Copy).then_inc(uw_out, 1)
                act.wait_ge(inter_done, c * 2 + 2)
                nc.scalar.activation(mixT[:, 0:T, bass.ds(c * P, P)], inter_ps, ACT.Copy).then_inc(inter_out, 1)

        @block.tensor
        def _(pe):
            pe.sem_inc(y_done, 1)
            pe.wait_ge(zeroed, 1)
            with pe.Fori(0, TC) as c:
                pe.wait_ge(staged, c * 6 + 6)
                for t in range(T):
                    nc.tensor.transpose(banks[:, 0, t * P:(t + 1) * P], x_c[:, T + t, :], k.at["ident"])
                for t in range(T):
                    last = nc.tensor.transpose(banks[:, 1, t * P:(t + 1) * P], x_c[:, 2 * T + t, :], k.at["ident"])
                last.then_inc(turn_done, 1)
                pe.wait_ge(steps_done, c + 1)
                pe.wait_ge(state_done, c * 2 * T + 1)
                for b in range(2):
                    last = nc.tensor.matmul(decay_ps[:, :, b, :], k.at["upto_64"], paired(steps[:, :, :])[:, :, b, :], start=True, stop=True)
                last.then_inc(decay_done, 1)
                for h in range(H):
                    last = nc.tensor.matmul(decay_t_ps[:, h // 2, h % 2, :], steps[:, h, :], k.at["upto_64"], start=True, stop=True)
                last.then_inc(decay_done, 1)
                for t in range(T):
                    last = nc.tensor.matmul(run_ps[:, t, :], g_wide[:, 2 * t:2 * t + 2, :].rearrange("p h n -> p (h n)"), k.at["upto_64"], start=True, stop=True)
                last.then_inc(run_done, 1)
                pe.wait_ge(rows_done, c * 3 + 3)
                for h in range(H):
                    at = slice(HD * (h % 2), HD * (h % 2) + HD)
                    last = nc.tensor.matmul(kk_ps[:, h // 2, h % 2, :], x_c[at, T + h // 2, :], x_c[at, T + h // 2, :], start=True, stop=True)
                last.then_inc(kk_done, 1)
                pe.wait_ge(exp_done, c * 3 + 1)
                for h in range(H):
                    at = slice(HD * (h % 2), HD * (h % 2) + HD)
                    last = nc.tensor.matmul(kq_ps[:, h // 2, h % 2, :], x_c[at, T + h // 2, :], x_c[at, h // 2, :], start=True, stop=True)
                last.then_inc(kq_done, 1)
                pe.wait_ge(low_done, c + 1)
                for h in range(H):
                    last = nc.tensor.transpose(low_t_ps[:, h // 2, h % 2, :], low[:, h, :], k.at["ident"])
                last.then_inc(low_turned, 1)
                pe.wait_ge(attn_done, c + 1)
                pe.wait_ge(exp_done, c * 3 + 3)
                for n in range(LEVELS):
                    pe.wait_ge(part_done, c * LEVELS + n + 1)
                    for b in range(2):
                        pe.wait_ge(inv_done, c * (2 * LEVELS) + 2 * n + b + 1)
                        for h in range(b, H, 2):
                            last = nc.tensor.matmul(y_ps[:, h // 2, b, :], part[:, h, :], inv[:, h, :], start=True, stop=True)
                        last.then_inc(y_done, 1)
                    for b in range(2):
                        pe.wait_ge(inv_t_done, c * (2 * LEVELS + 2) + 2 * n + b + 1)
                        pe.wait_ge(y_out, c * (2 * LEVELS) + 2 * n + b + 1)
                        if n < LEVELS - 1:
                            for h in range(b, H, 2):
                                last = nc.tensor.matmul(ty_ps[:, h // 2, b, :], inv_t[:, h, :], y[:, h, :], start=True, stop=True)
                            last.then_inc(ty_done, 1)
                        for h in range(b, H, 2):
                            last = nc.tensor.matmul(yt_ps[:, h // 2, b, :], y[:, h, :], inv_t[:, h, :], start=True, stop=True)
                        last.then_inc(yt_done, 1)
                pe.wait_ge(inv_t_done, c * (2 * LEVELS + 2) + 2 * LEVELS + 2)
                for h in range(H):
                    at = slice(HD * (h % 2), HD * (h % 2) + HD)
                    nc.tensor.matmul(u_ps[:, h, :], inv_t[:, h, :], v_beta[:, h, :], start=True, stop=True)
                    last = nc.tensor.matmul(w_ps[at, h // 2, :], k_beta[:, h, :], inv_t[:, h, :], start=True, stop=True)
                last.then_inc(uw_done, 1)
                pe.wait_ge(uw_out, c * 2 + 2)
                pe.wait_ge(qrun_done, c + 1)
                for i in range(2):
                    rows = slice(HD * i, HD * i + HD)
                    pe.wait_ge(state_done, c * (2 * T) + i * T + 1)
                    pe.sem_inc(admitted, 1)
                    for h in range(H):
                        at = slice(HD * (h % 2), HD * (h % 2) + HD)
                        last = nc.tensor.matmul(new_ps[rows, h // 2, h % 2, :], w_t[at, h // 2, rows], state[at, h // 2, :], start=True, stop=True)
                    last.then_inc(vn_done, 1)
                    for h in range(H):
                        at = slice(HD * (h % 2), HD * (h % 2) + HD)
                        last = nc.tensor.matmul(inter_ps[at, h // 2, rows], state[at, h // 2, :], q_run[at, h // 2, rows], start=True, stop=True)
                    last.then_inc(inter_done, 1)
                    pe.wait_ge(vn_out, c * 2 + i + 1)
                    pe.sem_inc(admitted, 1)
                    for h in range(H):
                        at = slice(HD * (h % 2), HD * (h % 2) + HD)
                        last = nc.tensor.matmul(grow_ps[at, h // 2, :], k_end[rows, h, :], v_new[rows, h, :], start=True, stop=True)
                    last.then_inc(grow_done, 1)
                for h in range(H):
                    at = slice(HD * (h % 2), HD * (h % 2) + HD)
                    last = nc.tensor.matmul(intra_ps[at, h // 2, :], v_new[:, h, :], attn_t[:, h, :], start=True, stop=True)
                last.then_inc(intra_done, 1)

        @block.vector
        def _(dve):
            dve.sem_inc(state_done, 1)
            dve.sem_inc(pass_out, 1)
            dve.wait_ge(zeroed, 1)
            with dve.Fori(0, TC) as c:
                dve.wait_ge(staged, c * 6 + 6)
                nc.vector.tensor_tensor(steps[:, :, :], each_head(k.at["after_64"]), per_head(small[:, 0, :], P), ALU.mult).then_inc(steps_done, 1)
                dve.wait_ge(turn_done, c + 1)
                nc.vector.tensor_tensor(v_beta[:, :, :], turned_v, per_head(small[:, 1, :], HD), ALU.mult).then_inc(rows_done, 1)
                nc.vector.tensor_tensor(k_beta[:, :, :], turned_k, per_head(small[:, 2, :], HD), ALU.mult).then_inc(rows_done, 1)
                nc.vector.tensor_tensor(k_end[:, :, :], turned_k, per_head(small[:, 3, :], HD), ALU.mult).then_inc(rows_done, 1)
                dve.wait_ge(kk_done, c + 1)
                dve.wait_ge(masked, c * 3 + 2)
                nc.vector.tensor_tensor(paired(low[:, :, :]), kk_ps, paired(decay[:, :, :]), ALU.mult).then_inc(low_done, 1)
                dve.wait_ge(kq_done, c + 1)
                dve.wait_ge(masked, c * 3 + 3)
                nc.vector.tensor_tensor(paired(attn_t[:, :, :]), kq_ps, paired(decay_t[:, :, :]), ALU.mult).then_inc(attn_done, 1)
                dve.wait_ge(low_done, c + 1)
                nc.vector.tensor_tensor(inv[:, :, :], low[:, :, :], each_head(k.at["first_mask"]), ALU.mult).then_inc(first_done, 1)
                dve.wait_ge(low_t_out, c + 1)
                nc.vector.tensor_tensor(inv_t[:, :, :], low_t[:, :, :], each_head(k.level_masks[0]), ALU.mult).then_inc(first_done, 1)
                dve.wait_ge(first_done, c * 2 + 2)
                nc.vector.tensor_tensor(inv[:, :, :], each_head(k.at["ident"]), inv[:, :, :], ALU.subtract).then_inc(inv_done, 2)
                nc.vector.tensor_tensor(inv_t[:, :, :], each_head(k.at["ident"]), inv_t[:, :, :], ALU.subtract).then_inc(inv_t_done, 2)
                for n in range(LEVELS):
                    for b in range(2):
                        here, here_t = (paired(x[:, :, :])[:, :, b, :] for x in (inv, inv_t))
                        if n < LEVELS - 1:
                            dve.wait_ge(ty_done, c * (2 * LEVELS - 2) + 2 * n + b + 1)
                            dve.wait_ge(inv_done, c * (2 * LEVELS) + 2 * n + b + 1)
                            nc.vector.tensor_tensor(here, here, ty_ps[:, :, b, :], ALU.subtract).then_inc(inv_done, 1)
                        dve.wait_ge(yt_done, c * (2 * LEVELS) + 2 * n + b + 1)
                        dve.wait_ge(inv_t_done, c * (2 * LEVELS + 2) + 2 * n + b + 1)
                        nc.vector.tensor_tensor(here_t, here_t, yt_ps[:, :, b, :], ALU.subtract).then_inc(inv_t_done, 1)
                dve.wait_ge(uw_out, c * 2 + 2)
                for i in range(2):
                    rows = slice(HD * i, HD * i + HD)
                    dve.wait_ge(vn_done, c * 2 + i + 1)
                    nc.vector.tensor_tensor(paired(v_new[rows, :, :]), paired(u[rows, :, :]), new_ps[rows, :, :, :], ALU.subtract).then_inc(vn_out, 1)
                    dve.wait_ge(grow_done, c * 2 + i + 1)
                    dve.wait_ge(inter_done, c * 2 + i + 1)
                    dve.wait_ge(state_done, c * (2 * T) + i * T + 1)
                    for t in range(T):
                        nc.vector.scalar_tensor_tensor(state[:, t, :], state[:, t, :], run[:, t, HD * i + HD - 1:HD * i + HD],
                                                       grow_ps[:, t, :], ALU.mult, ALU.add).then_inc(state_done, 1)
                dve.wait_ge(inter_out, c + 1)
                dve.wait_ge(intra_done, c + 1)
                nc.vector.tensor_tensor(mixT[:, 0:T, bass.ds(c * P, P)], mixT[:, 0:T, bass.ds(c * P, P)], intra_ps, ALU.add).then_inc(pass_out, 1)



def compress_keys(k, a, l, k2, v2, kc_dup, vc_rows):
    nc = k.nc
    M = CMP_LEN // 2
    G = 2
    n = G * N_CMP
    HID = P
    with ExitStack() as ctx:
        def sb(name, shape):
            return ctx.enter_context(k.sbuf(name, shape))

        w1 = sb("cmp_w1", [P, 2, M, HID])
        w2 = sb("cmp_w2", [P, 3, HD])
        pairs_of = sb("token_pairs", [P, 2, G, S])
        hid = sb("hid", [P, 2, n])
        pe_cols = sb("pe_cols", [P, 2])
        ps = ctx.enter_context(k.psum("cmp_ps", [P, 5, S]))
        (block, w_in, shifted, hid_done, pe_out, act_done, out_done) = ctx.enter_context(stage(
            nc, "w_in shifted hid_done pe_out act_done out_done"))

        @block.sync
        def _(sp):
            for i, name in enumerate(("k", "v")):
                rows = layer_of(a[f"nsa_cmp_{name}_w1_2"], l).rearrange("(m p) c -> p m c", p=P)
                for half in (slice(0, M // 2), slice(M // 2, M)):
                    sp.dma_start(w1[:, i, half, :], rows[:, half, :]).then_inc(w_in, 16)
            for i, name in enumerate(("k", "k", "v")):
                sp.dma_start(w2[:, i, :], layer_of(a[f"nsa_cmp_{name}_w2_2"], l)).then_inc(w_in, 16)

        @block.gpsimd
        def _(pool):
            for i, x in enumerate((k2, v2)):
                for g in range(G):
                    nc.gpsimd.tensor_copy(pairs_of[0:HD, i, g, :], x[g][0:HD, :]).then_inc(shifted, 1)
                    nc.gpsimd.tensor_copy(pairs_of[HD:P, i, g, 0:S - 1], x[1 - g][HD:P, 1:S]).then_inc(shifted, 1)

        @block.tensor
        def _(pe):
            pe.wait_ge(w_in, 16 * 7)
            for i in range(2):
                pe.wait_ge(shifted, 4 * i + 4)
                for m in range(M):
                    nc.tensor.matmul(ps[:, i, 0:n].rearrange("p (g n) -> p g n", g=G), w1[:, i, m, :],
                                     pairs_of[:, i, :, 2 * m:2 * m + CMP_STRIDE * (N_CMP - 1) + 1:CMP_STRIDE],
                                     start=(m == 0), stop=(m == M - 1))
                at = (V_PEK, V_PEV)[i]
                for m in range(M):
                    last = nc.tensor.matmul(ps[:, 2, i:i + 1], w1[:, i, m, :], k.vec2[:, at + m:at + m + 1],
                                            start=(m == 0), stop=(m == M - 1))
                last.then_inc(hid_done, 1)
            pe.wait_ge(act_done, 2)
            nc.tensor.matmul(ps[:, 3, 0:n], w2[:, 0:2, :], hid[:, 0, :], start=True, stop=True).then_inc(out_done, 1)
            for g in range(G):
                last = nc.tensor.matmul(ps[0:N_CMP, 4, g * HD:(g + 1) * HD], hid[:, 1, g * N_CMP:(g + 1) * N_CMP], w2[:, 2, :],
                                        start=True, stop=True)
            last.then_inc(out_done, 1)

        @block.vector
        def _(dve):
            dve.wait_ge(hid_done, 2)
            nc.vector.tensor_copy(pe_cols[:, :], ps[:, 2, 0:2]).then_inc(pe_out, 1)
            dve.wait_ge(out_done, 1)
            nc.vector.tensor_copy(kc_dup[:, :], ps[:, 3, 0:n])
            dve.wait_ge(out_done, 2)
            nc.vector.tensor_copy(vc_rows[0:N_CMP, :, :], ps[0:N_CMP, 4, 0:G * HD].rearrange("p (g n) -> p g n", g=G))

        @block.scalar
        def _(act):
            act.wait_ge(pe_out, 1)
            for i in range(2):
                nc.scalar.activation(hid[:, i, :], ps[:, i, 0:n], ACT.Silu, bias=pe_cols[:, i:i + 1]).then_inc(act_done, 1)


def sparse_attention(k, qT, ks2, kw2, vs_rows, vw_rows, kc_dup, vc_rows, gates, mixT, mix_at):
    nc = k.nc
    UNITS = 2 * TC
    T = NSA_T
    with ExitStack() as ctx:
        def sb(name, shape):
            return ctx.enter_context(k.sbuf(name, shape))

        q_pair, k_pair = sb("q_pair", [P, S]), sb("k_pair", [P, 2, S])
        v_pair = sb("v_pair", [P, 2, TC, 2, HD])
        kc_pair, vc_pair = sb("kc_pair", [P, N_CMP]), sb("vc_pair", [P, 2, HD])
        gate_pair = sb("gate_pair", [P, 3, 2, TC])
        probs, probs_t = sb("probs", [P, DEEP, 2, S]), sb("probs_t", [P, 2, 9, P])
        neg_max, sums = sb("neg_max", [P, DEEP, 2]), sb("sums", [P, DEEP, 2])
        cmp_p, cmp_col = sb("cmp_p", [P, UNITS, N_CMP]), sb("cmp_col", [P, 2, UNITS])
        banks = ctx.enter_context(k.psum("banks", [P, 8, S]))
        logits = banks[:, 0:4, :].rearrange("p (u m) n -> p u m n", m=2)
        turned = banks[:, 4:7, :].rearrange("p b (t n) -> p (b t) n", n=P)
        cmp_ps = banks[:, 4:6, 0:TC * N_CMP].rearrange("p u (c i) -> p u c i", c=TC)
        out_ps = banks[:, 7, :]
        (block, admitted, staged, cmp_done, cmp_step, cmp_exp, cmp_ready, logit_done, shifted, exp_done, recip_done, gated, scaled,
         turn_done, turn_out, pv_done, tile_out) = ctx.enter_context(stage(nc, (
             "admitted staged cmp_done cmp_step cmp_exp cmp_ready logit_done shifted exp_done recip_done gated scaled turn_done turn_out "
             "pv_done tile_out")))
        STAGED = 14

        def unit(n):
            u, qb = divmod(n, TC)
            return u, qb, (qb + 1) * P

        def by_unit(col):
            return col.unsqueeze(2).to_broadcast([P, UNITS, N_CMP])

        @block.gpsimd
        def _(pool):
            for t in range(T):
                if t:
                    pool.wait_ge(pv_done, t * UNITS + 1)
                    pool.wait_ge(gated, t * UNITS)
                nc.gpsimd.tensor_copy(q_pair[:, :], qT[:, t, :]).then_inc(staged, 1)
                for u in range(2):
                    g = (2 * t + u) // 3
                    for i, vx in enumerate((vs_rows, vw_rows)):
                        nc.gpsimd.tensor_copy(v_pair[:, i, :, u, :], vx[:, :, g * HD:(g + 1) * HD]).then_inc(staged, 1)
                    nc.gpsimd.tensor_copy(vc_pair[0:N_CMP, u, :], vc_rows[0:N_CMP, g, :]).then_inc(staged, 1)
                nc.gpsimd.tensor_copy(gate_pair[:, :, :, :].rearrange("p b u c -> p c b u"),
                                      gates.rearrange("p c (b h) -> p c b h", b=3)[:, :, :, 2 * t:2 * t + 2]).then_inc(staged, 1)
                for u in range(2):
                    g = (2 * t + u) // 3
                    at = slice(HD * u, HD * u + HD)
                    pool.wait_ge(staged, t * STAGED + 8 + 3 * u)
                    for i, kx in enumerate((ks2, kw2)):
                        nc.gpsimd.tensor_copy(k_pair[at, i, :], kx[int(g != u)][at, :]).then_inc(staged, 1)
                    nc.gpsimd.tensor_copy(kc_pair[at, :], kc_dup[at, g * N_CMP:(g + 1) * N_CMP]).then_inc(staged, 1)
                pool.wait_ge(staged, t * STAGED + STAGED)

        @block.tensor
        def _(pe):
            pe.sem_inc(pv_done, 1)
            pe.sem_inc(turn_done, 1)
            with pe.Fori(0, T) as i:
                def score(n):
                    u, qb, keys = unit(n)
                    at = slice(HD * u, HD * u + HD)
                    if n >= 2:
                        pe.wait_ge(shifted, i * (2 * UNITS) + 2 * n - 1)
                    for m in range(2):
                        last = nc.tensor.matmul(logits[:, n % 2, m, 0:keys], q_pair[at, qb * P:(qb + 1) * P], k_pair[at, m, 0:keys],
                                                start=True, stop=True)
                    last.then_inc(logit_done, 1)

                pe.wait_ge(turn_out, i * (2 * UNITS) + 1)
                pe.wait_ge(staged, i * STAGED + STAGED)
                for n in range(UNITS):
                    u, qb, _ = unit(n)
                    at = slice(HD * u, HD * u + HD)
                    last = nc.tensor.matmul(cmp_ps[:, u, qb, :], q_pair[at, qb * P:(qb + 1) * P], kc_pair[at, :], start=True, stop=True)
                last.then_inc(cmp_done, 1)
                pe.wait_ge(shifted, i * (2 * UNITS) + 1)
                score(0)
                score(1)
                for n in range(UNITS + 1):
                    if n + 2 < UNITS:
                        score(n + 2)
                    if n < UNITS:
                        _, qb, _ = unit(n)
                        pe.wait_ge(scaled, i * (2 * UNITS) + 2 * n + 3)
                        pe.wait_ge(cmp_ready, i + 1)
                        pe.wait_ge(turn_out, i * (2 * UNITS) + 2 * n + 1)
                        for m in range(2):
                            for b in range(qb + 1):
                                nc.tensor.transpose(turned[:, m * 4 + b, :], probs[:, n % DEEP, m, b * P:(b + 1) * P], k.at["ident"])
                        nc.tensor.transpose(turned[0:N_CMP, 8, :], cmp_p[:, n, :], k.at["ident"]).then_inc(turn_done, 1)
                    if n >= 1:
                        m = n - 1
                        u, qb, _ = unit(m)
                        pe.wait_ge(turn_out, i * (2 * UNITS) + 2 * m + 3)
                        if m == 0:
                            pe.wait_ge(tile_out, i + 1)
                        to = out_ps[HD * u:HD * u + HD, qb * P:(qb + 1) * P]
                        for branch in range(2):
                            for b in range(qb + 1):
                                nc.tensor.matmul(to, v_pair[:, branch, b, u, :], probs_t[:, m % 2, branch * 4 + b, :],
                                                 start=(branch == 0 and b == 0), stop=False)
                        nc.tensor.matmul(to, vc_pair[0:N_CMP, u, :], probs_t[0:N_CMP, m % 2, 8, :], start=False, stop=True).then_inc(pv_done, 1)

        @block.vector
        def _(dve):
            dve.sem_inc(scaled, 1)
            dve.sem_inc(tile_out, 1)
            dve.sem_inc(shifted, 1)
            with dve.Fori(0, T) as i:
                def shift(n):
                    u, qb, keys = unit(n)
                    p = n % DEEP
                    dve.wait_ge(logit_done, i * UNITS + n + 1)
                    dve.wait_ge(turn_done, i * UNITS + max(n - 2, 1))
                    dve.sem_inc(admitted, 1)
                    for m in range(2):
                        nc.vector.tensor_tensor_reduce(probs[:, p, m, 0:keys], logits[:, n % 2, m, 0:keys], k.at["causal_row"][:, S - keys:S],
                                                       -1.0, 3e38, ALU.add, ALU.min, neg_max[:, p, m:m + 1]).then_inc(shifted, 1)

                shift(0)
                shift(1)
                col, col2 = cmp_col[:, 0, :], cmp_col[:, 1, :]
                halves = cmp_p[:, :, :].rearrange("p (u c) i -> p u c i", u=2)
                dve.wait_ge(cmp_done, i + 1)
                dve.wait_ge(turn_done, i * UNITS + 1)
                for u in range(2):
                    nc.vector.tensor_tensor(halves[:, u], cmp_ps[:, u], k.at["cmp_add"].rearrange("p (c i) -> p c i", c=TC),
                                            ALU.add).then_inc(cmp_step, 1)
                dve.wait_ge(cmp_step, i * 9 + 2)
                nc.vector.tensor_reduce(col, cmp_p[:, :, :], AX, ALU.max).then_inc(cmp_step, 1)
                dve.wait_ge(cmp_step, i * 9 + 3)
                nc.vector.tensor_tensor(cmp_p[:, :, :], cmp_p[:, :, :], by_unit(col), ALU.subtract).then_inc(cmp_step, 1)
                dve.wait_ge(cmp_exp, i + 1)
                for u in range(2):
                    nc.vector.tensor_tensor(halves[:, u], halves[:, u], k.at["cmp_keep"].rearrange("p (c i) -> p c i", c=TC),
                                            ALU.mult).then_inc(cmp_step, 1)
                dve.wait_ge(cmp_step, i * 9 + 6)
                nc.vector.tensor_reduce(col2, cmp_p[:, :, :], AX, ALU.add).then_inc(cmp_step, 1)
                dve.wait_ge(cmp_step, i * 9 + 7)
                nc.vector.tensor_scalar(col2, col2, 1e-30, None, ALU.max).then_inc(cmp_step, 1)
                dve.wait_ge(cmp_step, i * 9 + 8)
                nc.vector.reciprocal(col2, col2).then_inc(cmp_step, 1)
                dve.wait_ge(cmp_step, i * 9 + 9)
                dve.wait_ge(staged, i * STAGED + STAGED)
                nc.vector.tensor_tensor(col, col2, gate_pair[:, 0, :, :].rearrange("p u c -> p (u c)"), ALU.mult).then_inc(recip_done, 1)
                dve.wait_ge(recip_done, i * (UNITS + 1) + 1)
                nc.vector.tensor_tensor(cmp_p[:, :, :], cmp_p[:, :, :], by_unit(col), ALU.mult).then_inc(cmp_ready, 1)
                for n in range(UNITS):
                    u, qb, keys = unit(n)
                    p = n % DEEP
                    dve.wait_ge(exp_done, i * (2 * UNITS) + 2 * n + 2)
                    nc.vector.reciprocal(sums[:, p, :], sums[:, p, :]).then_inc(recip_done, 1)
                    dve.wait_ge(recip_done, i * (UNITS + 1) + n + 2)
                    nc.vector.tensor_tensor(sums[:, p, :], sums[:, p, :], gate_pair[:, 1:3, u, qb], ALU.mult).then_inc(gated, 1)
                    dve.wait_ge(gated, i * UNITS + n + 1)
                    for m in range(2):
                        nc.vector.tensor_scalar(probs[:, p, m, 0:keys], probs[:, p, m, 0:keys], sums[:, p, m:m + 1], None,
                                                ALU.mult).then_inc(scaled, 1)
                    if n + 2 < UNITS:
                        shift(n + 2)
                dve.wait_ge(pv_done, i * UNITS + UNITS + 1)
                nc.vector.tensor_copy(tile_of(mixT, i + mix_at), out_ps).then_inc(tile_out, 1)

        @block.scalar
        def _(act):
            act.sem_inc(turn_out, 1)
            with act.Fori(0, T) as i:
                def exps(n):
                    u, qb, keys = unit(n)
                    p = n % DEEP
                    act.wait_ge(scaled, i * (2 * UNITS) + max(2 * n - 5, 1))
                    for m in range(2):
                        act.wait_ge(shifted, i * (2 * UNITS) + 2 * n + m + 2)
                        nc.scalar.activation(probs[:, p, m, 0:keys], probs[:, p, m, 0:keys], ACT.Exp, scale=-1.0,
                                             bias=neg_max[:, p, m:m + 1], accum_out=sums[:, p, m:m + 1]).then_inc(exp_done, 1)

                exps(0)
                act.wait_ge(cmp_step, i * 9 + 4)
                nc.scalar.activation(cmp_p[:, :, :], cmp_p[:, :, :], ACT.Exp).then_inc(cmp_exp, 1)
                for n in range(UNITS):
                    u, qb, keys = unit(n)
                    if n + 1 < UNITS:
                        exps(n + 1)
                    act.wait_ge(turn_done, i * UNITS + n + 2)
                    act.wait_ge(pv_done, i * UNITS + max(n, 1))
                    nc.scalar.activation(probs_t[:, n % 2, 0:8, :].rearrange("p (m b) q -> p m b q", m=2)[:, :, 0:qb + 1, :],
                                         turned[:, 0:8, :].rearrange("p (m b) q -> p m b q", m=2)[:, :, 0:qb + 1, :],
                                         ACT.Copy).then_inc(turn_out, 1)
                    nc.scalar.activation(probs_t[0:N_CMP, n % 2, 8, :], turned[0:N_CMP, 8, :], ACT.Copy).then_inc(turn_out, 1)



def stick_breaking(k, qT, kT, v_rows, mixT, mix_at):
    nc = k.nc
    WIDTH = [S - b * P for b in range(TC)]
    AT = [sum(WIDTH[:b]) for b in range(TC + 1)]
    N = AT[TC]
    with ExitStack() as ctx:
        def sb(name, shape):
            return ctx.enter_context(k.sbuf(name, shape))

        q_pair, k_pair, v_pair = sb("q_pair", [P, S]), sb("k_pair", [P, S]), sb("v_pair", [P, TC, P])
        z, soft, tmp = sb("z", [P, N]), sb("soft", [P, N]), sb("tmp", [P, N])
        banks = ctx.enter_context(k.psum("banks", [P, 8, S]))
        z_ps, sum_ps, out_ps = banks[:, 0:4, :], banks[:, 4:8, :], banks[:, 0, :]
        (block, staged, z_done, z_out, abs_done, exp_done, log_done, soft_done, sum_done, arg_done, weight_done, pv_done,
         head_out) = ctx.enter_context(stage(nc, (
             "staged z_done z_out abs_done exp_done log_done soft_done sum_done arg_done weight_done pv_done head_out")))

        @block.gpsimd
        def _(pool):
            with pool.Fori(0, SB_T) as i:
                pool.wait_ge(pv_done, i * 2 + 1)
                nc.gpsimd.tensor_copy(q_pair[:, :], tile_of(qT, i)).then_inc(staged, 1)
                nc.gpsimd.tensor_copy(k_pair[:, :], tile_of(kT, i)).then_inc(staged, 1)
                nc.gpsimd.tensor_copy(v_pair[:, :, :], v_rows[:, :, bass.ds(i * P, P)]).then_inc(staged, 1)

        @block.tensor
        def _(pe):
            pe.sem_inc(pv_done, 1)
            with pe.Fori(0, SB_T) as i:
                pe.wait_ge(staged, i * 3 + 3)
                for u in range(2):
                    at = slice(HD * u, HD * u + HD)
                    pe.wait_ge(head_out, i * 2 + u + 1)
                    for b in range(TC):
                        nc.tensor.matmul(z_ps[:, b, 0:WIDTH[b]], k_pair[at, b * P:(b + 1) * P], q_pair[at, b * P:S],
                                         start=True, stop=True).then_inc(z_done, 1)
                    pe.wait_ge(soft_done, i * 2 + u + 1)
                    for b in range(TC):
                        for later in range(b, TC):
                            last = nc.tensor.matmul(sum_ps[:, b, (later - b) * P:WIDTH[b]], k.at["from_here"] if later == b else k.at["ones"],
                                                    soft[:, AT[later]:AT[later + 1]], start=(later == b), stop=(later == TC - 1))
                        last.then_inc(sum_done, 1)
                    pe.wait_ge(weight_done, i * 2 + u + 1)
                    for b in range(TC):
                        last = nc.tensor.matmul(out_ps[at, b * P:S], v_pair[:, b, at], z[:, AT[b]:AT[b + 1]],
                                                start=(b == 0), stop=(b == TC - 1))
                    last.then_inc(pv_done, 1)

        @block.vector
        def _(dve):
            dve.sem_inc(head_out, 1)
            with dve.Fori(0, SB_T) as i:
                for u in range(2):
                    at = slice(HD * u, HD * u + HD)
                    n = i * 2 + u
                    for b in range(TC):
                        dve.wait_ge(z_done, i * (2 * TC) + u * TC + b + 1)
                        nc.vector.tensor_tensor(z[:, AT[b]:AT[b + 1]], z_ps[:, b, 0:WIDTH[b]], k.at["strict_row"][:, 0:WIDTH[b]],
                                                ALU.add).then_inc(z_out, 1)
                    dve.wait_ge(log_done, n + 1)
                    nc.vector.scalar_tensor_tensor(soft[:, :], z[:, :], 0.0, tmp[:, :], ALU.max, ALU.add).then_inc(soft_done, 1)
                    for b in range(TC):
                        dve.wait_ge(sum_done, i * (2 * TC) + u * TC + b + 1)
                        nc.vector.tensor_tensor(z[:, AT[b]:AT[b + 1]], z[:, AT[b]:AT[b + 1]], sum_ps[:, b, 0:WIDTH[b]],
                                                ALU.subtract).then_inc(arg_done, 1)
                    dve.wait_ge(pv_done, n + 2)
                    nc.vector.tensor_copy(tile_of(mixT, i + mix_at)[at, :], out_ps[at, :]).then_inc(head_out, 1)

        @block.scalar
        def _(act):
            with act.Fori(0, SB_T) as i:
                for u in range(2):
                    n = i * 2 + u
                    act.wait_ge(z_out, i * (2 * TC) + u * TC + TC)
                    nc.scalar.activation(tmp[:, :], z[:, :], ACT.Abs).then_inc(abs_done, 1)
                    act.wait_ge(abs_done, n + 1)
                    nc.scalar.activation(tmp[:, :], tmp[:, :], ACT.Exp, scale=-1.0).then_inc(exp_done, 1)
                    act.wait_ge(exp_done, n + 1)
                    nc.scalar.activation(tmp[:, :], tmp[:, :], ACT.Ln, bias=1.0).then_inc(log_done, 1)
                    act.wait_ge(arg_done, i * (2 * TC) + u * TC + TC)
                    nc.scalar.activation(z[:, :], z[:, :], ACT.Exp).then_inc(weight_done, 1)



def second_mixer(k, a, l, mixT):
    nc = k.nc
    w = layer_of(a["w_in_2"], l)
    with ExitStack() as ctx:
        def sb(name, shape):
            return ctx.enter_context(k.sbuf(name, shape))

        qkv = sb("gdn_qkv", [P, 3 * GDN_T, CONV - 1 + S])
        gz = sb("gdn_z", [P, GDN_T, S])
        by_token = sb("by_token", [P, TC, 2 * P + 30])
        vs_rows, vw_rows, ab = by_token[:, :, 0:P], by_token[:, :, P:2 * P], by_token[:, :, 2 * P:]
        nq = sb("nsa_q", [P, NSA_T, S])
        kv = sb("nsa_kv", [P, 4, S])
        sq, sk, sv_rows = sb("sb_q", [P, SB_T, S]), sb("sb_k", [P, SB_T, S]), sb("sb_v", [P, TC, N_SB * HD])
        cols = sb("gdn_cols", [P, 4, TC * N_GDN])
        gates = sb("nsa_gates", [P, TC, 3 * N_NSA])

        def feat(at, dst, scale=None):
            return ("feat", at, P, lambda e, ps: copy_out(nc, e, dst, ps, scale))

        def rows(at, width, dst, chunks):
            return ("rows", at, width, lambda e, ps: copy_out(nc, e, dst, ps), chunks)

        def gdn_tile(j):
            return qkv[:, j, CONV - 1:] if j < 3 * GDN_T else gz[:, j - 3 * GDN_T, :]

        project_items(k, w, [([(W_GDN + t * COLS, COLS)], [feat(j * P, gdn_tile(4 * t + j)) for j in range(4)]) for t in range(3)] + [
            ([(W_NQ, 384), (W_KC, P)], [feat(j * P, nq[:, j, :], HD ** -0.5) for j in range(NSA_T)] + [feat(3 * P, kv[:, 0, :])]),
            ([(W_KC + P, 2 * P), (W_KW, P)], [feat(j * P, kv[:, j + 1, :]) for j in range(3)]),
            ([(W_KC + 3 * P, P), (W_KW + P, P), (W_AB, 12), (W_GATE, 18)],
             [rows(0, 2 * P + 30, by_token[:, c:c + 1, :], (c,)) for c in range(TC)]),
            ([(W_SQ, 512)], [feat(j * P, sq[:, j, :], HD ** -0.5) for j in range(SB_T)] + [feat((2 + j) * P, sk[:, j, :]) for j in range(SB_T)]),
            ([(W_SV, 256)], [rows(0, 256, sv_rows[:, c:c + 2, :], (c, c + 1)) for c in (0, 2)]),
        ])
        kc2, vc2, ks2, kw2 = ((kv[:, j, :], turned[:, j, :]) for turned in (sb("nsa_kv_turned", [P, 4, S]),) for j in range(4))
        g, beta, beta_eg, to_end = (cols[:, i, :] for i in range(4))
        gdn_steps(k, a, l, ab, g, beta, beta_eg, to_end, gates[:, :, :])
        conv_silu(k, qkv, 3 * GDN_T, CONV, S, lambda t, j: k.vec2[:, bass.ds(t + (V_GCONV + 9 * j), 1)], None)
        norm_heads(k, [(qkv[:, t, CONV - 1:], HD ** -0.5 if t < GDN_T else 1.0, None) for t in range(2 * GDN_T)], 1.0)
        delta_rule(k, qkv, g, beta, beta_eg, to_end, mixT)
        rotate(k, [nq[:, j, :] for j in range(NSA_T)] + [kv[:, j, :] for j in (0, 2, 3)], k.at["swap_32"], k.cos, k.sin)
        swap_halves(k, [kc2, vc2, ks2, kw2])
        with k.sbuf("kc_dup", [P, 2 * N_CMP]) as kc_dup, k.sbuf("vc_rows", [P, 2, HD]) as vc_rows:
            compress_keys(k, a, l, kc2, vc2, kc_dup, vc_rows)
            sparse_attention(k, nq, ks2, kw2, vs_rows, vw_rows, kc_dup, vc_rows, gates[:, :, :], mixT, GDN_T)
        stick_breaking(k, sq, sk, sv_rows, mixT, GDN_T + NSA_T)
        norm_heads(k, [(mixT[:, j, :], k.vec2[:, V_GN:V_GN + 1], gz[:, j, :]) for j in range(GDN_T)]
                   + [(mixT[:, GDN_T + j, :], k.vec2[:, V_NN:V_NN + 1], None) for j in range(NSA_T)]
                   + [(mixT[:, GDN_T + NSA_T + j, :], k.vec2[:, V_SN:V_SN + 1], None) for j in range(SB_T)], 1.0 / HD)


def conv_ffn(k, a, l):
    v = layer_of(a["w_up_2"], l).rearrange("(k p) n -> p k n", p=P)
    half = FF_T * P
    with k.sbuf("ff", [P, FF_T, S]) as ff:
        def slot(t, part):
            return v[:, :, bass.ds(t * (2 * P) + part * half, 2 * P)]

        def tap(t, j, i):
            return k.vec2[:, bass.ds(2 * t + (V_FCONV + 2 * FF_T * i + (j if j < 2 else FF_T + j - 2)), 1)]

        project(k, [run(FF_T // 2, slot, None, parts=2)], conv=(tap, lambda t, j: tile_of(ff, 2 * t + j)))
        down_project(k, layer_of(a["w_down_2"], l), ff, 2)


def layer_input(k, a, l):
    nc = k.nc
    K = 2
    with k.sbuf("ple_gate", [P, DT, S]) as gate, k.sbuf("pT", [P, K, S]) as pT, k.sbuf("p_rows", [P, TC, K * P]) as p_rows:
        with (
            k.psum("turned", [P, K, S]) as turned,
            stage(nc, "p_in turn_done") as (block, p_in, turn_done),
        ):
            @block.sync
            def _(sp):
                sp.dma_start(p_rows[:, :, :], layer_of(a["p_2"], l)[0].rearrange("(c p) n -> p c n", p=P)).then_inc(p_in, 16)

            @block.tensor
            def _(pe):
                pe.wait_ge(p_in, 16)
                for f in range(K):
                    for c in range(TC):
                        last = nc.tensor.transpose(turned[:, f, c * P:(c + 1) * P], p_rows[:, c, f * P:(f + 1) * P], k.at["ident"])
                    last.then_inc(turn_done, 1)

            @block.vector
            def _(dve):
                for f in range(K):
                    dve.wait_ge(turn_done, f + 1)
                    nc.vector.tensor_copy(pT[:, f, :], turned[:, f, :])

        project(k, [run(2, weight_tiles(layer_of(a["w_ple_gate_2"], l), 0),
                        lambda e, t, j, ps: copy_out(nc, e, tile_of(gate, 4 * t + j), ps))])
        with stage(nc, "none") as (block, _none):
            @block.scalar
            def _(act):
                nc.scalar.activation(gate[:, :, :], gate[:, :, :], ACT.Sigmoid)
        down_project(k, layer_of(a["w_ple_2"], l), pT, K, post=lambda f: k.vec2[:, V_PLEN + f:V_PLEN + f + 1], gate=gate)


def store_output(k, a, yT):
    nc = k.nc
    with (
        k.sbuf("y_rows", [P, TC, D]) as y_rows, k.psum("turned", [P, TC, 2, S]) as turned,
        stage(nc, "turn_done out_done stored") as (block, turn_done, out_done, stored),
    ):
        @block.tensor
        def _(pe):
            for c in range(TC):
                for f in range(DT):
                    last = nc.tensor.transpose(turned[:, c, f // 4, (f % 4) * P:(f % 4 + 1) * P], yT[:, f, c * P:(c + 1) * P], k.at["ident"])
                last.then_inc(turn_done, 1)

        @block.vector
        def _(dve):
            for c in range(TC):
                dve.wait_ge(turn_done, c + 1)
                nc.vector.tensor_copy(y_rows[:, c, :], turned[:, c, :, :].rearrange("p b n -> p (b n)")).then_inc(out_done, 1)

        @block.sync
        def _(sp):
            for c in range(TC):
                sp.wait_ge(out_done, c + 1)
                sp.dma_start(a["y"][0, c * P:(c + 1) * P, :], y_rows[:, c, :]).then_inc(stored, 16)
            sp.wait_ge(stored, 16 * TC)


def place(k, buf, arrays):
    at = 0
    for name, array in arrays.items():
        k.at[name] = buf[:, at:at + array.shape[1]]
        at += array.shape[1]


def first_blocks(k, a):
    with ExitStack() as ctx:
        def sb(name, shape):
            return ctx.enter_context(k.sbuf(name, shape))

        k.vec = sb("vec", [P, 2 * P + 1])
        k.c_act = sb("c_act", [P, DT])[:, :]
        k.mod = sb("mod", [P, 96])
        k.pre_gain = sb("pre_gain", [P, 4, DT])
        k.post_gain = sb("post_gain", [P, 4, DT])
        k.ssd_d = sb("ssd_d", [P, SSD_HEADS])[:, :]
        k.band = sb("band", [P, HEADS, BAND])
        k.far = sb("far", [P, HEADS])[:, :]
        load_inputs(k, a)
        modulation(k, a)
        relative_bias(k, a)
        pre_norm(k, 0)
        with k.sbuf("mixT", [P, 16, S]) as mixT:
            even_ssd(k, a, mixT)
            even_diff(k, a, mixT)
            down_project(k, a["e_w_out"][0], mixT, 4, post=lambda f: k.post_gain[:, 0, f:f + 1])
        pre_norm(k, 1)
        squared_relu_mlp(k, a, 0, 1)
        pre_norm(k, 2)
        with k.sbuf("mixT", [P, 12, S]) as mixT:
            odd_mixer(k, a, mixT)
            down_project(k, a["o_w_out"][0], mixT, 4, post=lambda f: k.post_gain[:, 2, f:f + 1])
        pre_norm(k, 3)
        squared_relu_mlp(k, a, 1, 3)


def second_blocks(k, a):
    with k.sbuf("const2_sb", list(a["const2"].shape)) as const2, k.sbuf("vec2", [P, V_FCONV + 3 * 2 * FF_T]) as k.vec2, \
            k.sbuf("cos", [P, S]) as cos, k.sbuf("sin", [P, S]) as sin:
        place(k, const2, second_constants())
        k.level_masks = [k.at[f"level_{n}"] for n in range(6)]
        k.cos, k.sin = cos[:, :], sin[:, :]
        with stage(k.nc, "const_in") as (block, const_in):
            @block.sync
            def _(sp):
                sp.dma_start(const2[:, :], a["const2"]).then_inc(const_in, 16)
                sp.wait_ge(const_in, 16)
        rotary_tables(k, a)
        with k.nc.Fori(0, 2) as l:
            def gain(at):
                return lambda f: k.vec2[:, at + f:at + f + 1]

            layer_vectors(k, a, l)
            norm_into(k, gain(V_MIX))
            with k.sbuf("mix2T", [P, DT, S]) as mixT:
                second_mixer(k, a, l, mixT)
                down_project(k, layer_of(a["w_out_2"], l), mixT, 4)
            norm_into(k, gain(V_FFN))
            conv_ffn(k, a, l)
            norm_into(k, gain(V_PLE))
            layer_input(k, a, l)
        with k.sbuf("yT", [P, DT, S]) as yT:
            norm_into(k, gain(V_FIN), whole=yT)
            store_output(k, a, yT)


def build(nc, a):
    k = Kit(nc)
    with ExitStack() as ctx:
        def sb(name, shape):
            return ctx.enter_context(k.sbuf(name, shape))

        k.const = sb("const_sb", list(a["const"].shape))
        place(k, k.const, constants())
        k.xT = sb("xT", [P, DT, S])
        k.h_hi, k.h_lo = sb("h_hi", [P, DT, S]), sb("h_lo", [P, DT, S])
        first_blocks(k, a)
        second_blocks(k, a)


INS = ["x", "c", "rel_bias", "norm_gains", "mod_w", "mod_b", "mlp_w1", "mlp_w2", "e_w_in", "e_conv_w", "e_conv_b",
       "e_dt_bias", "e_A_log", "e_D", "e_ssd_norm", "e_lambda", "e_diff_norm", "e_w_out", "o_w_in", "o_sinks", "o_w_out",
       "p_2", "positions_2", "ln_mix_2", "w_in_2", "gdn_conv_2", "gdn_a_log_2", "gdn_dt_bias_2", "gdn_norm_2", "nsa_pe_k_2",
       "nsa_pe_v_2", "nsa_cmp_k_w1_2", "nsa_cmp_k_w2_2", "nsa_cmp_v_w1_2", "nsa_cmp_v_w2_2", "nsa_norm_2", "sb_norm_2",
       "w_out_2", "ln_ffn_2", "w_up_2", "ffn_conv_2", "w_down_2", "ln_ple_2", "w_ple_gate_2", "w_ple_2", "ple_norm_2",
       "ln_final_2"]


def kernel(**inputs):
    import concourse.bacc as bacc
    from concourse.bass_utils import run_bass_kernel_spmd as run

    nc = bacc.Bacc("TRN2", target_bir_lowering=False, num_devices=1)
    arrays, args = {}, {}

    def declare(name, array):
        arrays[f"in_{name}"] = array
        args[name] = nc.dram_tensor(f"in_{name}", array.shape, mybir.dt.from_np(array.dtype), kind="ExternalInput").ap()

    for name in INS:
        declare(name, np.ascontiguousarray(inputs[name]))
    for name, arrays_of in (("const", constants()), ("const2", second_constants())):
        declare(name, np.concatenate([v.astype(np.float32) for v in arrays_of.values()], axis=1))
    declare("one_hot", (np.arange(REL_BUCKETS)[:, None] == bucket_of(BAND - 1 - np.arange(3 * P))[None, :]).astype(np.float32))
    declare("ret_table", retention_constants()[0])
    args["y"] = nc.dram_tensor("out_y", (1, S, D), F32, kind="ExternalOutput").ap()
    build(nc, args)
    r = run(nc, [arrays], core_ids=[0])
    return r.results[0]["out_y"]
```
